# Optimizing a Trainium2 kernel written in Bass

```python
import jax, jax.numpy as jnp
from jax import lax
import numpy as np

D_MODEL = 1024
BATCH = 1
SEQ = 512
DEPTH = 1

N_HEADS = 8
N_KV_HEADS = 2
HEAD_DIM = 64
GQA_GROUP = N_HEADS // N_KV_HEADS
ATTN_DIM = N_HEADS * HEAD_DIM
KV_DIM = N_KV_HEADS * HEAD_DIM
WINDOW = 128
ATTN_BLOCK = 128
ROT_DIM = HEAD_DIM // 4
ROPE_THETA = 500000.0
CONV_DIM = D_MODEL // 2
CONV_WIDTH = 3
SPLIT_SIZES = (ATTN_DIM, KV_DIM, KV_DIM, CONV_DIM, CONV_DIM, CONV_DIM, D_MODEL, D_MODEL)
PROJ_WIDTH = sum(SPLIT_SIZES)
SPLIT_POINTS = tuple(int(v) for v in np.cumsum(SPLIT_SIZES)[:-1])
N_GROUPS = 4
EXPERTS_PER_GROUP = 8
N_EXPERTS = N_GROUPS * EXPERTS_PER_GROUP
TOP_K = 2
D_FF_EXPERT = D_MODEL // 4
MOE_BLOCK = 128
NORM_EPS = 1e-6
MASK_VALUE = -1e30


def rmsnorm(x, g):
    xf = x.astype(jnp.float32)
    xf = xf * lax.rsqrt(jnp.mean(xf * xf, axis=-1, keepdims=True) + NORM_EPS)
    return xf.astype(x.dtype) * g

def rope_tables(seq_len):
    inv_freq = ROPE_THETA ** (-jnp.arange(0, ROT_DIM, 2, dtype=jnp.float32) / ROT_DIM)
    ang = jnp.arange(seq_len, dtype=jnp.float32)[:, None] * inv_freq[None, :]
    return jnp.cos(ang), jnp.sin(ang)

def partial_rope(x, cos, sin):
    half = ROT_DIM // 2
    c = cos[None, :, None, :].astype(x.dtype)
    s = sin[None, :, None, :].astype(x.dtype)
    x1 = x[..., :half]
    x2 = x[..., half:ROT_DIM]
    return jnp.concatenate([x1 * c - x2 * s, x2 * c + x1 * s, x[..., ROT_DIM:]], axis=-1)

def band_keys(t):
    b, s, hk, hd = t.shape
    nb = s // ATTN_BLOCK
    tp = jnp.pad(t, ((0, 0), (WINDOW, WINDOW), (0, 0), (0, 0))).reshape(b, nb + 2, ATTN_BLOCK, hk, hd)
    return jnp.concatenate([tp[:, :-2], tp[:, 1:-1], tp[:, 2:]], axis=2)

def windowed_gqa(q, k, v, sink):
    b, s, _, hd = q.shape
    nb = s // ATTN_BLOCK
    qb = q.reshape(b, nb, ATTN_BLOCK, N_KV_HEADS, GQA_GROUP, hd)
    kw = band_keys(k)
    vw = band_keys(v)
    scores = jnp.einsum('bnqhgd,bnkhd->bnhgqk', qb, kw,
                        preferred_element_type=jnp.float32) * (HEAD_DIM ** -0.5)
    blk = jnp.arange(nb)[:, None, None] * ATTN_BLOCK
    qpos = blk + jnp.arange(ATTN_BLOCK)[None, :, None]
    kpos = blk - WINDOW + jnp.arange(3 * ATTN_BLOCK)[None, None, :]
    valid = (jnp.abs(qpos - kpos) <= WINDOW) & (kpos >= 0) & (kpos < s)
    scores = jnp.where(valid[None, :, None, None], scores, MASK_VALUE)
    sink_b = sink.astype(jnp.float32).reshape(1, 1, N_KV_HEADS, GQA_GROUP, 1, 1)
    m = jnp.maximum(jnp.max(scores, axis=-1, keepdims=True), sink_b)
    e = jnp.exp(scores - m)
    p = e / (jnp.sum(e, axis=-1, keepdims=True) + jnp.exp(sink_b - m))
    o = jnp.einsum('bnhgqk,bnkhd->bnqhgd', p.astype(v.dtype), vw)
    return o.reshape(b, s, N_HEADS * hd)

def short_gated_conv(gate_b, gate_c, xc, conv_w, conv_b):
    u = gate_c * xc
    up = jnp.pad(u, ((0, 0), (1, 1), (0, 0)))
    conv = up[:, :-2] * conv_w[0] + up[:, 1:-1] * conv_w[1] + up[:, 2:] * conv_w[2] + conv_b
    return gate_b * conv

def hierarchical_moe(h, w_rg, b_rg, w_re, b_re, w_gate, w_up, w_down):
    b, s, d = h.shape
    t = b * s
    hf = h.reshape(t, d)
    hf32 = hf.astype(jnp.float32)
    g_logits = hf32 @ w_rg.astype(jnp.float32) + b_rg.astype(jnp.float32)
    grp = jnp.argmax(g_logits, axis=-1)
    p_grp = jnp.take_along_axis(jax.nn.softmax(g_logits, axis=-1), grp[:, None], axis=-1)
    e_logits = (hf32 @ w_re.astype(jnp.float32) + b_re.astype(jnp.float32)).reshape(t, N_GROUPS, EXPERTS_PER_GROUP)
    e_in = jnp.take_along_axis(e_logits, grp[:, None, None], axis=1)[:, 0]
    top_p, top_i = lax.top_k(jax.nn.softmax(e_in, axis=-1), TOP_K)
    top_p = top_p / jnp.sum(top_p, axis=-1, keepdims=True)
    gates = (p_grp * top_p).reshape(t * TOP_K)
    expert = (grp[:, None] * EXPERTS_PER_GROUP + top_i).reshape(t * TOP_K)
    n_assign = t * TOP_K
    order = jnp.argsort(expert)
    e_sorted = expert[order]
    tok = order // TOP_K
    counts = jnp.bincount(expert, length=N_EXPERTS)
    starts = jnp.cumsum(counts) - counts
    padded = ((counts + MOE_BLOCK - 1) // MOE_BLOCK) * MOE_BLOCK
    pad_ends = jnp.cumsum(padded)
    pad_starts = pad_ends - padded
    dest = pad_starts[e_sorted] + (jnp.arange(n_assign) - starts[e_sorted])
    n_rows = n_assign + N_EXPERTS * MOE_BLOCK
    n_blocks = n_rows // MOE_BLOCK
    x_pad = jnp.zeros((n_rows, d), h.dtype).at[dest].set(hf[tok])
    block_e = jnp.minimum(jnp.searchsorted(pad_ends, jnp.arange(n_blocks) * MOE_BLOCK, side='right'),
                          N_EXPERTS - 1)

    def expert_block(args):
        xb, e = args
        hid = jax.nn.silu(xb @ w_gate[e]) * (xb @ w_up[e])
        return hid @ w_down[e]

    y_pad = lax.map(expert_block, (x_pad.reshape(n_blocks, MOE_BLOCK, d), block_e)).reshape(n_rows, d)
    y = y_pad[dest] * gates[order][:, None].astype(h.dtype)
    out = jnp.zeros((t, d), h.dtype).at[tok].add(y)
    return out.reshape(b, s, d)

def first_inputs(seed: int = 0) -> dict:
    key = jax.random.key(seed)
    ks = jax.random.split(key, 20)
    f32 = jnp.float32

    def nrm(k, shape, fan_in):
        return jax.random.normal(k, shape, f32) * (fan_in ** -0.5)

    def gain(k, shape):
        return 1.0 + 0.02 * jax.random.normal(k, shape, f32)

    return {
        "x": jax.random.normal(ks[0], (BATCH, SEQ, D_MODEL), f32),
        "norm1_g": gain(ks[1], (DEPTH, D_MODEL)),
        "w_in": nrm(ks[2], (DEPTH, D_MODEL, PROJ_WIDTH), D_MODEL),
        "q_norm_g": gain(ks[3], (DEPTH, HEAD_DIM)),
        "k_norm_g": gain(ks[4], (DEPTH, HEAD_DIM)),
        "attn_sink": 0.5 * jax.random.normal(ks[5], (DEPTH, N_HEADS), f32),
        "conv_w": nrm(ks[6], (DEPTH, CONV_WIDTH, CONV_DIM), CONV_WIDTH),
        "conv_b": 0.02 * jax.random.normal(ks[7], (DEPTH, CONV_DIM), f32),
        "w_attn_proj": nrm(ks[8], (DEPTH, ATTN_DIM, D_MODEL), ATTN_DIM),
        "w_conv_proj": nrm(ks[9], (DEPTH, CONV_DIM, D_MODEL), CONV_DIM),
        "w_out": nrm(ks[10], (DEPTH, D_MODEL, D_MODEL), D_MODEL),
        "norm2_g": gain(ks[11], (DEPTH, D_MODEL)),
        "w_router_group": nrm(ks[12], (DEPTH, D_MODEL, N_GROUPS), D_MODEL),
        "b_router_group": 0.01 * jax.random.normal(ks[13], (DEPTH, N_GROUPS), f32),
        "w_router_expert": nrm(ks[14], (DEPTH, D_MODEL, N_EXPERTS), D_MODEL),
        "b_router_expert": 0.01 * jax.random.normal(ks[15], (DEPTH, N_EXPERTS), f32),
        "w_gate_e": nrm(ks[16], (DEPTH, N_EXPERTS, D_MODEL, D_FF_EXPERT), D_MODEL),
        "w_up_e": nrm(ks[17], (DEPTH, N_EXPERTS, D_MODEL, D_FF_EXPERT), D_MODEL),
        "w_down_e": nrm(ks[18], (DEPTH, N_EXPERTS, D_FF_EXPERT, D_MODEL), D_FF_EXPERT),
    }

def first_block(x, norm1_g, w_in, q_norm_g, k_norm_g, attn_sink, conv_w, conv_b,
              w_attn_proj, w_conv_proj, w_out, norm2_g, w_router_group, b_router_group,
              w_router_expert, b_router_expert, w_gate_e, w_up_e, w_down_e):
    b, s, _ = x.shape
    cos, sin = rope_tables(s)
    for l in range(DEPTH):
        h = rmsnorm(x, norm1_g[l])
        proj = h @ w_in[l]
        q, k, v, cb, cc, cx, g_attn, g_conv = jnp.split(proj, SPLIT_POINTS, axis=-1)
        q = rmsnorm(q.reshape(b, s, N_HEADS, HEAD_DIM), q_norm_g[l])
        k = rmsnorm(k.reshape(b, s, N_KV_HEADS, HEAD_DIM), k_norm_g[l])
        v = v.reshape(b, s, N_KV_HEADS, HEAD_DIM)
        q = partial_rope(q, cos, sin)
        k = partial_rope(k, cos, sin)
        attn = windowed_gqa(q, k, v, attn_sink[l])
        conv = short_gated_conv(cb, cc, cx, conv_w[l], conv_b[l])
        merged = (jax.nn.sigmoid(g_attn) * (attn @ w_attn_proj[l])
                  + jax.nn.sigmoid(g_conv) * (conv @ w_conv_proj[l]))
        x = x + merged @ w_out[l]
        h2 = rmsnorm(x, norm2_g[l])
        x = x + hierarchical_moe(h2, w_router_group[l], b_router_group[l],
                                 w_router_expert[l], b_router_expert[l],
                                 w_gate_e[l], w_up_e[l], w_down_e[l])
    return x


DEPTH_2 = 2

GRID_W = 64
Q_BLOCK = 128
ROPE_THETA_2 = 10000.0
EPS = 1e-6
A_HEADS = 8
A_KV_HEADS = 2
B_HEADS = 8
B_Q_RANK = 384
B_KV_RANK = 256
B_NOPE = 64
B_ROPE = 32
B_V = 64
C_HEADS = 16
C_WIN_ROWS = 8
C_WIN_COLS = 16
D_FF = 4 * D_MODEL

A_Q = A_HEADS * HEAD_DIM
A_KV = A_KV_HEADS * HEAD_DIM
EVEN_SPLITS = (A_Q, A_Q + A_KV, A_Q + 2 * A_KV, A_Q + 2 * A_KV + B_Q_RANK,
               A_Q + 2 * A_KV + B_Q_RANK + B_KV_RANK)
EVEN_IN = A_Q + 2 * A_KV + B_Q_RANK + B_KV_RANK + B_ROPE
MIX_WIDTH = A_HEADS * HEAD_DIM + B_HEADS * B_V
C_WIDTH = C_HEADS * HEAD_DIM
N_EVEN = (DEPTH_2 + 1) // 2
N_ODD = DEPTH_2 // 2


def rmsnorm_2(x, g):
    xf = x.astype(jnp.float32)
    y = xf * lax.rsqrt(jnp.mean(xf * xf, axis=-1, keepdims=True) + EPS)
    return (y * g.astype(jnp.float32)).astype(x.dtype)

def rope_1d(x, pos):
    d = x.shape[-1]
    inv = ROPE_THETA_2 ** (-jnp.arange(0, d, 2, dtype=jnp.float32) / d)
    ang = pos[:, None] * inv[None, :]
    cos = jnp.cos(ang)[:, None, :].astype(x.dtype)
    sin = jnp.sin(ang)[:, None, :].astype(x.dtype)
    x1, x2 = jnp.split(x, 2, axis=-1)
    return jnp.concatenate([x1 * cos - x2 * sin, x2 * cos + x1 * sin], axis=-1)

def axial_rope(x, row, col):
    xr, xc = jnp.split(x, 2, axis=-1)
    return jnp.concatenate([rope_1d(xr, row), rope_1d(xc, col)], axis=-1)

def block_attention(q, k, v, scale):
    b, s, hq, d = q.shape
    hkv = k.shape[2]
    g = hq // hkv
    nblk = s // Q_BLOCK
    qb = q.reshape(b, nblk, Q_BLOCK, hkv, g, d).transpose(1, 0, 3, 4, 2, 5)
    kt = k.transpose(0, 2, 1, 3)
    vt = v.transpose(0, 2, 1, 3)

    def one(qblk):
        sc = jnp.einsum('bkgqd,bksd->bkgqs', qblk, kt).astype(jnp.float32) * scale
        p = jax.nn.softmax(sc, axis=-1).astype(vt.dtype)
        return jnp.einsum('bkgqs,bksd->bkgqd', p, vt)

    o = lax.map(one, qb)
    return o.transpose(1, 0, 4, 2, 3, 5).reshape(b, s, hq, -1)

def hybrid_attention(h, w_in, a_q_norm, a_k_norm, b_q_norm, b_w_uq, b_kv_norm, b_w_ukv,
                     w_out, row, col):
    b, s, _ = h.shape
    z = h @ w_in
    qa, ka, va, cq, ckv, kr = jnp.split(z, EVEN_SPLITS, axis=-1)
    qa = axial_rope(rmsnorm_2(qa.reshape(b, s, A_HEADS, HEAD_DIM), a_q_norm), row, col)
    ka = axial_rope(rmsnorm_2(ka.reshape(b, s, A_KV_HEADS, HEAD_DIM), a_k_norm), row, col)
    va = va.reshape(b, s, A_KV_HEADS, HEAD_DIM)
    oa = block_attention(qa, ka, va, HEAD_DIM ** -0.5)
    qb = (rmsnorm_2(cq, b_q_norm) @ b_w_uq).reshape(b, s, B_HEADS, B_NOPE + B_ROPE)
    q_nope, q_rope = jnp.split(qb, (B_NOPE,), axis=-1)
    q_rope = axial_rope(q_rope, row, col)
    kvb = (rmsnorm_2(ckv, b_kv_norm) @ b_w_ukv).reshape(b, s, B_HEADS, B_NOPE + B_V)
    k_nope, vb = jnp.split(kvb, (B_NOPE,), axis=-1)
    k_rope = axial_rope(kr[:, :, None, :], row, col)
    q_full = jnp.concatenate([q_nope, q_rope], axis=-1)
    k_full = jnp.concatenate([k_nope, jnp.broadcast_to(k_rope, (b, s, B_HEADS, B_ROPE))], axis=-1)
    ob = block_attention(q_full, k_full, vb, (B_NOPE + B_ROPE) ** -0.5)
    mixed = jnp.concatenate([oa.reshape(b, s, -1), ob.reshape(b, s, -1)], axis=-1)
    return mixed @ w_out

def neighbourhood_attention(h, w_qkv, rpb, w_out):
    b, s, _ = h.shape
    rows = s // GRID_W
    wr = min(C_WIN_ROWS, rows)
    wc = C_WIN_COLS
    nblk = s // Q_BLOCK
    q, k, v = jnp.split(h @ w_qkv, 3, axis=-1)
    q = q.reshape(b, s, C_HEADS, HEAD_DIM).transpose(0, 2, 1, 3)
    k = k.reshape(b, s, C_HEADS, HEAD_DIM).transpose(0, 2, 1, 3)
    v = v.reshape(b, s, C_HEADS, HEAD_DIM).transpose(0, 2, 1, 3)
    t = jnp.arange(s, dtype=jnp.int32)
    qr, qc = t // GRID_W, t % GRID_W
    rs = jnp.clip(qr - wr // 2, 0, rows - wr)
    cs = jnp.clip(qc - wc // 2, 0, GRID_W - wc)
    kr = rs[:, None, None] + jnp.arange(wr, dtype=jnp.int32)[None, :, None]
    kc = cs[:, None, None] + jnp.arange(wc, dtype=jnp.int32)[None, None, :]
    idx = (kr * GRID_W + kc).reshape(s, wr * wc)
    ridx = jnp.broadcast_to(kr - qr[:, None, None] + (C_WIN_ROWS - 1), (s, wr, wc)).reshape(s, -1)
    cidx = jnp.broadcast_to(kc - qc[:, None, None] + (C_WIN_COLS - 1), (s, wr, wc)).reshape(s, -1)
    qbk = q.reshape(b, C_HEADS, nblk, Q_BLOCK, HEAD_DIM).transpose(2, 0, 1, 3, 4)
    blk = lambda a: a.reshape(nblk, Q_BLOCK, -1)
    scale = HEAD_DIM ** -0.5

    def one(args):
        qblk, iblk, rblk, cblk = args
        kg = jnp.take(k, iblk, axis=2)
        vg = jnp.take(v, iblk, axis=2)
        bias = rpb[:, rblk, cblk].astype(jnp.float32)
        sc = jnp.einsum('bhqd,bhqkd->bhqk', qblk, kg).astype(jnp.float32) * scale + bias[None]
        p = jax.nn.softmax(sc, axis=-1).astype(vg.dtype)
        return jnp.einsum('bhqk,bhqkd->bhqd', p, vg)

    o = lax.map(one, (qbk, blk(idx), blk(ridx), blk(cidx)))
    o = o.transpose(1, 0, 3, 2, 4).reshape(b, s, C_WIDTH)
    return o @ w_out

def sq_relu_mlp(h, w_up, w_down):
    u = jax.nn.relu(h @ w_up)
    return (u * u) @ w_down

def second_inputs(seed: int = 0) -> dict:
    key = jax.random.key(seed)
    ks = jax.random.split(key, 20)

    def w(k, shape, fan_in):
        return jax.random.normal(k, shape, jnp.float32) * (fan_in ** -0.5)

    def gain(k, shape):
        return 1.0 + 0.05 * jax.random.normal(k, shape, jnp.float32)

    return {
        "x": jax.random.normal(ks[0], (BATCH, SEQ, D_MODEL), jnp.float32),
        "norm_mix": gain(ks[1], (DEPTH_2, D_MODEL)),
        "ev_w_in": w(ks[2], (N_EVEN, D_MODEL, EVEN_IN), D_MODEL),
        "ev_a_q_norm": gain(ks[3], (N_EVEN, HEAD_DIM)),
        "ev_a_k_norm": gain(ks[4], (N_EVEN, HEAD_DIM)),
        "ev_b_q_norm": gain(ks[5], (N_EVEN, B_Q_RANK)),
        "ev_b_w_uq": w(ks[6], (N_EVEN, B_Q_RANK, B_HEADS * (B_NOPE + B_ROPE)), B_Q_RANK),
        "ev_b_kv_norm": gain(ks[7], (N_EVEN, B_KV_RANK)),
        "ev_b_w_ukv": w(ks[8], (N_EVEN, B_KV_RANK, B_HEADS * (B_NOPE + B_V)), B_KV_RANK),
        "ev_w_out": w(ks[9], (N_EVEN, MIX_WIDTH, D_MODEL), MIX_WIDTH),
        "od_w_qkv": w(ks[10], (N_ODD, D_MODEL, 3 * C_WIDTH), D_MODEL),
        "od_rpb": 0.1 * jax.random.normal(ks[11], (N_ODD, C_HEADS, 2 * C_WIN_ROWS - 1, 2 * C_WIN_COLS - 1), jnp.float32),
        "od_w_out": w(ks[12], (N_ODD, C_WIDTH, D_MODEL), C_WIDTH),
        "norm_ffn": gain(ks[13], (DEPTH_2, D_MODEL)),
        "ffn_w_up": w(ks[14], (DEPTH_2, D_MODEL, D_FF), D_MODEL),
        "ffn_w_down": w(ks[15], (DEPTH_2, D_FF, D_MODEL), D_FF),
        "final_norm": gain(ks[16], (D_MODEL,)),
    }

def second_block(x, norm_mix, ev_w_in, ev_a_q_norm, ev_a_k_norm, ev_b_q_norm, ev_b_w_uq,
              ev_b_kv_norm, ev_b_w_ukv, ev_w_out, od_w_qkv, od_rpb, od_w_out,
              norm_ffn, ffn_w_up, ffn_w_down, final_norm):
    s = x.shape[1]
    t = jnp.arange(s, dtype=jnp.int32)
    row = (t // GRID_W).astype(jnp.float32)
    col = (t % GRID_W).astype(jnp.float32)
    h = x
    for layer in range(DEPTH_2):
        i = layer // 2
        hn = rmsnorm_2(h, norm_mix[layer])
        if layer % 2 == 0:
            h = h + hybrid_attention(hn, ev_w_in[i], ev_a_q_norm[i], ev_a_k_norm[i],
                                     ev_b_q_norm[i], ev_b_w_uq[i], ev_b_kv_norm[i],
                                     ev_b_w_ukv[i], ev_w_out[i], row, col)
        else:
            h = h + neighbourhood_attention(hn, od_w_qkv[i], od_rpb[i], od_w_out[i])
        h = h + sq_relu_mlp(rmsnorm_2(h, norm_ffn[layer]), ffn_w_up[layer], ffn_w_down[layer])
    return rmsnorm_2(h, final_norm)


def setup_inputs(seed=0):
    out = dict(first_inputs(seed))
    for name, value in second_inputs(seed + 1).items():
        if name != "x":
            out[name + "_2"] = value
    return out


def reference(
    x, norm1_g, w_in, q_norm_g, k_norm_g, attn_sink, conv_w, conv_b, w_attn_proj, w_conv_proj,
    w_out, norm2_g, w_router_group, b_router_group, w_router_expert, b_router_expert, w_gate_e,
    w_up_e, w_down_e, norm_mix_2, ev_w_in_2, ev_a_q_norm_2, ev_a_k_norm_2, ev_b_q_norm_2,
    ev_b_w_uq_2, ev_b_kv_norm_2, ev_b_w_ukv_2, ev_w_out_2, od_w_qkv_2, od_rpb_2, od_w_out_2,
    norm_ffn_2, ffn_w_up_2, ffn_w_down_2, final_norm_2,
):
    x = first_block(
        x, norm1_g, w_in, q_norm_g, k_norm_g, attn_sink, conv_w, conv_b, w_attn_proj,
        w_conv_proj, w_out, norm2_g, w_router_group, b_router_group, w_router_expert,
        b_router_expert, w_gate_e, w_up_e, w_down_e,
    )
    return second_block(
        x, norm_mix_2, ev_w_in_2, ev_a_q_norm_2, ev_a_k_norm_2, ev_b_q_norm_2, ev_b_w_uq_2,
        ev_b_kv_norm_2, ev_b_w_ukv_2, ev_w_out_2, od_w_qkv_2, od_rpb_2, od_w_out_2, norm_ffn_2,
        ffn_w_up_2, ffn_w_down_2, final_norm_2,
    )


_drawn_inputs = setup_inputs


def setup_inputs(seed=0):
    import zlib

    import numpy as np

    out = dict(_drawn_inputs(seed))
    spreads = {}
    factors = {'q_norm_g': 7.567,
     'k_norm_g': 8.0,
     'attn_sink': 8.0,
     'b_router_group': 7.907,
     'b_router_expert': 5.142,
     'norm_mix_2': 4.155,
     'ev_a_q_norm_2': 8.0,
     'ev_a_k_norm_2': 8.0,
     'ev_b_q_norm_2': 8.0,
     'ev_b_kv_norm_2': 8.0,
     'od_rpb_2': 7.115}
    for name, (base, spread) in spreads.items():
        noise = np.random.default_rng([zlib.crc32(name.encode()), seed]).standard_normal(out[name].shape)
        drawn = base * np.exp(spread * noise) if base else spread * noise
        out[name] = __import__('jax').numpy.asarray(drawn.astype(out[name].dtype))
    for name, factor in factors.items():
        out[name] = (out[name] * factor).astype(out[name].dtype)
    return out
```

```python
from contextlib import ExitStack

import numpy as np

import concourse.bass as bass
from concourse import mybir

F = mybir.dt.float32
R = mybir.dt.float32r
I32 = mybir.dt.int32
U32 = mybir.dt.uint32
ALU = mybir.AluOpType
ACT = mybir.ActivationFunctionType
AX = mybir.AxisListType.X

T = 512
D = 1024
KB = 1024
BASE = 16512
EPS = 1e-6
NEG = -1e30
CAP = 64
NE = 32
SLOTS = NE * CAP


class Queue:

    def __init__(self, eng, sem):
        self.eng, self.sem, self.n, self.seen = eng, sem, 0, {}

    def wait(self, *tokens):
        for t in tokens:
            if t is None:
                continue
            if isinstance(t, list):
                self.wait(*t)
                continue
            sem, value = t
            if self.seen.get(sem.name, 0) < value:
                self.seen[sem.name] = value
                self.eng.wait_ge(sem, value)

    def do(self, fn, *tokens):
        self.wait(*tokens)
        self.n += 1
        fn(self.eng).then_inc(self.sem, 1)
        return (self.sem, self.n)

    def plain(self, fn, *tokens):
        self.wait(*tokens)
        fn(self.eng)


class Count:

    def __init__(self, sem):
        self.sem, self.n = sem, 0

    def load(self, queue, fn, *tokens):
        queue.wait(*tokens)
        self.n += 16
        fn(queue.eng).then_inc(self.sem, 16)
        return (self.sem, self.n)


class Bank:
    def __init__(self, ap):
        self.ap, self.free = ap, []


def program(nc, A, dumps=None):
    ctx = ExitStack()
    with ctx:
        def sem(name):
            return ctx.enter_context(nc.semaphore(name))

        def at(name, shape, dt, kb):
            return nc.alloc_sbuf_tensor_at(name, shape, dt, offset=BASE + int(kb * KB))

        P, V, S, G, Y = (Queue(e, sem(f"q_{n}")) for n, e in (
            ("pe", nc.tensor), ("dve", nc.vector), ("act", nc.scalar), ("pool", nc.gpsimd), ("sp", nc.sync)))

        def count(name):
            return Count(sem(name))

        banks = [Bank(ctx.enter_context(nc.psum_tensor(f"bank{i}", [128, 512], F))) for i in range(8)]

        X = at("X", [128, 8, T], F, 0)
        H = [at(f"H{i}", [128, 2, 8, T], R, 16 + 32 * i) for i in range(2)]
        raw = [at(f"raw{i}", [128, 1024], F, 80 + 4 * i) for i in range(6)]
        whi = [at(f"whi{i}", [128, 1024], R, 104 + 4 * i) for i in range(3)]
        wlo = [at(f"wlo{i}", [128, 1024], R, 116 + 4 * i) for i in range(3)]
        ident = at("ident", [128, 128], F, 128)
        ones = at("ones", [128, 128], F, 128.5)
        bones = at("bones", [128, 128], F, 129)
        permF = at("permF", [128, 128], F, 129.5)
        permA = at("permA", [128, 128], F, 130)
        permB = at("permB", [128, 128], F, 130.5)
        triu = at("triu", [128, 128], F, 131)
        vec = at("vec", [128, 128], F, 131.5)
        st = [at(f"st{i}", [128, 8], F, 132 + i / 32) for i in range(4)]
        keep = at("keep", [128, 96], F, 132.25)
        keepi = at("keepi", [128, 16], U32, 132.75)
        io32 = at("io32", [128, 32], F, 133)
        bro = at("bro", [128, 36], F, 133.25)
        wr = at("wr", [128, 8, 36], F, 133.5)
        rbc = at("rbc", [128, T], F, 136)
        acc = at("acc", [128, T], F, 138)
        tm = [at(f"tm{i}", [128, T], F, 140 + 2 * i) for i in range(2)]

        c_const = count("s_const")
        for sb_, name in ((ident, "c_ident"), (ones, "c_ones"), (bones, "c_bones"), (permF, "c_permF"),
                          (permA, "c_permA"), (permB, "c_permB"), (triu, "c_triu"), (vec, "vec"),
                          (io32, "c_io32"), (bro, "b_router"), (wr, "w_router")):
            src = A[name]
            if name == "w_router":
                src = src.rearrange("p (k n) -> p k n", n=36)
            c_ready = c_const.load(Y, lambda e, a=sb_, b=src: e.dma_start(a[:], b))
        c_x = count("s_x")
        x_load = [c_x.load(Y, lambda e: e.dma_start(X[:, :, :], A["xT"].rearrange("p (k t) -> p k t", t=T)))]
        VEC = {}
        for n, (name, w) in enumerate(VECS):
            VEC[name] = sum(k for _, k in VECS[:n])

        nsink = at("nsink", [128, 8], F, 134.625)
        t_ns = V.do(lambda e: e.tensor_scalar(nsink[:, :], vec[:, VEC["sink"]:VEC["sink"] + 8], -1.0, None,
                                              ALU.mult), c_ready)

        def col(name, i=0, p0=0, p1=128):
            c = VEC[name] + i
            return vec[p0:p1, c:c + 1]

        class Stream:
            def __init__(self, name, chunks, guard):
                self.chunks, self.sems = chunks, [count(f"s_{name}{i}") for i in range(6)]
                self.raw_free = [list(guard) for _ in range(6)]
                self.split_free = [list(guard) for _ in range(3)]
                self.loaded, self.ready, self.done_load, self.done_split = {}, {}, 0, 0
                for _ in range(min(6, len(chunks))):
                    self.load()

            def load(self):
                c = self.done_load
                if c >= len(self.chunks):
                    return
                ap, kt, m = self.chunks[c]
                self.loaded[c] = self.sems[c % 6].load(
                    Y, lambda e: e.dma_start(raw[c % 6][:, 0:kt * m], ap), self.raw_free[c % 6])
                self.done_load += 1

            def split_to(self, last):
                while self.done_split <= min(last, len(self.chunks) - 1):
                    c = self.done_split
                    _, kt, m = self.chunks[c]
                    r, h, lo = raw[c % 6][:, 0:kt * m], whi[c % 3][:, 0:kt * m], wlo[c % 3][:, 0:kt * m]
                    th = S.do(lambda e, r=r, h=h: e.copy(h, r), self.loaded[c], self.split_free[c % 3])
                    tl = V.do(lambda e, r=r, h=h, lo=lo: e.tensor_tensor(lo, r, h.bitcast(F), ALU.subtract),
                              th, self.loaded[c], self.split_free[c % 3])
                    self.ready[c] = [th, tl]
                    self.raw_free[c % 6] = [th, tl]
                    self.done_split += 1
                    self.load()

            def used(self, c, token):
                self.split_free[c % 3] = [token]

        bank_turn = [0]

        def gemm(stream, parts, pool, m=128):
            bank = banks[pool[bank_turn[0] % len(pool)]]
            bank_turn[0] += 1
            out = bank.ap[0:m, :]
            P.wait(bank.free)
            total = sum(len(tiles) for _, tiles in parts) * 3
            n = 0
            for c, tiles in parts:
                stream.split_to(c)
                P.wait(stream.ready[c])
                for k, (hi, lo, tok) in enumerate(tiles):
                    P.wait(tok)
                    wh = whi[c % 3][:, k * m:(k + 1) * m]
                    wl = wlo[c % 3][:, k * m:(k + 1) * m]
                    for w, x in ((wh, hi), (wh, lo), (wl, hi)):
                        fn = lambda e, w=w, x=x, n=n: e.matmul(out, w, x, start=(n == 0), stop=(n == total - 1))
                        n += 1
                        if k == len(tiles) - 1 and w is wl:
                            tok = P.do(fn)
                        else:
                            P.plain(fn)
                stream.used(c, tok)
                stream.split_to(c + 2)
            return bank, tok

        sq_free = [[], []]

        class Norm:

            def __init__(self, Hn, gname, acc_free=()):
                self.H, self.g, self.tok = Hn, gname, {}
                self.acc_tok = list(acc_free)

            def tile(self, i, xtok, free, split=True, f32=None):
                if split:
                    hi, lo = self.H[:, 0, i, :], self.H[:, 1, i, :]
                    th = S.do(lambda e: e.activation(hi, X[:, i, :], ACT.Identity, bias=0.0, scale=col(self.g, i)),
                              xtok, free, c_ready)
                    tl = V.do(lambda e: e.scalar_tensor_tensor(lo, X[:, i, :], col(self.g, i), hi.bitcast(F),
                                                               ALU.mult, ALU.subtract), th, xtok, free)
                    self.tok[i] = [th, tl]
                elif f32 is not None:
                    self.tok[i] = [S.do(lambda e: e.activation(f32[:, i, :], X[:, i, :], ACT.Identity, bias=0.0,
                                                               scale=col(self.g, i)), xtok, free)]
                if i == 0:
                    self.acc_tok = [S.do(lambda e: e.activation(acc[:, :], X[:, i, :], ACT.Square),
                                         xtok, self.acc_tok)]
                else:
                    q = tm[i % 2]
                    ts = S.do(lambda e: e.activation(q[:, :], X[:, i, :], ACT.Square), xtok, sq_free[i % 2])
                    self.acc_tok = [V.do(lambda e: e.tensor_tensor(acc[:, :], acc[:, :], q[:, :], ALU.add),
                                         ts, self.acc_tok)]
                    sq_free[i % 2] = list(self.acc_tok)

            def tiles(self):
                return [(self.H[:, 0, i, :], self.H[:, 1, i, :], self.tok[i]) for i in range(8)]

            def finish(self, bank, rfree):
                tp = P.do(lambda e: e.matmul(bank.ap[:, :], ones[:, :], acc[:, :], start=True, stop=True),
                          self.acc_tok, bank.free, c_ready)
                self.acc_read = [tp]
                t = S.do(lambda e: e.activation(rbc[:, :], bank.ap[:, :], ACT.Ln, bias=col("eps"), scale=1.0 / D),
                         tp, rfree)
                bank.free = [t]
                self.r = [S.do(lambda e: e.activation(rbc[:, :], rbc[:, :], ACT.Exp, scale=-0.5), t)]

        def table(name, *tokens):
            S.plain(lambda e: e.preload_act_table_set(name), *tokens)

        def transpose(out, in_, idn):
            return lambda e: e.transpose(out, in_, idn)

        def attention(pairs, PT, Pb, scale, pt_free, p_free, names, cap_evac):
            units = []
            for pi, pr in enumerate(pairs):
                for hd in range(2):
                    for b in range(4):
                        units.append((pi, hd, b))
            n = len(units)
            state = {}
            pt_ready = {}
            pfree = [list(p_free) for _ in Pb]
            ptfree = [list(pt_free), list(pt_free)]
            sfree = [[] for _ in st]
            SB, TB, OB = names

            def scores(u):
                pi, hd, b = units[u]
                pr = pairs[pi]
                lo, hi = pr["kbs"][b]
                nk = (hi - lo) * 128
                bank = banks[SB[u % len(SB)]]
                q, k = pr["q"](hd, b), pr["k"](hd, lo, hi)
                ts = P.do(lambda e: e.matmul(bank.ap[:, 0:nk], q, k, start=True, stop=True),
                          bank.free, pr["ready"](hd, b))
                pb, s = Pb[u % len(Pb)], st[u % 4]
                if pr["mask"]:
                    m = pr["mask"](hd, b)
                    tv = V.do(lambda e: e.tensor_tensor_reduce(out=pb[:, 0:nk], in0=bank.ap[:, 0:nk], in1=m,
                                                               scale=1.0, scalar=-3e38, op0=ALU.add, op1=ALU.max,
                                                               accum_out=s[:, 0:1]),
                              ts, pfree[u % len(Pb)], sfree[u % 4],
                              pr["mask_ready"](hd) if callable(pr["mask_ready"]) else pr["mask_ready"])
                    bank.free = [tv]
                    pr["mask_used"](hd, b, tv)
                    src = pb
                else:
                    tv = V.do(lambda e: e.tensor_reduce(s[:, 0:1], bank.ap[:, 0:nk], AX, ALU.max),
                              ts, sfree[u % 4])
                    src = bank.ap
                if pr["sink"] is not None:
                    ns, sk = pr["sink"](hd)
                    tn = V.do(lambda e: e.tensor_scalar(s[:, 1:2], s[:, 0:1], -scale, ns, ALU.mult, ALU.min), tv)
                else:
                    tn = V.do(lambda e: e.tensor_scalar(s[:, 1:2], s[:, 0:1], -scale, None, ALU.mult), tv)
                te = S.do(lambda e: e.activation(pb[:, 0:nk], src[:, 0:nk], ACT.Exp, bias=s[:, 1:2], scale=scale,
                                                 accum_out=s[:, 2:3]), tn, tv, ts, pfree[u % len(Pb)])
                if not pr["mask"]:
                    bank.free = [te]
                toks = [te]
                if pr["sink"] is not None:
                    toks.append(S.do(lambda e: e.activation(s[:, 3:4], s[:, 1:2], ACT.Exp, bias=sk, scale=1.0), tn))
                state[u] = toks

            def norm(u):
                pi, hd, b = units[u]
                lo, hi = pairs[pi]["kbs"][b]
                nk = (hi - lo) * 128
                pb, s = Pb[u % len(Pb)], st[u % 4]
                t = state[u]
                if pairs[pi]["sink"] is not None:
                    t = [V.do(lambda e: e.tensor_tensor(s[:, 2:3], s[:, 2:3], s[:, 3:4], ALU.add), t)]
                tr = V.do(lambda e: e.reciprocal(s[:, 4:5], s[:, 2:3]), t)
                tg = G.do(lambda e: e.tensor_scalar(pb[:, 0:nk], pb[:, 0:nk], s[:, 4:5], 1.0, ALU.mult, ALU.mult),
                          tr, state[u])
                sfree[u % 4] = [tg]
                state[u] = [tg]

            def turn(u):
                pi, hd, b = units[u]
                lo, hi = pairs[pi]["kbs"][b]
                pb = Pb[u % len(Pb)]
                bank = banks[TB[u % len(TB)]]
                P.wait(state[u], bank.free)
                for j in range(hi - lo):
                    fn = transpose(bank.ap[:, j * 128:(j + 1) * 128], pb[:, j * 128:(j + 1) * 128], ident[:, :])
                    if j == hi - lo - 1:
                        tt = P.do(fn)
                    else:
                        P.plain(fn)
                pfree[u % len(Pb)] = [tt]
                dst = PT[hd][:, lo:hi, b * 128:(b + 1) * 128]
                srcb = bank.ap[:, 0:(hi - lo) * 128].rearrange("p (k q) -> p k q", q=128)
                if u % 2:
                    tc = S.do(lambda e: e.copy(dst, srcb), tt, ptfree[hd])
                else:
                    tc = V.do(lambda e: e.tensor_copy(dst, srcb), tt, ptfree[hd])
                bank.free = [tc]
                pt_ready.setdefault(pi, []).append(tc)

            def values(pi):
                pr = pairs[pi]
                bank = banks[OB[pi % len(OB)]]
                P.wait(bank.free, pt_ready[pi], pr["v_ready"])
                full = all(k == (0, 4) for k in pr["kbs"])
                for kb in range(4):
                    qs = [b for b in range(4) if pr["kbs"][b][0] <= kb < pr["kbs"][b][1]]
                    q0, q1 = qs[0] * 128, (qs[-1] + 1) * 128
                    for hd in range(2):
                        fn = lambda e, kb=kb, hd=hd, q0=q0, q1=q1: e.matmul(
                            bank.ap[64 * hd:64 * hd + 64, q0:q1], pr["v"](kb, hd), PT[hd][:, kb, q0:q1],
                            start=(kb == 0), stop=(kb == 3), skip_group_check=not full)
                        if kb == 3 and hd == 1:
                            to = P.do(fn)
                        else:
                            P.plain(fn)
                ptfree[0], ptfree[1] = [to], [to]
                bank.free = pr["out"](bank, to)

            for t in range(n + 2):
                if t < n:
                    scores(t)
                if 1 <= t <= n:
                    norm(t - 1)
                if t >= 2:
                    u = t - 2
                    if u % 8 == 0 and u > 0:
                        values(u // 8 - 1)
                    turn(u)
            values(len(pairs) - 1)
            return [P.n and (P.sem, P.n)]

        W1 = []
        for i in range(6):
            W1.append((A["w1_in"][i], 8, 128))
        for i in range(12):
            W1.append((A["w1_conv"][i], 8, 128))
        for i in range(8):
            W1 += [(A["w1_ga"][i], 8, 128), (A["w1_ap"][i], 4, 128), (A["w1_gc"][i], 8, 128), (A["w1_cp"][i], 4, 128)]
        for i in range(8):
            W1.append((A["w1_out"][i], 8, 128))

        stream = Stream("a", W1, [])
        cur = [0]

        def nxt():
            cur[0] += 1
            return cur[0] - 1

        c_t = count("s_tabs")
        ropeF = at("ropeF", [128, 2, T], F, 156)
        maskF = at("maskF", [128, 384], F, 160)
        zero = at("zero", [128, 1024], F, 200)
        t_tab = c_t.load(Y, lambda e: e.dma_start(ropeF[:, :, :], A["c_ropeF"].rearrange("p (a t) -> p a t", a=2)))
        t_tab = c_t.load(Y, lambda e: e.dma_start(maskF[:, :], A["c_maskF"]))

        c_zero = count("s_zero")
        t_z = G.do(lambda e: e.memset(zero[:, :], 0.0))
        for i in range(SLOTS // 128):
            zeroed = c_zero.load(Y, lambda e, i=i: e.dma_start(A["hbuf"][i * 128:(i + 1) * 128, :], zero[:, :]), t_z)

        table("natural_log_exp_and_others")
        n1 = Norm(H[0], "g1")
        for i in range(8):
            n1.tile(i, x_load, [])
        n1.finish(banks[7], [])
        G8 = [0, 1, 2, 3]

        qF = at("qF", [128, 4, T], F, 144)
        kF = at("kF", [128, T], F, 152)
        vF = at("vF", [128, 4, 128], F, 154)
        qz = [at(f"qz{i}", [128, T], F, 188 + 2 * i) for i in range(2)]
        qs = [at(f"qs{i}", [128, T], F, 192 + 2 * i) for i in range(2)]
        qn = [at(f"qn{i}", [128, T], F, 196 + 2 * i) for i in range(2)]

        def head_norm_rope(i, bank, tok, r, g, perm, rope, dst, fr, extra, Z=None):
            z, s, m = Z[0][i % 2], Z[1][i % 2], Z[2][i % 2]
            f = fr.setdefault(i % 2, [])
            t1 = V.do(lambda e: e.tensor_tensor(z[:, :], bank.ap[:, :], r[:, :], ALU.mult), tok, extra, f)
            bank.free = [t1]
            t2 = S.do(lambda e: e.activation(s[:, :], z[:, :], ACT.Square), t1, f)
            b2 = banks[4 + i % 2]
            t3 = P.do(lambda e: e.matmul(b2.ap[:, :], bones[:, :], s[:, :], start=True, stop=True), t2, b2.free)
            t4 = S.do(lambda e: e.activation(s[:, :], b2.ap[:, :], ACT.Ln, bias=col("eps"), scale=1.0 / 64), t3)
            b2.free = [t4]
            t5 = S.do(lambda e: e.activation(s[:, :], s[:, :], ACT.Exp, scale=-0.5), t4)
            t6 = V.do(lambda e: e.scalar_tensor_tensor(m[:, :], z[:, :], g, s[:, :], ALU.mult, ALU.mult), t5, t1, f)
            return rope_only(i, m, t6, perm, rope, dst, fr, extra, z, s, 128)

        def rope_only(i, m, t6, perm, rope, dst, fr, extra, z, s, M):
            b3 = banks[6 + i % 2]
            t7 = P.do(lambda e: e.matmul(b3.ap[0:M, :], perm[0:M, 0:M], m[0:M, :], start=True, stop=True),
                      t6, b3.free)
            t8 = G.do(lambda e: e.tensor_tensor(z[0:M, :], m[0:M, :], rope[0:M, 0, :], ALU.mult), t6, extra)
            t9 = V.do(lambda e: e.tensor_tensor(s[0:M, :], b3.ap[0:M, :], rope[0:M, 1, :], ALU.mult), t7, t6, extra)
            b3.free = [t9]
            t10 = V.do(lambda e: e.tensor_tensor(dst, z[0:M, :], s[0:M, :], ALU.add), t8, t9, extra)
            fr[i % 2] = [t10, t7]
            return [t10]

        fr = {}
        qk_ready = {}
        pend = []
        rX = [n1.r, t_tab]

        def later(fn):
            pend.append(fn)
            while len(pend) > 1:
                pend.pop(0)()

        def flush():
            while pend:
                pend.pop(0)()

        ZF = (qz, qs, qn)
        for i in range(6):
            bank, tok = gemm(stream, [(nxt(), n1.tiles())], G8)
            if i < 4:
                def w(i=i, bank=bank, tok=tok):
                    qk_ready[i] = head_norm_rope(i, bank, tok, rbc, col("qg"), permF, ropeF, qF[:, i, :], fr, rX, ZF)
            elif i == 4:
                def w(i=i, bank=bank, tok=tok):
                    qk_ready["k"] = head_norm_rope(i, bank, tok, rbc, col("kg"), permF, ropeF, kF[:, :], fr, rX, ZF)
            else:
                def w(i=i, bank=bank, tok=tok):
                    z = qz[i % 2]
                    t1 = V.do(lambda e: e.tensor_tensor(z[:, :], bank.ap[:, :], rbc[:, :], ALU.mult), tok, rX,
                              fr.get(i % 2))
                    bank.free = [t1]
                    b2 = banks[4 + i % 2]
                    P.wait(t1, b2.free)
                    for b in range(4):
                        f = transpose(b2.ap[:, b * 128:(b + 1) * 128], z[:, b * 128:(b + 1) * 128], ident[:, :])
                        if b < 3:
                            P.plain(f)
                        else:
                            t2 = P.do(f)
                    t3 = V.do(lambda e: e.tensor_copy(vF[:, :, :], b2.ap[:, :].rearrange("p (a b) -> p a b", b=128)), t2)
                    b2.free = [t3]
                    qk_ready["v"] = [t3]
            later(w)

        upad = [at(f"upad{i}", [128, T + 2], F, 183 + 2.25 * i) for i in range(2)]
        cf = [at(f"cf{i}", [128, T], F, 162 + 2 * i) for i in range(6)]
        t_pad = []
        for i in range(2):
            t_pad.append(V.do(lambda e, i=i: e.memset(upad[i][:, 0:1], 0.0)))
            t_pad.append(V.do(lambda e, i=i: e.memset(upad[i][:, T + 1:T + 2], 0.0)))
        H1 = H[1][:, :, :, :].rearrange("p a k t -> p (a k) t")
        attn_hi, attn_lo = (lambda i: H1[:, i, :]), (lambda i: H1[:, 4 + i, :])
        conv_hi, conv_lo = (lambda i: H1[:, 8 + i, :]), (lambda i: H1[:, 12 + i, :])
        conv_tok, cfree = {}, [[], []]
        for i in range(4):
            bc = gemm(stream, [(nxt(), n1.tiles())], G8)
            if i == 0:
                flush()
            bx = gemm(stream, [(nxt(), n1.tiles())], G8)
            bb = gemm(stream, [(nxt(), n1.tiles())], G8)
            u, (ta, tb, tc) = upad[i % 2], cf[3 * (i % 2):3 * (i % 2) + 3]
            f = cfree[i % 2]
            a1 = V.do(lambda e: e.tensor_tensor(ta[:, :], bc[0].ap[:, :], rbc[:, :], ALU.mult), bc[1], n1.r, f)
            bc[0].free = [a1]
            a2 = V.do(lambda e: e.tensor_tensor(tb[:, :], bx[0].ap[:, :], rbc[:, :], ALU.mult), bx[1], f)
            bx[0].free = [a2]
            a3 = V.do(lambda e: e.tensor_tensor(u[:, 1:T + 1], ta[:, :], tb[:, :], ALU.mult), a1, a2, t_pad, f)
            a4 = S.do(lambda e: e.activation(tc[:, :], u[:, 1:T + 1], ACT.Identity, bias=col("cvb", i),
                                             scale=col("cv1", i)), a3, f)
            a5 = V.do(lambda e: e.scalar_tensor_tensor(ta[:, :], u[:, 0:T], col("cv0", i), tc[:, :],
                                                       ALU.mult, ALU.add), a4, a3)
            a6 = V.do(lambda e: e.scalar_tensor_tensor(tb[:, :], u[:, 2:T + 2], col("cv2", i), ta[:, :],
                                                       ALU.mult, ALU.add), a5)
            a7 = V.do(lambda e: e.tensor_tensor(tc[:, :], bb[0].ap[:, :], rbc[:, :], ALU.mult), bb[1], a5)
            bb[0].free = [a7]
            a8 = V.do(lambda e: e.tensor_tensor(ta[:, :], tc[:, :], tb[:, :], ALU.mult), a6, a7)
            a9 = S.do(lambda e: e.copy(conv_hi(i), ta[:, :]), a8)
            a10 = V.do(lambda e: e.tensor_tensor(conv_lo(i), ta[:, :], conv_hi(i).bitcast(F), ALU.subtract), a9)
            cfree[i % 2] = [a10]
            conv_tok[i] = [a9, a10]

        PTF = [at(f"PTF{i}", [128, 4, T], F, 162 + 8 * i) for i in range(2)]
        PbF = [at(f"PbF{i}", [128, 384], F, 188 + 1.5 * i) for i in range(4)]
        before = [(V.sem, V.n), (S.sem, S.n), (G.sem, G.n), (P.sem, P.n)]
        attn_tok = {}

        def split_out(hi, lo, view=None):
            def out(bank, to):
                src = view(bank.ap) if view else bank.ap[:, :]
                a = S.do(lambda e: e.copy(hi, src), to)
                b = V.do(lambda e: e.tensor_tensor(lo, src, hi.bitcast(F), ALU.subtract), a, to)
                return [a, b]
            return out

        KBS = [(0, 2), (0, 3), (1, 4), (2, 4)]
        prs = []
        for i in range(4):
            def out(bank, to, i=i):
                attn_tok[i] = split_out(attn_hi(i), attn_lo(i))(bank, to)
                return attn_tok[i]

            prs.append(dict(
                q=lambda hd, b, i=i: qF[64 * hd:64 * hd + 64, i, b * 128:(b + 1) * 128],
                k=lambda hd, lo, hi: kF[64 * hd:64 * hd + 64, lo * 128:hi * 128],
                kbs=KBS, ready=lambda hd, b, i=i: [qk_ready[i], qk_ready["k"]],
                mask=lambda hd, b: maskF[:, 128 if b == 0 else 0:256 if b == 3 else 384],
                mask_ready=[t_tab, t_ns], mask_used=lambda *a: None,
                sink=lambda hd, i=i: (nsink[:, i + 4 * hd:i + 4 * hd + 1], col("sink", i + 4 * hd)),
                v=lambda kb, hd: vF[:, kb, 64 * hd:64 * hd + 64], v_ready=qk_ready["v"], out=out))
        attention(prs, PTF, PbF, 0.125, before, before, ([0, 1, 2], [3, 4], [5, 6]), None)

        table("sigmoid_and_others")
        M1 = at("M1", [128, 2, 8, T], R, 144)
        gm = [at(f"gm{i}", [128, T], F, 176 + 2 * i) for i in range(8)]
        before = [(V.sem, V.n), (S.sem, S.n), (G.sem, G.n), (P.sem, P.n)]
        gfree = [list(before), list(before)]
        merged = {}
        at_tiles = [(attn_hi(k), attn_lo(k), attn_tok[k]) for k in range(4)]
        cv_tiles = [(conv_hi(k), conv_lo(k), conv_tok[k]) for k in range(4)]
        AB = [0, 1, 2, 3, 4, 5, 6, 7]
        for i in range(8):
            ga = gemm(stream, [(nxt(), n1.tiles())], AB)
            ap = gemm(stream, [(nxt(), at_tiles)], AB)
            gc = gemm(stream, [(nxt(), n1.tiles())], AB)
            cp = gemm(stream, [(nxt(), cv_tiles)], AB)
            a, b, c, d = gm[4 * (i % 2):4 * (i % 2) + 4]
            f = gfree[i % 2]
            t1 = V.do(lambda e: e.tensor_tensor(a[:, :], ga[0].ap[:, :], rbc[:, :], ALU.mult), ga[1], f)
            ga[0].free = [t1]
            t2 = S.do(lambda e: e.activation(a[:, :], a[:, :], ACT.Sigmoid), t1)
            t3 = V.do(lambda e: e.tensor_tensor(b[:, :], a[:, :], ap[0].ap[:, :], ALU.mult), t2, ap[1], f)
            ap[0].free = [t3]
            t4 = V.do(lambda e: e.tensor_tensor(c[:, :], gc[0].ap[:, :], rbc[:, :], ALU.mult), gc[1], f)
            gc[0].free = [t4]
            t5 = S.do(lambda e: e.activation(c[:, :], c[:, :], ACT.Sigmoid), t4)
            t6 = V.do(lambda e: e.tensor_tensor(d[:, :], c[:, :], cp[0].ap[:, :], ALU.mult), t5, cp[1], f)
            cp[0].free = [t6]
            t7 = V.do(lambda e: e.tensor_tensor(b[:, :], b[:, :], d[:, :], ALU.add), t3, t6)
            t8 = S.do(lambda e: e.copy(M1[:, 0, i, :], b[:, :]), t7, before)
            t9 = V.do(lambda e: e.tensor_tensor(M1[:, 1, i, :], b[:, :], M1[:, 0, i, :].bitcast(F), ALU.subtract),
                      t8, before)
            gfree[i % 2] = [t9]
            merged[i] = [t8, t9]
        table("natural_log_exp_and_others")
        r_read = [(V.sem, V.n)]

        XG = at("XG", [128, 8, T], F, 176)
        m_tiles = [(M1[:, 0, k, :], M1[:, 1, k, :], merged[k]) for k in range(8)]
        n2 = Norm(None, "g2", n1.acc_read)
        lg = banks[7]
        h_dead = [(P.sem, P.n)]
        gates_done = [(V.sem, V.n), (S.sem, S.n)]

        GU = [[at("GU00", [128, 8, 512], F, 16), at("GU01", [128, 8, 512], F, 32)],
              [at("GU10", [128, 8, 512], F, 64), at("GU11", [128, 8, 512], F, 80)],
              [at("GU20", [128, 8, 512], F, 112), at("GU21", [128, 8, 512], F, 144)]]
        DN = [[at("DN00", [128, 2, 1024], F, 48), at("DN01", [128, 2, 1024], F, 56)],
              [at("DN10", [128, 2, 1024], F, 96), at("DN11", [128, 2, 1024], F, 104)],
              [at("DN20", [128, 2, 1024], F, 160), at("DN21", [128, 2, 1024], F, 168)]]
        c_gu = [count(f"s_gu{i}") for i in range(3)]
        c_dn = [count(f"s_dn{i}") for i in range(3)]
        gu_at, dn_at = {}, {}

        def load_pair(p, *tokens):
            s = p % 3
            for j in range(2):
                gu_at[p] = c_gu[s].load(Y, lambda e, j=j: e.dma_start(
                    GU[s][j][:, :, :], A["w_gu"][2 * p + j].rearrange("p (k n) -> p k n", n=512)), *tokens)
            for j in range(2):
                dn_at[p] = c_dn[s].load(Y, lambda e, j=j: e.dma_start(
                    DN[s][j][:, :, :], A["w_dn"][2 * p + j].rearrange("p (k n) -> p k n", n=1024)), *tokens)

        def logits(k):
            P.wait(lg.free, n2.tok[k], c_ready)
            fn = lambda e: e.matmul(lg.ap[0:36, :], wr[:, k, :], XG[:, k, :], start=(k == 0), stop=(k == 7))
            if k == 7:
                return P.do(fn)
            P.plain(fn)

        for i in range(8):
            bank, tok = gemm(stream, [(nxt(), m_tiles)], [0, 1, 2, 3])
            if i == 0:
                load_pair(0, h_dead)
            if i >= 1:
                logits(i - 1)
            xt = V.do(lambda e: e.tensor_tensor(X[:, i, :], X[:, i, :], bank.ap[:, :], ALU.add), tok, x_load)
            bank.free = [xt]
            n2.tile(i, [xt], gates_done, split=False, f32=XG)
        t_lg = logits(7)
        w_done = [(P.sem, P.n)]
        load_pair(1, w_done, (V.sem, V.n), (S.sem, S.n))
        rc = keep[:, 0:4]
        sc = banks[4]
        P.wait(sc.free, n2.acc_tok)
        for b in range(4):
            fn = lambda e, b=b: e.matmul(sc.ap[:, b:b + 1], acc[:, b * 128:(b + 1) * 128], ones[:, 0:1],
                                         start=True, stop=True)
            if b < 3:
                P.plain(fn)
            else:
                ts = P.do(fn)
        t1 = S.do(lambda e: e.activation(rc, sc.ap[:, 0:4], ACT.Ln, bias=col("eps"), scale=1.0 / D), ts)
        sc.free = [t1]
        t_rc = S.do(lambda e: e.activation(rc, rc, ACT.Exp, scale=-0.5), t1)
        n2.finish(banks[5], r_read)
        n2r = n2.r

        lgs = at("lgs", [36, T], F, 192)
        t1 = V.do(lambda e: e.tensor_copy(lgs[:, :], lg.ap[0:36, :]), t_lg, gates_done)
        lg.free = [t1]
        lb = banks[6]
        P.wait(t1, lb.free)
        for b in range(4):
            fn = transpose(lb.ap[:, b * 36:(b + 1) * 36], lgs[:, b * 128:(b + 1) * 128], ident[0:36, 0:36])
            if b < 3:
                P.plain(fn)
            else:
                t_lt = P.do(fn)

        rows = [at(f"rows{b}", [128, D], F, 144 + 4 * b) for b in range(4)]
        row_tok = {b: [] for b in range(4)}
        n = 0
        for b in range(4):
            for hf in range(2):
                bank = banks[n % 4]
                P.wait(bank.free, n2.tok[7])
                for k in range(4):
                    fn = transpose(bank.ap[:, k * 128:(k + 1) * 128], XG[:, 4 * hf + k, b * 128:(b + 1) * 128],
                                   ident[:, :])
                    if k < 3:
                        P.plain(fn)
                    else:
                        t1 = P.do(fn)
                dst = rows[b][:, hf * 512:(hf + 1) * 512]
                t2 = S.do(lambda e: e.activation(dst, bank.ap[:, :], ACT.Copy, bias=0.0, scale=rc[:, b:b + 1]),
                          t1, t_rc, w_done)
                bank.free = [t2]
                row_tok[b].append(t2)
                n += 1

        off = [194.0]

        def small(name, *shape):
            n = int(np.prod(shape))
            t = at(name, [128] + list(shape), F, off[0])
            off[0] += max(n * 4, 32) / 1024
            return t

        L = small("L", 4, 36)
        last = None
        for b in range(4):
            last = V.do(lambda e: e.scalar_tensor_tensor(L[:, b, :], lb.ap[:, b * 36:(b + 1) * 36], rc[:, b:b + 1],
                                                         bro[:, :], ALU.mult, ALU.add), t_lt, t_rc, c_ready)
        lb.free = [last]
        GL = L[:, :, 0:4]
        EL = L[:, :, 4:36].rearrange("p t (g e) -> p t g e", e=8)

        def v(fn, *tokens):
            return V.do(fn, (V.sem, V.n), *tokens)

        def first_max(vals, n, name):
            mx, df, ix, mi, oh = (small(name + c, 4, 1 if c in "mi" else n) for c in ("m", "d", "x", "i", "o"))
            v(lambda e: e.tensor_reduce(mx[:, :, :], vals, AX, ALU.max))
            v(lambda e: e.tensor_tensor(df[:, :, :], vals, mx[:, :, :].to_broadcast([128, 4, n]), ALU.is_ge))
            v(lambda e: e.tensor_scalar(ix[:, :, :], df[:, :, :], -100.0, 100.0, ALU.mult, ALU.add))
            v(lambda e: e.tensor_tensor(ix[:, :, :], ix[:, :, :],
                                        io32[:, 0:n].unsqueeze(1).to_broadcast([128, 4, n]), ALU.add))
            v(lambda e: e.tensor_reduce(mi[:, :, :], ix[:, :, :], AX, ALU.min))
            v(lambda e: e.tensor_tensor(oh[:, :, :], ix[:, :, :], mi[:, :, :].to_broadcast([128, 4, n]),
                                        ALU.is_equal))
            return mx, oh

        gmx, goh = first_max(GL, 4, "g")
        gd, gs, pg = small("gd", 4, 4), small("gs", 4, 1), small("pg", 4, 1)
        t1 = v(lambda e: e.tensor_tensor(gd[:, :, :], GL, gmx[:, :, :].to_broadcast([128, 4, 4]), ALU.subtract))
        t2 = S.do(lambda e: e.activation(gd[:, :, :], gd[:, :, :], ACT.Exp), t1)
        ei4, ein = small("ei4", 4, 4, 8), small("ein", 4, 8)
        v(lambda e: e.tensor_tensor(ei4[:, :, :, :], EL, goh[:, :, :].unsqueeze(3).to_broadcast([128, 4, 4, 8]),
                                    ALU.mult))
        v(lambda e: e.tensor_reduce(ein[:, :, :], ei4[:, :, :, :].rearrange("p t g e -> p t e g"), AX, ALU.add))
        v(lambda e: e.tensor_reduce(gs[:, :, :], gd[:, :, :], AX, ALU.add), t2)
        v(lambda e: e.reciprocal(pg[:, :, :], gs[:, :, :]))
        m1, o1 = first_max(ein[:, :, :], 8, "u")
        e2 = small("e2", 4, 8)
        v(lambda e: e.scalar_tensor_tensor(e2[:, :, :], o1[:, :, :], NEG, ein[:, :, :], ALU.mult, ALU.add))
        m2, o2 = first_max(e2[:, :, :], 8, "v")
        dd, ex = small("dd", 4, 1), small("ex", 4, 1)
        t1 = v(lambda e: e.tensor_tensor(dd[:, :, :], m2[:, :, :], m1[:, :, :], ALU.subtract))
        t2 = S.do(lambda e: e.activation(ex[:, :, :], dd[:, :, :], ACT.Exp), t1)
        AS = [small(f"AS{k}", 4, 32) for k in range(3)]
        for k, o in ((0, o1), (1, o2)):
            v(lambda e: e.tensor_tensor(AS[k][:, :, :].rearrange("p t (g e) -> p t g e", e=8),
                                        goh[:, :, :].unsqueeze(3).to_broadcast([128, 4, 4, 8]),
                                        o[:, :, :].unsqueeze(2).to_broadcast([128, 4, 4, 8]), ALU.mult))
        t_as = v(lambda e: e.tensor_tensor(AS[2][:, :, :], AS[0][:, :, :], AS[1][:, :, :], ALU.add))
        dn, gt = small("dn", 4, 1), [small("gt0", 4, 1), small("gt1", 4, 1)]
        v(lambda e: e.tensor_scalar(dn[:, :, :], ex[:, :, :], 1.0, None, ALU.add), t2)
        v(lambda e: e.reciprocal(dn[:, :, :], dn[:, :, :]))
        v(lambda e: e.tensor_tensor(gt[0][:, :, :], dn[:, :, :], pg[:, :, :], ALU.mult))
        v(lambda e: e.tensor_tensor(gt[1][:, :, :], gt[0][:, :, :], ex[:, :, :], ALU.mult))
        rk = banks[6]
        P.wait(t_as, rk.free)
        for b in range(4):
            for b2 in range(b + 1):
                w = triu if b2 == b else ones
                fn = lambda e, b=b, b2=b2, w=w: e.matmul(rk.ap[:, 32 * b:32 * b + 32], w[:, :], AS[2][:, b2, :],
                                                         start=(b2 == 0), stop=(b2 == b))
                if b == 3 and b2 == 3:
                    t_rk = P.do(fn)
                else:
                    P.plain(fn)
        RK = small("RK", 4, 32)
        t1 = v(lambda e: e.tensor_copy(RK[:, :, :], rk.ap[:, 0:128].rearrange("p (t n) -> p t n", n=32)), t_rk)
        rk.free = [t1]
        tmp, rr, es, ok = small("tmp", 4, 32), small("rr", 4), small("es", 4), small("ok", 4)
        gov = small("gov", 2, 4)
        flag = small("flag", 8)
        for k in range(2):
            v(lambda e: e.tensor_tensor(tmp[:, :, :], AS[k][:, :, :], RK[:, :, :], ALU.mult))
            v(lambda e: e.tensor_reduce(rr[:, :], tmp[:, :, :], AX, ALU.add))
            v(lambda e: e.tensor_tensor(tmp[:, :, :], AS[k][:, :, :],
                                        io32[:, :].unsqueeze(1).to_broadcast([128, 4, 32]), ALU.mult))
            v(lambda e: e.tensor_reduce(es[:, :], tmp[:, :, :], AX, ALU.add))
            v(lambda e: e.tensor_scalar(ok[:, :], rr[:, :], float(CAP), None, ALU.is_lt))
            v(lambda e: e.scalar_tensor_tensor(es[:, :], es[:, :], float(CAP), rr[:, :], ALU.mult, ALU.add))
            v(lambda e: e.tensor_tensor(rr[:, :], es[:, :], ok[:, :], ALU.mult))
            v(lambda e: e.tensor_copy(keepi[:, 8 + 4 * k:12 + 4 * k], rr[:, :]))
            v(lambda e: e.tensor_scalar(es[:, :], es[:, :], -4096.0, None, ALU.add))
            v(lambda e: e.tensor_tensor(es[:, :], es[:, :], ok[:, :], ALU.mult))
            v(lambda e: e.tensor_scalar(es[:, :], es[:, :], 4096.0, None, ALU.add))
            t_idx = v(lambda e: e.tensor_copy(keepi[:, 4 * k:4 * k + 4], es[:, :]))
            g = keep[:, 4 + 4 * k:8 + 4 * k]
            v(lambda e: e.tensor_tensor(g, gt[k][:, :, 0], ok[:, :], ALU.mult))
            v(lambda e: e.tensor_tensor(gov[:, k, :], gt[k][:, :, 0], g, ALU.subtract))
            v(lambda e: e.tensor_scalar(flag[:, 4 * k:4 * k + 4], ok[:, :], -1.0, 1.0, ALU.mult, ALU.add))
        GO = at("GO", [128, 4, 32], F, 134.75)
        fl = at("fl", [128, 1], F, 135.25)
        fli = at("fli", [1, 1], I32, 135.375)
        v(lambda e: e.tensor_tensor(GO[:, :, :], AS[0][:, :, :],
                                    gov[:, 0, :].unsqueeze(2).to_broadcast([128, 4, 32]), ALU.mult))
        v(lambda e: e.tensor_tensor(tmp[:, :, :], AS[1][:, :, :],
                                    gov[:, 1, :].unsqueeze(2).to_broadcast([128, 4, 32]), ALU.mult))
        v(lambda e: e.tensor_tensor(GO[:, :, :], GO[:, :, :], tmp[:, :, :], ALU.add))
        t1 = v(lambda e: e.tensor_reduce(fl[:, :], flag[:, :], AX, ALU.add))
        t2 = P.do(lambda e: e.matmul(rk.ap[0:1, 0:1], fl[:, 0:1], ones[:, 0:1], start=True, stop=True), t1, rk.free)
        t_flag = v(lambda e: e.tensor_copy(fli[:, :], rk.ap[0:1, 0:1]), t2)
        rk.free = [t_flag]
        route_done = [(V.sem, V.n), (S.sem, S.n), (P.sem, P.n)]

        c_sc = count("s_scatter")
        for k in range(2):
            for b in range(4):
                t_sc = c_sc.load(G, lambda e, k=k, b=b: e.indirect_dma_start(
                    out=A["hbuf"], out_offset=bass.IndirectOffsetOnAxis(ap=keepi[:, 4 * k + b:4 * k + b + 1], axis=0),
                    in_=rows[b][:, :], in_offset=None, bounds_check=SLOTS - 1, oob_is_err=False),
                    t_idx, row_tok[b], zeroed)
        load_pair(2, w_done, route_done, t_sc)
        for q in (P, V, S, G, Y):
            q.wait(t_flag)
        left_over = nc.values_load(fli[0:1, 0:1], min_val=0, max_val=1024)

        hb = at("hb", [128, D], F, 200)
        hT = [at(f"hT{i}", [128, 8, 128], F, 192 + 4 * i) for i in range(2)]
        yb = at("yb", [128, D], F, 140)
        hid = at("hid", [128, 256], F, 204)
        hidT = at("hidT", [128, 2, 128], F, 205)
        c_hb, c_y = count("s_hb"), count("s_y")
        table("silu_and_others")
        NP = NE // 2
        hb_free, hT_free, hT_tok = [list(route_done)], [list(route_done), list(route_done)], {}
        hid_free, hidT_free, yb_free = [list(route_done)], [list(route_done)], [list(route_done)]
        y_tok = None

        def turn_rows(p):
            t = c_hb.load(Y, lambda e: e.dma_start(hb[:, :], A["hbuf"][p * 128:(p + 1) * 128, :]), t_sc, hb_free[0])
            toks = []
            for hf in range(2):
                bank = banks[hf]
                P.wait(bank.free, t)
                for k in range(4):
                    fn = transpose(bank.ap[:, k * 128:(k + 1) * 128],
                                   hb[:, (4 * hf + k) * 128:(4 * hf + k + 1) * 128], ident[:, :])
                    if k < 3:
                        P.plain(fn)
                    else:
                        t1 = P.do(fn)
                dst = hT[p % 2][:, 4 * hf:4 * hf + 4, :]
                src = bank.ap[:, :].rearrange("p (k q) -> p k q", q=128)
                if hf:
                    t2 = V.do(lambda e: e.tensor_copy(dst, src), t1, hT_free[p % 2])
                else:
                    t2 = S.do(lambda e: e.copy(dst, src), t1, hT_free[p % 2])
                bank.free = [t2]
                toks.append(t2)
            hb_free[0] = [t1]
            hT_tok[p] = toks

        turn_rows(0)
        for p in range(NP):
            s = p % 3
            bank = banks[2 + p % 2]
            P.wait(bank.free, hT_tok[p], gu_at[p])
            for k in range(8):
                for j in range(2):
                    fn = lambda e, k=k, j=j: e.matmul(bank.ap[64 * j:64 * j + 64, :],
                                                      hT[p % 2][:, k, 64 * j:64 * j + 64], GU[s][j][:, k, :],
                                                      start=(k == 0), stop=(k == 7))
                    if k == 7 and j == 1:
                        t1 = P.do(fn)
                    else:
                        P.plain(fn)
            hT_free[p % 2] = [t1]
            t2 = S.do(lambda e: e.activation(hid[:, :], bank.ap[:, 0:256], ACT.Silu), t1, hid_free[0])
            t3 = V.do(lambda e: e.tensor_tensor(hid[:, :], hid[:, :], bank.ap[:, 256:512], ALU.mult), t2, t1)
            bank.free = [t3]
            if p + 1 < NP:
                turn_rows(p + 1)
            tb = banks[4]
            P.wait(t3, tb.free)
            P.plain(transpose(tb.ap[:, 0:128], hid[:, 0:128], ident[:, :]))
            t4 = P.do(transpose(tb.ap[:, 128:256], hid[:, 128:256], ident[:, :]))
            hid_free[0] = [t4]
            t5 = V.do(lambda e: e.tensor_copy(hidT[:, :, :], tb.ap[:, 0:256].rearrange("p (k q) -> p k q", q=128)),
                      t4, hidT_free[0])
            tb.free = [t5]
            toks = []
            for h2 in range(2):
                ob = banks[5 + h2]
                P.wait(t5, dn_at[p], ob.free)
                for k in range(2):
                    for j in range(2):
                        fn = lambda e, k=k, j=j, h2=h2, ob=ob: e.matmul(
                            ob.ap[64 * j:64 * j + 64, :], hidT[:, k, 64 * j:64 * j + 64],
                            DN[s][j][:, k, h2 * 512:(h2 + 1) * 512], start=(k == 0), stop=(k == 1))
                        if k == 1 and j == 1:
                            t6 = P.do(fn)
                        else:
                            P.plain(fn)
                dst = yb[:, h2 * 512:(h2 + 1) * 512]
                if h2:
                    t7 = V.do(lambda e: e.tensor_copy(dst, ob.ap[:, :]), t6, yb_free[0])
                else:
                    t7 = S.do(lambda e: e.copy(dst, ob.ap[:, :]), t6, yb_free[0])
                ob.free = [t7]
                toks.append(t7)
            hidT_free[0] = [t6]
            y_tok = c_y.load(Y, lambda e, p=p: e.dma_start(A["ybuf"][p * 128:(p + 1) * 128, :], yb[:, :]), toks)
            yb_free[0] = [y_tok]
            if p + 3 < NP:
                load_pair(p + 3, t6)
            if p == 13:
                p13 = [t6]
            if p == 14:
                p14 = [t6]
        moe_done = [t6]

        YG = [[at(f"YG{k}{b}", [128, D], F, 144 + 16 * k + 4 * b) for b in range(4)] for k in range(2)]
        c_yg = [count(f"s_yg{b}") for b in range(4)]
        W2 = []
        for i in range(6):
            W2.append((A["w2_in"][i], 8, 128))
        for i in range(5):
            W2.append((A["w2_c"][i], 8, 128))
        W2.append((A["w2_kr"][0], 8, 96))
        for i in range(8):
            W2.append((A["w2_uq"][i], 3, 96))
        for i in range(8):
            W2.append((A["w2_ukv"][i], 2, 128))
        for i in range(8):
            W2.append((A["w2_evo"][i], 8, 128))

        def ffn_chunks(l):
            for q in range(4):
                for i in range(8):
                    W2.append((A[f"w_up{l}"][8 * q + i], 8, 128))
                for i in range(8):
                    W2.append((A[f"w_down{l}"][8 * q + i], 8, 128))

        ffn_chunks(0)
        for i in range(24):
            W2.append((A["w2_qkv"][i], 8, 128))
        for i in range(8):
            W2.append((A["w2_odo"][i], 8, 128))
        ffn_chunks(1)
        stream2 = Stream("b", W2, p13 + p14)
        cur[0] = 0
        c_t2 = count("s_tabs2")

        yg_tok = {}
        for b in range(4):
            for k in range(2):
                yg_tok[b] = c_yg[b].load(G, lambda e, k=k, b=b: e.indirect_dma_start(
                    out=YG[k][b][:, :], out_offset=None, in_=A["ybuf"],
                    in_offset=bass.IndirectOffsetOnAxis(ap=keepi[:, 8 + 4 * k + b:9 + 4 * k + b], axis=0),
                    bounds_check=SLOTS - 1, oob_is_err=False), y_tok, p14)
        xmoe = {}
        n3 = Norm(H[0], "gm0", n2.acc_read)
        bn = 0
        for b in range(4):
            y0, y1 = YG[0][b], YG[1][b]
            t1 = V.do(lambda e: e.tensor_scalar(y0[:, :], y0[:, :], keep[:, 4 + b:5 + b], None, ALU.mult),
                      yg_tok[b], (V.sem, V.n))
            t2 = V.do(lambda e: e.scalar_tensor_tensor(y0[:, :], y1[:, :], keep[:, 8 + b:9 + b], y0[:, :],
                                                       ALU.mult, ALU.add), t1)
            for hf in range(2):
                bank = banks[bn % 8]
                bn += 1
                P.wait(bank.free, t2)
                for k in range(4):
                    fn = transpose(bank.ap[:, k * 128:(k + 1) * 128],
                                   y0[:, (4 * hf + k) * 128:(4 * hf + k + 1) * 128], ident[:, :])
                    if k < 3:
                        P.plain(fn)
                    else:
                        t3 = P.do(fn)
                xs = X[:, 4 * hf:4 * hf + 4, b * 128:(b + 1) * 128]
                t4 = V.do(lambda e: e.tensor_tensor(xs, xs, bank.ap[:, :].rearrange("p (k q) -> p k q", q=128),
                                                    ALU.add), t3)
                bank.free = [t4]
        xmoe = [t4]

        at_branch = [(V.sem, V.n), (S.sem, S.n), (G.sem, G.n), (P.sem, P.n)]
        oq = {q: Queue(q.eng, sem(f"o_{n}")) for q, n in ((P, "pe"), (V, "dve"), (S, "act"))}
        oY = Queue(nc.sync, None)
        oP, oV, oS = oq[P], oq[V], oq[S]
        ow = [count(f"s_ow{i}") for i in range(2)]
        oGU = [at(f"oGU{i}", [128, 8, 512], F, 16 + 16 * i) for i in range(2)]
        oDN = [at(f"oDN{i}", [128, 2, 1024], F, 48 + 8 * i) for i in range(2)]
        odg = at("odg", [128, T], F, 144)
        oa = [at(f"oa{i}", [128, T], F, 146 + 2 * i) for i in range(2)]
        ob_ = [at(f"ob{i}", [128, T], F, 150 + 2 * i) for i in range(2)]

        def rest_load(x, used):
            s = x % 2
            ow[s].load(oY, lambda e: e.dma_start(
                oGU[s][:, :, :], A["w_gu"][x].rearrange("p (k n) -> p k n", n=512)), used)
            return ow[s].load(oY, lambda e: e.dma_start(
                oDN[s][:, :, :], A["w_dn"][x].rearrange("p (k n) -> p k n", n=1024)), used)

        def rest_all():
            gate, ups, outs = banks[0].ap, [b.ap for b in banks[1:5]], [b.ap for b in banks[5:8]]
            free = {i: None for i in range(8)}
            used, hid_used, dg_used, wt, x_tok = {}, None, None, {}, None
            wt[0] = rest_load(0, None)
            wt[1] = rest_load(1, None)
            for x in range(NE):
                s = x % 2
                t0 = None
                for b in range(4):
                    t0 = oV.do(lambda e, b=b: e.tensor_scalar(odg[:, b * 128:(b + 1) * 128], ident[:, :],
                                                              GO[:, b, x:x + 1], None, ALU.mult), dg_used)
                tg = oP.do(lambda e: e.matmul(gate[:, :], ones[:, :], odg[:, :], start=True, stop=True), t0, free[0])
                dg_used = tg
                oP.wait(wt[x])
                hid_tok = []
                for m in range(2):
                    t = []
                    for j in range(2):
                        oP.wait(free[1 + 2 * m + j])
                        for k in range(8):
                            fn = lambda e, k=k: e.matmul(
                                ups[2 * m + j][:, :], oGU[s][:, k, (2 * j + m) * 128:(2 * j + m + 1) * 128],
                                XG[:, k, :], start=(k == 0), stop=(k == 7))
                            if k == 7:
                                t.append(oP.do(fn))
                            else:
                                oP.plain(fn)
                    a, b = oa[m], ob_[m]
                    t1 = oV.do(lambda e: e.tensor_tensor(a[:, :], ups[2 * m][:, :], rbc[:, :], ALU.mult), t[0], hid_used)
                    t2 = oV.do(lambda e: e.tensor_tensor(b[:, :], ups[2 * m + 1][:, :], rbc[:, :], ALU.mult), t[1])
                    free[1 + 2 * m], free[2 + 2 * m] = t1, t2
                    t3 = oS.do(lambda e: e.activation(a[:, :], a[:, :], ACT.Silu), t1)
                    t4 = oV.do(lambda e: e.tensor_tensor(b[:, :], b[:, :], gate[:, :], ALU.mult), t2, tg)
                    free[0] = t4
                    hid_tok.append(oV.do(lambda e: e.tensor_tensor(a[:, :], a[:, :], b[:, :], ALU.mult), t3, t4))
                for i in range(8):
                    n = 5 + i % 3
                    oP.wait(free[n], hid_tok)
                    for k in range(2):
                        fn = lambda e, k=k: e.matmul(outs[n - 5][:, :], oDN[s][:, k, i * 128:(i + 1) * 128],
                                                     oa[k][:, :], start=(k == 0), stop=(k == 1))
                        if k:
                            hid_used = oP.do(fn)
                        else:
                            oP.plain(fn)
                    x_tok = oV.do(lambda e: e.tensor_tensor(X[:, i, :], X[:, i, :], outs[n - 5][:, :], ALU.add),
                                  hid_used, x_tok)
                    free[n] = x_tok
                if x + 2 < NE:
                    wt[x + 2] = rest_load(x + 2, hid_used)

        with nc.If(left_over > 0):
            for q in (oP, oV, oS, oY):
                q.wait(at_branch)
            rest_all()
            for q in (oP, oV, oS, oY):
                q.wait((oP.sem, oP.n), (oV.sem, oV.n), (oS.sem, oS.n))
        table("natural_log_exp_and_others")

        before = [(V.sem, V.n), (S.sem, S.n), (G.sem, G.n), (P.sem, P.n)]
        for i in range(8):
            n3.tile(i, xmoe, moe_done + before)
        n3.finish(banks[7], n2r)
        ropeA = at("ropeA", [128, 2, T], F, 156)
        ropeB = at("ropeB", [96, 2, T], F, 152)
        t_tabA = c_t2.load(Y, lambda e: e.dma_start(ropeA[:, :, :], A["c_ropeA"].rearrange("p (a t) -> p a t", a=2)),
                           before)
        qA = at("qA", [128, 4, T], F, 144)
        kA = at("kA", [128, T], F, 152)
        vA = at("vA", [128, 4, 128], F, 154)
        CH = at("CH", [128, 2, 5, T], R, 182)
        KR = at("KR", [96, T], F, 202)
        wz = [at(f"wz{i}", [128, T], F, 162 + 2 * i) for i in range(2)]
        ws = [at(f"ws{i}", [128, T], F, 166 + 2 * i) for i in range(2)]
        wn = [at(f"wn{i}", [128, T], F, 170 + 2 * i) for i in range(2)]
        facc = [at(f"facc{i}", [128, T], F, 174 + 2 * i) for i in range(2)]
        fq = [at(f"fq{i}", [128, T], F, 178 + 2 * i) for i in range(2)]
        fr = {0: list(before), 1: list(before)}
        rX = [n3.r, t_tabA]
        ZA = (wz, ws, wn)
        qk2 = {}

        def v_natural(i, z, t1, dst, names, p0=0, p1=128):
            b2 = banks[names]
            P.wait(t1, b2.free)
            w = p1 - p0
            for b in range(4):
                f = transpose(b2.ap[:, b * w:(b + 1) * w], z[p0:p1, b * 128:(b + 1) * 128], ident[p0:p1, p0:p1])
                if b < 3:
                    P.plain(f)
                else:
                    t2 = P.do(f)
            t3 = V.do(lambda e: e.tensor_copy(dst, b2.ap[:, 0:4 * w].rearrange("p (a b) -> p a b", b=w)), t2)
            b2.free = [t3]
            return [t3], t2

        for i in range(6):
            bank, tok = gemm(stream2, [(nxt(), n3.tiles())], G8)
            if i < 5:
                def w(i=i, bank=bank, tok=tok):
                    dst, g = (qA[:, i, :], "aqg") if i < 4 else (kA[:, :], "akg")
                    qk2[i if i < 4 else "k"] = head_norm_rope(i, bank, tok, rbc, col(g), permA, ropeA, dst, fr,
                                                              rX, ZA)
            else:
                def w(i=i, bank=bank, tok=tok):
                    z = wz[i % 2]
                    t1 = V.do(lambda e: e.tensor_tensor(z[:, :], bank.ap[:, :], rbc[:, :], ALU.mult), tok, rX,
                              fr.get(i % 2))
                    bank.free = [t1]
                    qk2["v"], fr[i % 2] = v_natural(i, z, t1, vA[:, :, :], 4 + i % 2)
                    fr[i % 2] = [fr[i % 2]]
            later(w)

        c_tok, fac_tok = {}, [[], []]
        for i in range(5):
            bank, tok = gemm(stream2, [(nxt(), n3.tiles())], G8)
            if i == 0:
                flush()
            a = 0 if i < 3 else 1
            th = S.do(lambda e: e.activation(CH[:, 0, i, :], bank.ap[:, :], ACT.Identity, bias=0.0,
                                             scale=col("bg", i)), tok, before)
            q = tm[i % 2]
            dst = facc[a] if i in (0, 3) else q
            ts = S.do(lambda e: e.activation(dst[:, :], bank.ap[:, :], ACT.Square), tok, before,
                      [] if i in (0, 3) else sq_free[i % 2])
            tl = V.do(lambda e: e.scalar_tensor_tensor(CH[:, 1, i, :], bank.ap[:, :], col("bg", i),
                                                       CH[:, 0, i, :].bitcast(F), ALU.mult, ALU.subtract),
                      th, ts, tok, before)
            c_tok[i] = [th, tl]
            if i in (0, 3):
                fac_tok[a] = [ts]
            else:
                fac_tok[a] = [V.do(lambda e: e.tensor_tensor(facc[a][:, :], facc[a][:, :], q[:, :], ALU.add),
                                   ts, fac_tok[a])]
                sq_free[i % 2] = list(fac_tok[a])
            bank.free = [th, tl, ts]
        bank, tok = gemm(stream2, [(nxt(), n3.tiles())], G8, m=96)
        t_krz = V.do(lambda e: e.tensor_tensor(KR[:, :], bank.ap[0:96, :], rbc[0:96, :], ALU.mult), tok, n3.r, before)
        bank.free = [t_krz]
        r2 = wn[0]
        f_ready = []
        t_r2 = V.do(lambda e: e.tensor_tensor(r2[:, :], rbc[:, :], rbc[:, :], ALU.mult), n3.r, fr[0], fr[1])
        for a, w in ((0, 384), (1, 256)):
            bk = banks[4 + a]
            t1 = P.do(lambda e: e.matmul(bk.ap[:, :], ones[:, :], facc[a][:, :], start=True, stop=True),
                      fac_tok[a], bk.free)
            t2 = V.do(lambda e: e.tensor_tensor(facc[a][:, :], bk.ap[:, :], r2[:, :], ALU.mult), t1, t_r2)
            bk.free = [t2]
            t3 = S.do(lambda e: e.activation(facc[a][:, :], facc[a][:, :], ACT.Ln, bias=col("eps"), scale=1.0 / w),
                      t2)
            t4 = S.do(lambda e: e.activation(facc[a][:, :], facc[a][:, :], ACT.Exp, scale=-0.5), t3)
            f_ready.append(V.do(lambda e: e.tensor_tensor(fq[a][:, :], facc[a][:, :], rbc[:, :], ALU.mult), t4, n3.r))

        PTA = [at(f"PTA{i}", [128, 4, T], F, 162 + 8 * i) for i in range(2)]
        PbA = [at(f"PbA{i}", [128, T], F, 16 + 2 * i) for i in range(4)]
        fQ = [at(f"fQ{i}", [128, T], F, 178 + 2 * i) for i in range(2)]
        before = [(V.sem, V.n), (S.sem, S.n), (G.sem, G.n), (P.sem, P.n)]
        FULL = [(0, 4)] * 4
        H1v = H[1]
        mix_tok = {}
        prs = []
        for i in range(4):
            def out(bank, to, i=i):
                mix_tok[i] = split_out(H1v[:, 0, i, :], H1v[:, 1, i, :])(bank, to)
                return mix_tok[i]

            prs.append(dict(
                q=lambda hd, b, i=i: qA[64 * hd:64 * hd + 64, i, b * 128:(b + 1) * 128],
                k=lambda hd, lo, hi: kA[64 * hd:64 * hd + 64, lo * 128:hi * 128],
                kbs=FULL, ready=lambda hd, b, i=i: [qk2[i], qk2["k"]], mask=None, sink=None,
                v=lambda kb, hd: vA[:, kb, 64 * hd:64 * hd + 64], v_ready=qk2["v"], out=out))
        attention(prs, PTA, PbA, 0.125, before, before, ([0, 1, 2], [3, 4], [5, 6]), None)

        before = [(V.sem, V.n), (S.sem, S.n), (G.sem, G.n), (P.sem, P.n)]
        qB = at("qB", [96, 8, T], F, 16)
        kB = at("kB", [96, 8, T], F, 32)
        vB = at("vB", [128, 4, T], F, 144)
        bz = [at(f"bz{i}", [128, T], F, 162 + 2 * i) for i in range(2)]
        bs = [at(f"bs{i}", [128, T], F, 166 + 2 * i) for i in range(2)]
        t_tabB = c_t2.load(Y, lambda e: e.dma_start(ropeB[:, :, :], A["c_ropeB"].rearrange("p (a t) -> p a t", a=2)),
                           before)
        fr = {0: list(before), 1: list(before)}
        rX = [t_tabB, f_ready]
        krt = [KR, None]
        cq = [(CH[:, 0, k, :], CH[:, 1, k, :], c_tok[k]) for k in range(3)]
        ckv = [(CH[:, 0, k, :], CH[:, 1, k, :], c_tok[k]) for k in range(3, 5)]
        t_kr = rope_only(1, KR, t_krz, permB, ropeB, bs[0][0:96, :], fr, [rX, before], bz[1], bs[1], 96)
        t_kc = G.do(lambda e: e.tensor_copy(kB[64:96, :, :], bs[0][64:96, :].unsqueeze(1).to_broadcast([32, 8, T])),
                    t_kr, before)
        fr[0] = [t_kc]
        bq, bk2, bv = {}, {}, {}
        for i in range(8):
            bank, tok = gemm(stream2, [(nxt(), cq)], G8, m=96)

            def w(i=i, bank=bank, tok=tok):
                dst = qB[:, i, :]
                t1 = V.do(lambda e: e.tensor_tensor(dst, bank.ap[0:96, :], fq[0][0:96, :], ALU.mult), tok, rX, before)
                bank.free = [t1]
                bq[i] = rope_only(i, dst, t1, permB, ropeB, dst, fr, [rX, fr[i % 2]], bz[i % 2], bs[i % 2], 96)
            later(w)
        vt_free = [[], []]
        for i in range(8):
            bank, tok = gemm(stream2, [(nxt(), ckv)], G8)
            if i == 0:
                flush()
                vz = [at(f"vz{j}", [128, T], F, 170 + 2 * j) for j in range(2)]

            def w(i=i, bank=bank, tok=tok):
                z = vz[i % 2]
                t1 = V.do(lambda e: e.tensor_tensor(kB[0:64, i, :], bank.ap[0:64, :], fq[1][0:64, :], ALU.mult), tok,
                          rX, before)
                t2 = V.do(lambda e: e.tensor_tensor(z[64:128, :], bank.ap[64:128, :], fq[1][64:128, :], ALU.mult),
                          tok, before, vt_free[i % 2])
                bank.free = [t1, t2]
                bk2[i] = [t1, t_kc]
                bv[i], tf = v_natural(i, z, t2, vB[:, :, 64 * i:64 * i + 64], 4 + i % 2, 64, 128)
                vt_free[i % 2] = [tf]
            later(w)
        flush()
        PTB = [at(f"PTB{i}", [128, 4, T], F, 162 + 8 * i) for i in range(2)]
        PbB = [at(f"PbB{i}", [128, T], F, 182 + 2 * i) for i in range(4)]
        before = [(V.sem, V.n), (S.sem, S.n), (G.sem, G.n), (P.sem, P.n)]
        prs = []
        for i in range(4):
            def out(bank, to, i=i):
                mix_tok[4 + i] = split_out(H1v[:, 0, 4 + i, :], H1v[:, 1, 4 + i, :])(bank, to)
                return mix_tok[4 + i]

            prs.append(dict(
                q=lambda hd, b, i=i: qB[0:96, 2 * i + hd, b * 128:(b + 1) * 128],
                k=lambda hd, lo, hi, i=i: kB[0:96, 2 * i + hd, lo * 128:hi * 128],
                kbs=FULL, ready=lambda hd, b, i=i: [bq[2 * i + hd], bk2[2 * i + hd]], mask=None, sink=None,
                v=lambda kb, hd, i=i: vB[:, kb, 64 * (2 * i + hd):64 * (2 * i + hd) + 64],
                v_ready=[bv[2 * i], bv[2 * i + 1]], out=out))
        attention(prs, PTB, PbB, float(np.float32(96.0) ** np.float32(-0.5)), before, before,
                  ([0, 1, 2], [3, 4], [5, 6]), None)

        def project(tiles, Hn, gname, prev, h_free):
            nn = Norm(Hn, gname, prev.acc_read)
            for i in range(8):
                bank, tok = gemm(stream2, [(nxt(), tiles)], G8)
                xt = V.do(lambda e: e.tensor_tensor(X[:, i, :], X[:, i, :], bank.ap[:, :], ALU.add), tok, (V.sem, V.n))
                bank.free = [xt]
                nn.tile(i, [xt], h_free, split=Hn is not None)
            nn.finish(banks[7], [(V.sem, V.n), prev.r])
            return nn

        U = at("U", [128, 2, 8, T], R, 144)
        fu = [at(f"fu{i}", [128, T], F, 176 + 2 * i) for i in range(4)]

        def ffn(nn, Hn, gname, h_free):
            before = [(V.sem, V.n), (S.sem, S.n), (G.sem, G.n), (P.sem, P.n)]
            ffree = [list(before), list(before)]
            down = list(before)
            out = Norm(Hn, gname, nn.acc_read)
            for q in range(4):
                u_tok = {}
                for i in range(8):
                    bank, tok = gemm(stream2, [(nxt(), nn.tiles())], G8)
                    a, b = fu[2 * (i % 2)], fu[2 * (i % 2) + 1]
                    t1 = V.do(lambda e: e.scalar_tensor_tensor(a[:, :], bank.ap[:, :], 0.0, rbc[:, :],
                                                               ALU.max, ALU.mult), tok, nn.r, ffree[i % 2])
                    bank.free = [t1]
                    t2 = S.do(lambda e: e.activation(b[:, :], a[:, :], ACT.Square), t1, ffree[i % 2])
                    t3 = S.do(lambda e: e.copy(U[:, 0, i, :], b[:, :]), t2, down)
                    t4 = V.do(lambda e: e.tensor_tensor(U[:, 1, i, :], b[:, :], U[:, 0, i, :].bitcast(F),
                                                        ALU.subtract), t3, down)
                    ffree[i % 2] = [t4]
                    u_tok[i] = [t3, t4]
                tiles = [(U[:, 0, k, :], U[:, 1, k, :], u_tok[k]) for k in range(8)]
                for i in range(8):
                    bank, tok = gemm(stream2, [(nxt(), tiles)], G8)
                    xt = V.do(lambda e: e.tensor_tensor(X[:, i, :], X[:, i, :], bank.ap[:, :], ALU.add), tok,
                              (V.sem, V.n))
                    bank.free = [xt]
                    if q == 3:
                        out.tile(i, [xt], h_free, split=Hn is not None)
                down = [tok]
            out.finish(banks[7], [(V.sem, V.n)])
            return out

        before = [(V.sem, V.n), (S.sem, S.n), (G.sem, G.n), (P.sem, P.n)]
        mixt = [(H[1][:, 0, k, :], H[1][:, 1, k, :], mix_tok[k]) for k in range(8)]
        n4 = project(mixt, H[0], "gf0", n3, before)
        n5 = ffn(n4, H[1], "gm1", [(P.sem, P.n)])

        before = [(V.sem, V.n), (S.sem, S.n), (G.sem, G.n), (P.sem, P.n)]
        qC = at("qC", [128, 8, T], F, 144)
        kC = at("kC", [128, 8, T], F, 160)
        vC = at("vC", [128, 4, D], F, 176)
        cz = [at(f"cz{i}", [128, T], F, 192 + 2 * i) for i in range(2)]

        def by_row(ap):
            return ap.rearrange("p (r b c) -> p r b c", b=4, c=16)

        def blocked(ap):
            return ap.rearrange("p (b r c) -> p r b c", b=4, c=16)

        rb8 = at("rb8", [128, T], F, 196)
        t_rb8 = V.do(lambda e: e.tensor_scalar(rb8[:, :], rbc[:, :], 0.125, None, ALU.mult), n5.r, before)
        qc, kc, vc = {}, {}, {}
        zf = [list(before), list(before)]
        for i in range(24):
            bank, tok = gemm(stream2, [(nxt(), n5.tiles())], G8)

            if i < 16:
                dst = (qC if i < 8 else kC)[:, i % 8, :]
                if i < 8:
                    t1 = V.do(lambda e: e.tensor_tensor(blocked(dst), by_row(bank.ap[:, :]), by_row(rb8[:, :]),
                                                        ALU.mult), tok, t_rb8, before)
                else:
                    t1 = V.do(lambda e: e.tensor_tensor(blocked(dst), by_row(bank.ap[:, :]), by_row(rbc[:, :]),
                                                        ALU.mult), tok, n5.r, before)
                bank.free = [t1]
                (qc if i < 8 else kc)[i % 8] = [t1]
            else:
                def w(i=i, bank=bank, tok=tok):
                    z = cz[i % 2]
                    t1 = V.do(lambda e: e.tensor_tensor(blocked(z[:, :]), by_row(bank.ap[:, :]), by_row(rbc[:, :]),
                                                        ALU.mult), tok, n5.r, zf[i % 2])
                    bank.free = [t1]
                    vc[i % 8], tf = v_natural(i, z, t1, vC[:, :, 128 * (i % 8):128 * (i % 8) + 128], 4 + i % 2)
                    zf[i % 2] = [tf]
                later(w)
        flush()
        before = [(V.sem, V.n), (S.sem, S.n), (G.sem, G.n), (P.sem, P.n)]
        bia = [at(f"bia{i}", [128, 896], F, 192 + 3.5 * i) for i in range(2)]
        PTC = [at(f"PTC{i}", [128, 4, T], F, 48 + 8 * i) for i in range(2)]
        PbC = [at(f"PbC{i}", [128, 384], F, 64 + 1.5 * i) for i in range(4)]
        c_b = [count("s_bia0"), count("s_bia1")]
        bia_at, bia_free = {}, [list(before), list(before)]
        bia_used = {}

        def load_bias(h):
            bia_at[h] = c_b[h % 2].load(Y, lambda e: e.dma_start(bia[h % 2][:, :], A["c_bias"][h]), bia_free[h % 2])

        load_bias(0)
        load_bias(1)
        BO = [(0, 256), (256, 640), (256, 640), (640, 896)]

        def used(pi, hd, b, t):
            if b == 3:
                h = 2 * pi + hd
                bia_free[h % 2] = [t]
                if h + 2 < 16:
                    load_bias(h + 2)

        odd_tok = {}
        prs = []

        for i in range(8):
            def out(bank, to, i=i):
                view = lambda ap: ap[:, :].rearrange("p (b r c) -> p r b c", b=4, c=16)
                odd_tok[i] = split_out(by_row(H[0][:, 0, i, :]), by_row(H[0][:, 1, i, :]), view)(bank, to)
                return odd_tok[i]

            prs.append(dict(
                q=lambda hd, b, i=i: qC[64 * hd:64 * hd + 64, i, b * 128:(b + 1) * 128],
                k=lambda hd, lo, hi, i=i: kC[64 * hd:64 * hd + 64, i, lo * 128:hi * 128],
                kbs=KBS, ready=lambda hd, b, i=i: [qc[i], kc[i]],
                mask=lambda hd, b: bia[hd][:, BO[b][0]:BO[b][1]],
                mask_ready=lambda hd, i=i: bia_at[2 * i + hd], mask_used=lambda hd, b, t, i=i: used(i, hd, b, t),
                sink=None,
                v=lambda kb, hd, i=i: vC[:, kb, 128 * i + 64 * hd:128 * i + 64 * hd + 64], v_ready=vc[i], out=out))
        attention(prs, PTC, PbC, 1.0, before, before, ([0, 1, 2], [3, 4], [5, 6]), None)

        before = [(V.sem, V.n), (S.sem, S.n), (G.sem, G.n), (P.sem, P.n)]
        oddt = [(H[0][:, 0, k, :], H[0][:, 1, k, :], odd_tok[k]) for k in range(8)]
        n6 = project(oddt, H[1], "gf1", n5, before)
        n7 = ffn(n6, None, None, [])

        c_out = count("s_out")
        for i in range(8):
            t1 = V.do(lambda e: e.scalar_tensor_tensor(X[:, i, :], X[:, i, :], col("gfin", i), rbc[:, :],
                                                       ALU.mult, ALU.mult), n7.r, (V.sem, V.n), (S.sem, S.n))
            t_out = c_out.load(Y, lambda e: e.dma_start(A["outT"][:, i * T:(i + 1) * T], X[:, i, :]), t1)
        Y.wait(t_out, y_tok, t_sc, zeroed)



VECS = [("eps", 1), ("g1", 8), ("g2", 8), ("gm0", 8), ("gf0", 8), ("gm1", 8), ("gf1", 8), ("gfin", 8),
        ("qg", 1), ("kg", 1), ("aqg", 1), ("akg", 1), ("sink", 8), ("cv0", 4), ("cv1", 4),
        ("cv2", 4), ("cvb", 4), ("bg", 5)]


def tables():
    f = np.float32
    c = {}
    eye = np.eye(128, dtype=f)
    c["c_ident"] = eye
    c["c_ones"] = np.ones((128, 128), f)
    b = np.zeros((128, 128), f)
    b[:64, :64] = 1
    b[64:, 64:] = 1
    c["c_bones"] = b
    c["c_triu"] = np.triu(np.ones((128, 128), f), 1)
    c["c_io32"] = np.broadcast_to(np.arange(32, dtype=f), (128, 32)).copy()

    def perm(pairs, size=128):
        m = np.zeros((128, 128), f)
        for a, b_ in pairs:
            m[b_, a] = -1
            m[a, b_] = 1
        return m

    t = np.arange(T, dtype=f)

    def table(size, parts):
        cs = np.zeros((size, 2, T), f)
        cs[:, 0] = 1
        for a, b_, ang in parts:
            for i in (a, b_):
                cs[i, 0], cs[i, 1] = np.cos(ang), np.sin(ang)
        return cs.reshape(size, 2 * T)

    inv = (f(500000.0) ** (-np.arange(0, 16, 2, dtype=f) / f(16))).astype(f)
    pf = [(64 * h + i, 64 * h + i + 8) for h in range(2) for i in range(8)]
    c["c_permF"] = perm(pf)
    c["c_ropeF"] = table(128, [(64 * h + i, 64 * h + i + 8, (t * inv[i]).astype(f)) for h in range(2) for i in range(8)])
    row, colm = (t // 64).astype(f), (t % 64).astype(f)

    def axial(base, d):
        inv = (f(10000.0) ** (-np.arange(0, d, 2, dtype=f) / f(d))).astype(f)
        out = []
        for part, pos in ((0, row), (1, colm)):
            for i in range(d // 2):
                a = base + part * d + i
                out.append((a, a + d // 2, (pos * inv[i]).astype(f)))
        return out

    pa = axial(0, 32) + axial(64, 32)
    c["c_permA"] = perm([x[:2] for x in pa])
    c["c_ropeA"] = table(128, pa)
    pb = axial(64, 16)
    c["c_permB"] = perm([x[:2] for x in pb])
    c["c_ropeB"] = table(96, pb)
    i, j = np.arange(128)[:, None], np.arange(384)[None, :] - 128
    c["c_maskF"] = np.where(np.abs(i - j) <= 128, 0, NEG).astype(f)
    return c


def layout(v):
    f = np.float32
    a = {}

    def arr(n):
        return np.asarray(v[n])

    def tiles(w, m=128):
        k, n = w.shape
        return np.ascontiguousarray(w.reshape(k // 128, 128, n // m, m).transpose(2, 1, 0, 3)).reshape(
            n // m, 128, (k // 128) * m)

    x = arr("x")[0]
    a["xT"] = np.ascontiguousarray(x.T.reshape(8, 128, T).transpose(1, 0, 2)).reshape(128, 8 * T)
    w = arr("w_in")[0]
    pair = np.concatenate([np.r_[64 * i:64 * i + 64, 64 * (i + 4):64 * (i + 4) + 64] for i in range(4)])
    a["w1_in"] = tiles(np.concatenate([w[:, 0:512][:, pair], w[:, 512:768]], 1))
    cb, cc, cx = w[:, 768:1280], w[:, 1280:1792], w[:, 1792:2304]
    a["w1_conv"] = tiles(np.concatenate([p[:, 128 * i:128 * i + 128] for i in range(4) for p in (cc, cx, cb)], 1))
    a["w1_ga"] = tiles(w[:, 2304:3328])
    a["w1_gc"] = tiles(w[:, 3328:4352])
    a["w1_ap"] = tiles(arr("w_attn_proj")[0][pair])
    a["w1_cp"] = tiles(arr("w_conv_proj")[0])
    a["w1_out"] = tiles(arr("w_out")[0])
    wr = np.concatenate([arr("w_router_group")[0], arr("w_router_expert")[0]], 1)
    a["w_router"] = np.ascontiguousarray(wr.reshape(8, 128, 36).transpose(1, 0, 2)).reshape(128, 288)
    br = np.concatenate([arr("b_router_group")[0], arr("b_router_expert")[0]])
    a["b_router"] = np.broadcast_to(br, (128, 36)).copy()
    gu = np.concatenate([arr("w_gate_e")[0], arr("w_up_e")[0]], 2)
    a["w_gu"] = np.ascontiguousarray(gu.reshape(NE, 8, 128, 512).transpose(0, 2, 1, 3)).reshape(NE, 128, 4096)
    a["w_dn"] = np.ascontiguousarray(arr("w_down_e")[0].reshape(NE, 2, 128, D).transpose(0, 2, 1, 3)).reshape(
        NE, 128, 2048)
    w = arr("ev_w_in_2")[0]
    a["w2_in"] = tiles(np.concatenate([w[:, 0:512][:, pair], w[:, 512:768]], 1))
    a["w2_c"] = tiles(w[:, 768:1408])
    a["w2_kr"] = tiles(np.concatenate([np.zeros((D, 64), f), w[:, 1408:1440]], 1), 96)
    a["w2_uq"] = tiles(arr("ev_b_w_uq_2")[0], 96)
    a["w2_ukv"] = tiles(arr("ev_b_w_ukv_2")[0])
    rows = np.concatenate([pair, np.arange(512, 1024)])
    a["w2_evo"] = tiles(arr("ev_w_out_2")[0][rows])
    for l in range(2):
        a[f"w_up{l}"] = tiles(arr("ffn_w_up_2")[l])
        d = arr("ffn_w_down_2")[l].reshape(4, 8, 128, 8, 128).transpose(0, 3, 2, 1, 4)
        a[f"w_down{l}"] = np.ascontiguousarray(d).reshape(32, 128, 1024)
    a["w2_qkv"] = tiles(arr("od_w_qkv_2")[0])
    a["w2_odo"] = tiles(arr("od_w_out_2")[0])

    rpb = arr("od_rpb_2")[0]
    q = np.arange(128)
    qr, qcl = q // 16, q % 16
    out = np.full((16, 128, 896), NEG, f)
    for base, nb, first, lo in ((0, 2, 0, 0), (256, 3, 1, 0), (640, 2, 3, 2)):
        k = np.arange(nb * 128)
        kr, kcl = (k % 128) // 16, (lo + k // 128) * 16 + k % 16
        c = first * 16 + qcl
        cs = np.clip(c - 8, 0, 48)
        valid = (kcl[None] >= cs[:, None]) & (kcl[None] < cs[:, None] + 16)
        qi, ki = np.nonzero(valid)
        out[:, qi, base + ki] = rpb[:, kr[ki] - qr[qi] + 7, kcl[ki] - c[qi] + 15]
    a["c_bias"] = out

    vec = np.zeros((128, 128), f)
    cols = {"eps": np.full((1, 128), EPS, f)}

    def feat(g):
        return np.asarray(g).reshape(-1, 128)

    cols["g1"], cols["g2"] = feat(arr("norm1_g")[0]), feat(arr("norm2_g")[0])
    for l in range(2):
        cols[f"gm{l}"], cols[f"gf{l}"] = feat(arr("norm_mix_2")[l]), feat(arr("norm_ffn_2")[l])
    cols["gfin"] = feat(arr("final_norm_2"))
    for n, s in (("qg", "q_norm_g"), ("kg", "k_norm_g"), ("aqg", "ev_a_q_norm_2"), ("akg", "ev_a_k_norm_2")):
        g = arr(s)[0]
        cols[n] = np.concatenate([g, g])[None]
    cols["sink"] = np.broadcast_to(arr("attn_sink")[0][:, None], (8, 128))
    for j in range(3):
        cols[f"cv{j}"] = feat(arr("conv_w")[0, j])
    cols["cvb"] = feat(arr("conv_b")[0])
    cols["bg"] = feat(np.concatenate([arr("ev_b_q_norm_2")[0], arr("ev_b_kv_norm_2")[0]]))
    c = 0
    for n, w_ in VECS:
        if n in cols:
            vec[:, c:c + w_] = cols[n].T
        c += w_
    a["vec"] = vec
    a.update(tables())
    return a


def kernel(**inputs):
    import concourse.bacc as bacc
    from concourse.bass_utils import run_bass_kernel_spmd as run

    nc = bacc.Bacc("TRN2", target_bir_lowering=False, num_devices=1)
    arrays = layout(inputs)
    A = {}
    for name, a in arrays.items():
        A[name] = nc.dram_tensor("in_" + name, a.shape, mybir.dt.from_np(a.dtype), kind="ExternalInput").ap()
    A["hbuf"] = nc.dram_tensor("hbuf", (SLOTS, D), F, kind="Internal").ap()
    A["ybuf"] = nc.dram_tensor("ybuf", (SLOTS, D), F, kind="Internal").ap()
    A["outT"] = nc.dram_tensor("outT", (128, 8 * T), F, kind="ExternalOutput").ap()
    program(nc, A)
    r = run(nc, [{"in_" + n: a for n, a in arrays.items()}], core_ids=[0])
    o = r.results[0]["outT"].reshape(128, 8, T).transpose(2, 1, 0).reshape(1, T, D)
    return np.ascontiguousarray(o)
```

```python
from contextlib import ExitStack

import numpy as np

import concourse.bass as bass
from concourse import mybir

F = mybir.dt.float32
R = mybir.dt.float32r
I32 = mybir.dt.int32
U32 = mybir.dt.uint32
ALU = mybir.AluOpType
ACT = mybir.ActivationFunctionType
AX = mybir.AxisListType.X

T = 512
D = 1024
KB = 1024
BASE = 16512
EPS = 1e-6
NEG = -1e30
CAP = 64
NE = 32
SLOTS = NE * CAP


class Queue:

    def __init__(self, eng, sem):
        self.eng, self.sem, self.n, self.seen = eng, sem, 0, {}

    def wait(self, *tokens):
        for t in tokens:
            if t is None:
                continue
            if isinstance(t, list):
                self.wait(*t)
                continue
            sem, value = t
            if self.seen.get(sem.name, 0) < value:
                self.seen[sem.name] = value
                self.eng.wait_ge(sem, value)

    def do(self, fn, *tokens):
        self.wait(*tokens)
        self.n += 1
        fn(self.eng).then_inc(self.sem, 1)
        return (self.sem, self.n)

    def plain(self, fn, *tokens):
        self.wait(*tokens)
        fn(self.eng)


class Count:

    def __init__(self, sem):
        self.sem, self.n = sem, 0

    def load(self, queue, fn, *tokens):
        queue.wait(*tokens)
        self.n += 16
        fn(queue.eng).then_inc(self.sem, 16)
        return (self.sem, self.n)


class Bank:
    def __init__(self, ap):
        self.ap, self.free = ap, []


def program(nc, A, dumps=None):
    ctx = ExitStack()
    with ctx:
        def sem(name):
            return ctx.enter_context(nc.semaphore(name))

        def at(name, shape, dt, kb):
            return nc.alloc_sbuf_tensor_at(name, shape, dt, offset=BASE + int(kb * KB))

        P, V, S, G, Y = (Queue(e, sem(f"q_{n}")) for n, e in (
            ("pe", nc.tensor), ("dve", nc.vector), ("act", nc.scalar), ("pool", nc.gpsimd), ("sp", nc.sync)))

        def count(name):
            return Count(sem(name))

        banks = [Bank(ctx.enter_context(nc.psum_tensor(f"bank{i}", [128, 512], F))) for i in range(8)]

        X = at("X", [128, 8, T], F, 0)
        H = [at(f"H{i}", [128, 2, 8, T], R, 16 + 32 * i) for i in range(2)]
        raw = [at(f"raw{i}", [128, 1024], F, 80 + 4 * i) for i in range(6)]
        whi = [at(f"whi{i}", [128, 1024], R, 104 + 4 * i) for i in range(3)]
        wlo = [at(f"wlo{i}", [128, 1024], R, 116 + 4 * i) for i in range(3)]
        ident = at("ident", [128, 128], F, 128)
        ones = at("ones", [128, 128], F, 128.5)
        bones = at("bones", [128, 128], F, 129)
        permF = at("permF", [128, 128], F, 129.5)
        permA = at("permA", [128, 128], F, 130)
        permB = at("permB", [128, 128], F, 130.5)
        triu = at("triu", [128, 128], F, 131)
        vec = at("vec", [128, 128], F, 131.5)
        st = [at(f"st{i}", [128, 8], F, 132 + i / 32) for i in range(4)]
        keep = at("keep", [128, 96], F, 132.25)
        keepi = at("keepi", [128, 16], U32, 132.75)
        io32 = at("io32", [128, 32], F, 133)
        bro = at("bro", [128, 36], F, 133.25)
        wr = at("wr", [128, 8, 36], F, 133.5)
        rbc = at("rbc", [128, T], F, 136)
        acc = at("acc", [128, T], F, 138)
        tm = [at(f"tm{i}", [128, T], F, 140 + 2 * i) for i in range(2)]

        c_const, c_vec = count("s_const"), count("s_vec")
        vec_ready = c_vec.load(Y, lambda e: e.dma_start(vec[:], A["vec"]))
        c_x = [count(f"s_x{i}") for i in range(8)]
        xT = A["xT"].rearrange("p (k t) -> p k t", t=T)
        x_load = []

        def load_x(i):
            x_load.append(c_x[i].load(Y, lambda e: e.dma_start(X[:, i, :], xT[:, i, :])))

        consts = ((ident, "c_ident"), (ones, "c_ones"), (bones, "c_bones"), (permF, "c_permF"),
                          (permA, "c_permA"), (permB, "c_permB"), (triu, "c_triu"),
                  (io32, "c_io32"), (bro, "b_router"), (wr, "w_router"))
        VEC = {}
        for n, (name, w) in enumerate(VECS):
            VEC[name] = sum(k for _, k in VECS[:n])

        nsink = at("nsink", [128, 8], F, 134.625)
        t_ns = V.do(lambda e: e.tensor_scalar(nsink[:, :], vec[:, VEC["sink"]:VEC["sink"] + 8], -1.0, None,
                                              ALU.mult), vec_ready)

        def col(name, i=0, p0=0, p1=128):
            c = VEC[name] + i
            return vec[p0:p1, c:c + 1]

        class Stream:
            def __init__(self, name, chunks, guard, split_guard, ahead=6):
                self.chunks, self.sems = chunks, [count(f"s_{name}{i}") for i in range(6)]
                self.raw_free = [list(guard) for _ in range(6)]
                self.split_free = [list(split_guard) for _ in range(3)]
                self.loaded, self.ready, self.done_load, self.done_split = {}, {}, 0, 0
                for _ in range(ahead):
                    self.load()

            def load(self):
                c = self.done_load
                if c >= len(self.chunks):
                    return
                ap, kt, m = self.chunks[c]
                self.loaded[c] = self.sems[c % 6].load(
                    Y, lambda e: e.dma_start(raw[c % 6][:, 0:kt * m], ap), self.raw_free[c % 6])
                self.done_load += 1

            def split_to(self, last):
                while self.done_split <= min(last, len(self.chunks) - 1):
                    c = self.done_split
                    _, kt, m = self.chunks[c]
                    r, h, lo = raw[c % 6][:, 0:kt * m], whi[c % 3][:, 0:kt * m], wlo[c % 3][:, 0:kt * m]
                    th = S.do(lambda e, r=r, h=h: e.copy(h, r), self.loaded[c], self.split_free[c % 3])
                    tl = V.do(lambda e, r=r, h=h, lo=lo: e.tensor_tensor(lo, r, h.bitcast(F), ALU.subtract),
                              th, self.loaded[c], self.split_free[c % 3])
                    self.ready[c] = [th, tl]
                    self.raw_free[c % 6] = [th, tl]
                    self.done_split += 1
                    self.load()

            def used(self, c, token):
                self.split_free[c % 3] = [token]

        def gemm_group(stream, chunks, tiles, pool, m=128):
            outs = [banks[b] for b in pool[:len(chunks)]]
            bank_turn[0] = len(chunks)
            toks = [None] * len(chunks)
            for k, (hi, lo, tok) in enumerate(tiles):
                P.wait(tok)
                for j, c in enumerate(chunks):
                    if k == 0:
                        P.wait(stream.ready[c], outs[j].free)
                    wh = whi[c % 3][:, k * m:(k + 1) * m]
                    wl = wlo[c % 3][:, k * m:(k + 1) * m]
                    for n, (w, x) in enumerate(((wh, hi), (wh, lo), (wl, hi))):
                        first, last = k == 0 and n == 0, k == len(tiles) - 1 and n == 2
                        fn = lambda e: e.matmul(outs[j].ap[0:m, :], w, x, start=first, stop=last)
                        if last:
                            toks[j] = P.do(fn)
                            stream.used(c, toks[j])
                            stream.split_to(c + 3)
                        else:
                            P.plain(fn)
            return list(zip(outs, toks))

        bank_turn = [0]
        pend = []

        def later(fn, n=1):
            pend.append([n, fn])

        def tick():
            due = []
            for p in pend:
                p[0] -= 1
                if p[0] <= 0:
                    due.append(p)
            for p in due:
                pend.remove(p)
                p[1]()

        def flush():
            while pend:
                tick()

        def gemm(stream, parts, pool, m=128):
            bank = banks[pool[bank_turn[0] % len(pool)]]
            bank_turn[0] += 1
            out = bank.ap[0:m, :]
            P.wait(bank.free)
            total = sum(len(tiles) for _, tiles in parts) * 3
            n = 0
            for c, tiles in parts:
                stream.split_to(c)
                P.wait(stream.ready[c])
                for k, (hi, lo, tok) in enumerate(tiles):
                    P.wait(tok)
                    wh = whi[c % 3][:, k * m:(k + 1) * m]
                    wl = wlo[c % 3][:, k * m:(k + 1) * m]
                    for w, x in ((wh, hi), (wh, lo), (wl, hi)):
                        fn = lambda e, w=w, x=x, n=n: e.matmul(out, w, x, start=(n == 0), stop=(n == total - 1))
                        n += 1
                        if k == len(tiles) - 1 and w is wl:
                            tok = P.do(fn)
                        else:
                            P.plain(fn)
                stream.used(c, tok)
                stream.split_to(c + 2)
            tick()
            return bank, tok

        sq_free = [[], []]

        class Norm:

            def __init__(self, Hn, gname, acc_free=()):
                self.H, self.g, self.tok = Hn, gname, {}
                self.acc_tok = list(acc_free)

            def tile(self, i, xtok, free, split=True, f32=None):
                if split:
                    hi, lo = self.H[:, 0, i, :], self.H[:, 1, i, :]
                    th = S.do(lambda e: e.activation(hi, X[:, i, :], ACT.Identity, bias=0.0, scale=col(self.g, i)),
                              xtok, free, vec_ready)
                    tl = V.do(lambda e: e.scalar_tensor_tensor(lo, X[:, i, :], col(self.g, i), hi.bitcast(F),
                                                               ALU.mult, ALU.subtract), th, xtok, free)
                    self.tok[i] = [th, tl]
                elif f32 is not None:
                    self.tok[i] = [S.do(lambda e: e.activation(f32[:, i, :], X[:, i, :], ACT.Identity, bias=0.0,
                                                               scale=col(self.g, i)), xtok, free)]
                if i == 0:
                    self.acc_tok = [S.do(lambda e: e.activation(acc[:, :], X[:, i, :], ACT.Square),
                                         xtok, self.acc_tok)]
                else:
                    q = tm[i % 2]
                    ts = S.do(lambda e: e.activation(q[:, :], X[:, i, :], ACT.Square), xtok, sq_free[i % 2])
                    self.acc_tok = [V.do(lambda e: e.tensor_tensor(acc[:, :], acc[:, :], q[:, :], ALU.add),
                                         ts, self.acc_tok)]
                    sq_free[i % 2] = list(self.acc_tok)

            def tiles(self):
                return [(self.H[:, 0, i, :], self.H[:, 1, i, :], self.tok[i]) for i in range(8)]

            def finish(self, bank, rfree):
                tp = P.do(lambda e: e.matmul(bank.ap[:, :], ones[:, :], acc[:, :], start=True, stop=True),
                          self.acc_tok, bank.free, c_ready)
                self.acc_read = [tp]
                t = S.do(lambda e: e.activation(rbc[:, :], bank.ap[:, :], ACT.Ln, bias=col("eps"), scale=1.0 / D),
                         tp, rfree)
                bank.free = [t]
                self.r = [S.do(lambda e: e.activation(rbc[:, :], rbc[:, :], ACT.Exp, scale=-0.5), t)]

        def table(name, *tokens):
            S.plain(lambda e: e.preload_act_table_set(name), *tokens)

        def transpose(out, in_, idn):
            return lambda e: e.transpose(out, in_, idn)

        def attention(pairs, PT, Pb, scale, pt_free, p_free, names):
            units = []
            for pi, pr in enumerate(pairs):
                for hd in range(2):
                    for b in range(4):
                        units.append((pi, hd, b))
            n = len(units)
            state = {}
            pt_ready = {}
            pfree = [list(p_free) for _ in Pb]
            ptfree = [list(pt_free), list(pt_free)]
            LAG = 3
            sfree = [[] for _ in st]
            SB, TB, OB = names

            def scores(u):
                pi, hd, b = units[u]
                pr = pairs[pi]
                lo, hi = pr["kbs"][b]
                nk = (hi - lo) * 128
                bank = banks[SB[u % len(SB)]]
                q, k = pr["q"](hd, b), pr["k"](hd, lo, hi)
                ts = P.do(lambda e: e.matmul(bank.ap[:, 0:nk], q, k, start=True, stop=True),
                          bank.free, pr["ready"](hd, b))
                pb, s = Pb[u % len(Pb)], st[u % 4]
                if pr["mask"]:
                    m = pr["mask"](hd, b)
                    tv = V.do(lambda e: e.tensor_tensor_reduce(out=pb[:, 0:nk], in0=bank.ap[:, 0:nk], in1=m,
                                                               scale=1.0, scalar=-3e38, op0=ALU.add, op1=ALU.max,
                                                               accum_out=s[:, 0:1]),
                              ts, pfree[u % len(Pb)], sfree[u % 4],
                              pr["mask_ready"](hd) if callable(pr["mask_ready"]) else pr["mask_ready"])
                    bank.free = [tv]
                    pr["mask_used"](hd, b, tv)
                    src = pb
                else:
                    tv = V.do(lambda e: e.tensor_reduce(s[:, 0:1], bank.ap[:, 0:nk], AX, ALU.max),
                              ts, sfree[u % 4])
                    src = bank.ap
                if pr["sink"] is not None:
                    ns, sk = pr["sink"](hd)
                    tn = V.do(lambda e: e.tensor_scalar(s[:, 1:2], s[:, 0:1], -scale, ns, ALU.mult, ALU.min), tv)
                else:
                    tn = V.do(lambda e: e.tensor_scalar(s[:, 1:2], s[:, 0:1], -scale, None, ALU.mult), tv)
                te = S.do(lambda e: e.activation(pb[:, 0:nk], src[:, 0:nk], ACT.Exp, bias=s[:, 1:2], scale=scale,
                                                 accum_out=s[:, 2:3]), tn, tv, ts, pfree[u % len(Pb)])
                if not pr["mask"]:
                    bank.free = [te]
                toks = [te]
                if pr["sink"] is not None:
                    toks.append(S.do(lambda e: e.activation(s[:, 3:4], s[:, 1:2], ACT.Exp, bias=sk, scale=1.0), tn))
                state[u] = toks

            def norm(u):
                pi, hd, b = units[u]
                lo, hi = pairs[pi]["kbs"][b]
                nk = (hi - lo) * 128
                pb, s = Pb[u % len(Pb)], st[u % 4]
                t = state[u]
                if pairs[pi]["sink"] is not None:
                    t = [V.do(lambda e: e.tensor_tensor(s[:, 2:3], s[:, 2:3], s[:, 3:4], ALU.add), t)]
                tr = V.do(lambda e: e.reciprocal(s[:, 4:5], s[:, 2:3]), t)
                tg = G.do(lambda e: e.tensor_scalar(pb[:, 0:nk], pb[:, 0:nk], s[:, 4:5], 1.0, ALU.mult, ALU.mult),
                          tr, state[u])
                sfree[u % 4] = [tg]
                state[u] = [tg]

            def turn(u):
                pi, hd, b = units[u]
                lo, hi = pairs[pi]["kbs"][b]
                pb = Pb[u % len(Pb)]
                bank = banks[TB[u % len(TB)]]
                P.wait(state[u], bank.free)
                for j in range(hi - lo):
                    fn = transpose(bank.ap[:, j * 128:(j + 1) * 128], pb[:, j * 128:(j + 1) * 128], ident[:, :])
                    if j == hi - lo - 1:
                        tt = P.do(fn)
                    else:
                        P.plain(fn)
                pfree[u % len(Pb)] = [tt]
                dst = PT[pi % 2][hd][:, lo:hi, b * 128:(b + 1) * 128]
                srcb = bank.ap[:, 0:(hi - lo) * 128].rearrange("p (k q) -> p k q", q=128)
                if u % 2:
                    tc = S.do(lambda e: e.copy(dst, srcb), tt, ptfree[pi % 2])
                else:
                    tc = V.do(lambda e: e.tensor_copy(dst, srcb), tt, ptfree[pi % 2])
                bank.free = [tc]
                pt_ready.setdefault(pi, []).append(tc)

            def values(pi):
                pr = pairs[pi]
                bank = banks[OB[pi % len(OB)]]
                P.wait(bank.free, pt_ready[pi], pr["v_ready"])
                full = all(k == (0, 4) for k in pr["kbs"])
                for kb in range(4):
                    qs = [b for b in range(4) if pr["kbs"][b][0] <= kb < pr["kbs"][b][1]]
                    q0, q1 = qs[0] * 128, (qs[-1] + 1) * 128
                    for hd in range(2):
                        fn = lambda e, kb=kb, hd=hd, q0=q0, q1=q1: e.matmul(
                            bank.ap[64 * hd:64 * hd + 64, q0:q1], pr["v"](kb, hd), PT[pi % 2][hd][:, kb, q0:q1],
                            start=(kb == 0), stop=(kb == 3), skip_group_check=not full)
                        if kb == 3 and hd == 1:
                            to = P.do(fn)
                        else:
                            P.plain(fn)
                ptfree[pi % 2] = [to]
                bank.free = pr["out"](bank, to)

            for t in range(n + LAG):
                if t < n:
                    scores(t)
                if 1 <= t <= n:
                    norm(t - 1)
                u = t - LAG
                if u >= 0:
                    turn(u)
                    if u % 8 == 1 and u > 1:
                        values(u // 8 - 1)
            values(len(pairs) - 1)
            return [P.n and (P.sem, P.n)]

        W1 = []
        for i in range(6):
            W1.append((A["w1_in"][i], 8, 128))
        for i in range(12):
            W1.append((A["w1_conv"][i], 8, 128))
        for i in range(8):
            W1 += [(A["w1_ga"][i], 8, 128), (A["w1_ap"][i], 4, 128), (A["w1_gc"][i], 8, 128), (A["w1_cp"][i], 4, 128)]
        for i in range(8):
            W1.append((A["w1_out"][i], 8, 128))

        load_x(0)
        stream = Stream("a", W1, [], [], 1)
        for i in range(1, 8):
            load_x(i)
            if i % 3 == 0:
                stream.load()
        for sb_, name in consts:
            src = A[name]
            if name == "w_router":
                src = src.rearrange("p (k n) -> p k n", n=36)
            c_ready = c_const.load(Y, lambda e, a=sb_, b=src: e.dma_start(a[:], b))
        for i in range(3):
            stream.load()
        cur = [0]

        def nxt():
            cur[0] += 1
            return cur[0] - 1

        c_t = count("s_tabs")
        ropeF = at("ropeF", [128, 2, T], F, 156)
        maskF = at("maskF", [128, 384], F, 160)
        zero = at("zero", [128, 1024], F, 200)
        t_tab = c_t.load(Y, lambda e: e.dma_start(ropeF[:, :, :], A["c_ropeF"].rearrange("p (a t) -> p a t", a=2)))
        t_tab = c_t.load(Y, lambda e: e.dma_start(maskF[:, :], A["c_maskF"]))

        c_zero = count("s_zero")
        t_z = G.do(lambda e: e.memset(zero[:, :], 0.0))

        def zero_rows(i):
            return c_zero.load(Y, lambda e: e.dma_start(A["hbuf"][i * 128:(i + 1) * 128, :], zero[:, :]), t_z)

        G8 = [0, 1, 2, 3]
        table("natural_log_exp_and_others")
        n1 = Norm(H[0], "g1")
        for i in range(8):
            n1.tile(i, x_load[i], [])
            if i in (0, 3, 6):
                stream.split_to(i // 3)
        first = gemm_group(stream, [nxt() for _ in range(3)], n1.tiles(), G8)
        n1.finish(banks[7], [])

        qF = at("qF", [128, 4, T], F, 144)
        kF = at("kF", [128, T], F, 152)
        vF = at("vF", [128, 4, 128], F, 154)
        qz = [at(f"qz{i}", [128, T], F, 188 + 2 * i) for i in range(2)]
        qs = [at(f"qs{i}", [128, T], F, 192 + 2 * i) for i in range(2)]
        qn = [at(f"qn{i}", [128, T], F, 196 + 2 * i) for i in range(2)]

        def head_norm_rope(i, bank, tok, r, g, perm, rope, dst, fr, extra, Z, done):
            z, s, m = Z[0][i % 2], Z[1][i % 2], Z[2][i % 2]
            f = fr.setdefault(i % 2, [])
            t1 = V.do(lambda e: e.tensor_tensor(z[:, :], bank.ap[:, :], r[:, :], ALU.mult), tok, extra, f)
            bank.free = [t1]
            t2 = S.do(lambda e: e.activation(s[:, :], z[:, :], ACT.Square), t1, f)

            def norm():
                b2 = banks[4 + i % 2]
                t3 = P.do(lambda e: e.matmul(b2.ap[:, :], bones[:, :], s[:, :], start=True, stop=True), t2, b2.free,
                          c_ready)
                t4 = S.do(lambda e: e.activation(s[:, :], b2.ap[:, :], ACT.Ln, bias=col("eps"), scale=1.0 / 64), t3)
                b2.free = [t4]
                t5 = S.do(lambda e: e.activation(s[:, :], s[:, :], ACT.Exp, scale=-0.5), t4)
                t6 = V.do(lambda e: e.scalar_tensor_tensor(m[:, :], z[:, :], g, s[:, :], ALU.mult, ALU.mult),
                          t5, t1, f)
                later(lambda: turned(t6))

            def turned(t6):
                done(rope_only(i, m, t6, perm, rope, dst, fr, extra, z, s))

            later(norm)

        def rope_only(i, m, t6, perm, rope, dst, fr, extra, z, s):
            b3 = banks[6 + i % 2]
            t7 = P.do(lambda e: e.matmul(b3.ap[:, :], perm[:, :], m[:, :], start=True, stop=True), t6, b3.free)
            t8 = G.do(lambda e: e.tensor_tensor(z[:, :], m[:, :], rope[:, 0, :], ALU.mult), t6, extra)
            t9 = V.do(lambda e: e.tensor_tensor(s[:, :], b3.ap[:, :], rope[:, 1, :], ALU.mult), t7, t6, extra)
            b3.free = [t9]
            t10 = V.do(lambda e: e.tensor_tensor(dst, z[:, :], s[:, :], ALU.add), t8, t9, extra)
            fr[i % 2] = [t10, t7]
            return [t10]

        fr = {}
        qk_ready = {}
        rX = [n1.r, t_tab]

        ZF = (qz, qs, qn)
        for i in range(6):
            bank, tok = first[i]
            if i < 5:
                dst, g = (qF[:, i, :], "qg") if i < 4 else (kF[:, :], "kg")
                head_norm_rope(i, bank, tok, rbc, col(g), permF, ropeF, dst, fr, rX, ZF,
                               lambda t, i=i: qk_ready.update({i if i < 4 else "k": t}))
            else:
                z = qz[i % 2]
                t1 = V.do(lambda e: e.tensor_tensor(z[:, :], bank.ap[:, :], rbc[:, :], ALU.mult), tok, rX,
                          fr.get(i % 2))
                bank.free = [t1]

                def w(i=i, z=z, t1=t1):
                    b2 = banks[4 + i % 2]
                    P.wait(t1, b2.free)
                    for b in range(4):
                        f = transpose(b2.ap[:, b * 128:(b + 1) * 128], z[:, b * 128:(b + 1) * 128], ident[:, :])
                        if b < 3:
                            P.plain(f)
                        else:
                            t2 = P.do(f)
                    t3 = V.do(lambda e: e.tensor_copy(vF[:, :, :], b2.ap[:, :].rearrange("p (a b) -> p a b", b=128)), t2)
                    b2.free = [t3]
                    qk_ready["v"] = [t3]
                later(w)
            if i < 5:
                first.append(gemm(stream, [(nxt(), n1.tiles())], G8))

        upad = [at(f"upad{i}", [128, T + 2], F, 183 + 2.25 * i) for i in range(2)]
        cf = [at(f"cf{i}", [128, T], F, 162 + 2 * i) for i in range(6)]
        t_pad = []
        for i in range(2):
            t_pad.append(V.do(lambda e, i=i: e.memset(upad[i][:, 0:1], 0.0)))
            t_pad.append(V.do(lambda e, i=i: e.memset(upad[i][:, T + 1:T + 2], 0.0)))
        H1 = H[1][:, :, :, :].rearrange("p a k t -> p (a k) t")
        attn_hi, attn_lo = (lambda i: H1[:, i, :]), (lambda i: H1[:, 4 + i, :])
        conv_hi, conv_lo = (lambda i: H1[:, 8 + i, :]), (lambda i: H1[:, 12 + i, :])
        conv_tok, cfree = {}, [[], []]
        for i in range(4):
            bc = first[6] if i == 0 else gemm(stream, [(nxt(), n1.tiles())], G8)
            for j in range(4):
                zeroed = zero_rows(4 * i + j)
            bx = first[7] if i == 0 else gemm(stream, [(nxt(), n1.tiles())], G8)
            bb = gemm(stream, [(nxt(), n1.tiles())], G8)
            u, (ta, tb, tc) = upad[i % 2], cf[3 * (i % 2):3 * (i % 2) + 3]
            f = cfree[i % 2]
            a1 = V.do(lambda e: e.tensor_tensor(ta[:, :], bc[0].ap[:, :], rbc[:, :], ALU.mult), bc[1], n1.r, f)
            bc[0].free = [a1]
            a2 = V.do(lambda e: e.tensor_tensor(tb[:, :], bx[0].ap[:, :], rbc[:, :], ALU.mult), bx[1], f)
            bx[0].free = [a2]
            a3 = V.do(lambda e: e.tensor_tensor(u[:, 1:T + 1], ta[:, :], tb[:, :], ALU.mult), a1, a2, t_pad, f)
            a4 = S.do(lambda e: e.activation(tc[:, :], u[:, 1:T + 1], ACT.Identity, bias=col("cvb", i),
                                             scale=col("cv1", i)), a3, f)
            a5 = V.do(lambda e: e.scalar_tensor_tensor(ta[:, :], u[:, 0:T], col("cv0", i), tc[:, :],
                                                       ALU.mult, ALU.add), a4, a3)
            a6 = V.do(lambda e: e.scalar_tensor_tensor(tb[:, :], u[:, 2:T + 2], col("cv2", i), ta[:, :],
                                                       ALU.mult, ALU.add), a5)
            a7 = V.do(lambda e: e.tensor_tensor(tc[:, :], bb[0].ap[:, :], rbc[:, :], ALU.mult), bb[1], a5)
            bb[0].free = [a7]
            a8 = V.do(lambda e: e.tensor_tensor(ta[:, :], tc[:, :], tb[:, :], ALU.mult), a6, a7)
            a9 = S.do(lambda e: e.copy(conv_hi(i), ta[:, :]), a8)
            a10 = V.do(lambda e: e.tensor_tensor(conv_lo(i), ta[:, :], conv_hi(i).bitcast(F), ALU.subtract), a9)
            cfree[i % 2] = [a10]
            conv_tok[i] = [a9, a10]

        PTF = [[at("PTF0", [128, 4, T], F, 162), at("PTF1", [128, 4, T], F, 170)],
               [at("PTF2", [128, 4, T], F, 178), at("PTF3", [128, 4, T], F, 194)]]
        PbF = [at(f"PbF{i}", [128, 384], F, 188 + 1.5 * i) for i in range(4)]
        flush()
        before = [(V.sem, V.n), (S.sem, S.n), (G.sem, G.n), (P.sem, P.n), zeroed]
        attn_tok = {}

        def split_out(hi, lo, view=None):
            def out(bank, to):
                src = view(bank.ap) if view else bank.ap[:, :]
                a = S.do(lambda e: e.copy(hi, src), to)
                b = V.do(lambda e: e.tensor_tensor(lo, src, hi.bitcast(F), ALU.subtract), a, to)
                return [a, b]
            return out

        KBS = [(0, 2), (0, 3), (1, 4), (2, 4)]
        prs = []
        for i in range(4):
            def out(bank, to, i=i):
                attn_tok[i] = split_out(attn_hi(i), attn_lo(i))(bank, to)
                return attn_tok[i]

            prs.append(dict(
                q=lambda hd, b, i=i: qF[64 * hd:64 * hd + 64, i, b * 128:(b + 1) * 128],
                k=lambda hd, lo, hi: kF[64 * hd:64 * hd + 64, lo * 128:hi * 128],
                kbs=KBS, ready=lambda hd, b, i=i: [qk_ready[i], qk_ready["k"]],
                mask=lambda hd, b: maskF[:, 128 if b == 0 else 0:256 if b == 3 else 384],
                mask_ready=[t_tab, t_ns], mask_used=lambda *a: None,
                sink=lambda hd, i=i: (nsink[:, i + 4 * hd:i + 4 * hd + 1], col("sink", i + 4 * hd)),
                v=lambda kb, hd: vF[:, kb, 64 * hd:64 * hd + 64], v_ready=qk_ready["v"], out=out))
        attention(prs, PTF, PbF, 0.125, before, before, ([0, 1, 2, 7], [3, 4], [5, 6]))

        table("sigmoid_and_others")
        M1 = at("M1", [128, 2, 8, T], R, 144)
        gm = [at(f"gm{i}", [128, T], F, 176 + 2 * i) for i in range(8)]
        before = [(V.sem, V.n), (S.sem, S.n), (G.sem, G.n), (P.sem, P.n)]
        gfree = [list(before), list(before)]
        merged = {}
        at_tiles = [(attn_hi(k), attn_lo(k), attn_tok[k]) for k in range(4)]
        cv_tiles = [(conv_hi(k), conv_lo(k), conv_tok[k]) for k in range(4)]
        AB = [0, 1, 2, 3, 4, 5, 6, 7]
        for i in range(8):
            ga = gemm(stream, [(nxt(), n1.tiles())], AB)
            ap = gemm(stream, [(nxt(), at_tiles)], AB)
            gc = gemm(stream, [(nxt(), n1.tiles())], AB)
            cp = gemm(stream, [(nxt(), cv_tiles)], AB)
            a, b, c, d = gm[4 * (i % 2):4 * (i % 2) + 4]
            f = gfree[i % 2]
            t1 = V.do(lambda e: e.tensor_tensor(a[:, :], ga[0].ap[:, :], rbc[:, :], ALU.mult), ga[1], f)
            ga[0].free = [t1]
            t2 = S.do(lambda e: e.activation(a[:, :], a[:, :], ACT.Sigmoid), t1)
            t3 = V.do(lambda e: e.tensor_tensor(b[:, :], a[:, :], ap[0].ap[:, :], ALU.mult), t2, ap[1], f)
            ap[0].free = [t3]
            t4 = V.do(lambda e: e.tensor_tensor(c[:, :], gc[0].ap[:, :], rbc[:, :], ALU.mult), gc[1], f)
            gc[0].free = [t4]
            t5 = S.do(lambda e: e.activation(c[:, :], c[:, :], ACT.Sigmoid), t4)
            t6 = V.do(lambda e: e.tensor_tensor(d[:, :], c[:, :], cp[0].ap[:, :], ALU.mult), t5, cp[1], f)
            cp[0].free = [t6]
            t7 = V.do(lambda e: e.tensor_tensor(b[:, :], b[:, :], d[:, :], ALU.add), t3, t6)
            t8 = S.do(lambda e: e.copy(M1[:, 0, i, :], b[:, :]), t7, before)
            t9 = V.do(lambda e: e.tensor_tensor(M1[:, 1, i, :], b[:, :], M1[:, 0, i, :].bitcast(F), ALU.subtract),
                      t8, before)
            gfree[i % 2] = [t9]
            merged[i] = [t8, t9]
        table("natural_log_exp_and_others")
        r_read = [(V.sem, V.n)]

        XG = at("XG", [128, 8, T], F, 176)
        m_tiles = [(M1[:, 0, k, :], M1[:, 1, k, :], merged[k]) for k in range(8)]
        n2 = Norm(None, "g2", n1.acc_read)
        lg = banks[7]
        h_dead = [(P.sem, P.n)]
        gates_done = [(V.sem, V.n), (S.sem, S.n)]

        GU = [[at("GU00", [128, 8, 512], F, 16), at("GU01", [128, 8, 512], F, 32)],
              [at("GU10", [128, 8, 512], F, 64), at("GU11", [128, 8, 512], F, 80)],
              [at("GU20", [128, 8, 512], F, 112), at("GU21", [128, 8, 512], F, 144)]]
        DN = [[at("DN00", [128, 2, 1024], F, 48), at("DN01", [128, 2, 1024], F, 56)],
              [at("DN10", [128, 2, 1024], F, 96), at("DN11", [128, 2, 1024], F, 104)],
              [at("DN20", [128, 2, 1024], F, 160), at("DN21", [128, 2, 1024], F, 168)]]
        c_gu = [count(f"s_gu{i}") for i in range(3)]
        c_dn = [count(f"s_dn{i}") for i in range(3)]
        gu_at, dn_at = {}, {}

        def load_gu(p, j, *tokens):
            s = p % 3
            gu_at[p] = c_gu[s].load(Y, lambda e: e.dma_start(
                GU[s][j][:, :, :], A["w_gu"][2 * p + j].rearrange("p (k n) -> p k n", n=512)), *tokens)

        def load_dn(p, j, *tokens):
            s = p % 3
            dn_at[p] = c_dn[s].load(Y, lambda e: e.dma_start(
                DN[s][j][:, :, :], A["w_dn"][2 * p + j].rearrange("p (k n) -> p k n", n=1024)), *tokens)

        def load_pair(p, *tokens):
            for load in (load_gu, load_dn):
                for j in range(2):
                    load(p, j, *tokens)

        def logits(k):
            P.wait(lg.free, n2.tok[k], c_ready)
            fn = lambda e: e.matmul(lg.ap[0:36, :], wr[:, k, :], XG[:, k, :], start=(k == 0), stop=(k == 7))
            if k == 7:
                return P.do(fn)
            P.plain(fn)

        for i in range(8):
            bank, tok = gemm(stream, [(nxt(), m_tiles)], [0, 1, 2, 3])
            if i == 0:
                load_pair(0, h_dead)
                load_gu(1, 0, h_dead)
            if i >= 1:
                logits(i - 1)
            xt = V.do(lambda e: e.tensor_tensor(X[:, i, :], X[:, i, :], bank.ap[:, :], ALU.add), tok, x_load)
            bank.free = [xt]
            n2.tile(i, [xt], gates_done, split=False, f32=XG)
        t_lg = logits(7)
        w_done = [(P.sem, P.n)]
        ring_done = [w_done, (V.sem, V.n), (S.sem, S.n)]
        load_gu(1, 1, ring_done)
        for j in range(2):
            load_dn(1, j, ring_done)
        for j in range(2):
            load_gu(2, j, ring_done)
        rc = keep[:, 0:4]
        sc = banks[4]
        P.wait(sc.free, n2.acc_tok)
        for b in range(4):
            fn = lambda e, b=b: e.matmul(sc.ap[:, b:b + 1], acc[:, b * 128:(b + 1) * 128], ones[:, 0:1],
                                         start=True, stop=True)
            if b < 3:
                P.plain(fn)
            else:
                ts = P.do(fn)
        t1 = S.do(lambda e: e.activation(rc, sc.ap[:, 0:4], ACT.Ln, bias=col("eps"), scale=1.0 / D), ts)
        sc.free = [t1]
        t_rc = S.do(lambda e: e.activation(rc, rc, ACT.Exp, scale=-0.5), t1)
        n2.finish(banks[5], r_read)
        n2r = n2.r

        lgs = at("lgs", [36, T], F, 192)
        t1 = V.do(lambda e: e.tensor_copy(lgs[:, :], lg.ap[0:36, :]), t_lg, gates_done)
        lg.free = [t1]
        lb = banks[6]
        P.wait(t1, lb.free)
        for b in range(4):
            fn = transpose(lb.ap[:, b * 36:(b + 1) * 36], lgs[:, b * 128:(b + 1) * 128], ident[0:36, 0:36])
            if b < 3:
                P.plain(fn)
            else:
                t_lt = P.do(fn)

        rows = [at(f"rows{b}", [128, D], F, 160 + 4 * b) for b in range(4)]
        row_tok = {b: [] for b in range(4)}
        n = 0
        for b in range(4):
            for hf in range(2):
                bank = banks[n % 4]
                P.wait(bank.free, n2.tok[7])
                for k in range(4):
                    fn = transpose(bank.ap[:, k * 128:(k + 1) * 128], XG[:, 4 * hf + k, b * 128:(b + 1) * 128],
                                   ident[:, :])
                    if k < 3:
                        P.plain(fn)
                    else:
                        t1 = P.do(fn)
                dst = rows[b][:, hf * 512:(hf + 1) * 512]
                t2 = S.do(lambda e: e.activation(dst, bank.ap[:, :], ACT.Copy, bias=0.0, scale=rc[:, b:b + 1]),
                          t1, t_rc, w_done)
                bank.free = [t2]
                row_tok[b].append(t2)
                n += 1

        off = [194.0]

        def small(name, *shape):
            n = int(np.prod(shape))
            t = at(name, [128] + list(shape), F, off[0])
            off[0] += max(n * 4, 32) / 1024
            return t

        L = small("L", 4, 36)
        last = None
        for b in range(4):
            last = V.do(lambda e: e.scalar_tensor_tensor(L[:, b, :], lb.ap[:, b * 36:(b + 1) * 36], rc[:, b:b + 1],
                                                         bro[:, :], ALU.mult, ALU.add), t_lt, t_rc, c_ready)
        lb.free = [last]
        GL = L[:, :, 0:4]
        EL = L[:, :, 4:36].rearrange("p t (g e) -> p t g e", e=8)

        def v(fn, *tokens):
            return V.do(fn, (V.sem, V.n), *tokens)

        def first_max(vals, n, name):
            mx, df, ix, mi, oh = (small(name + c, 4, 1 if c in "mi" else n) for c in ("m", "d", "x", "i", "o"))
            v(lambda e: e.tensor_reduce(mx[:, :, :], vals, AX, ALU.max))
            v(lambda e: e.tensor_tensor(df[:, :, :], vals, mx[:, :, :].to_broadcast([128, 4, n]), ALU.is_ge))
            v(lambda e: e.tensor_scalar(ix[:, :, :], df[:, :, :], -100.0, 100.0, ALU.mult, ALU.add))
            v(lambda e: e.tensor_tensor(ix[:, :, :], ix[:, :, :],
                                        io32[:, 0:n].unsqueeze(1).to_broadcast([128, 4, n]), ALU.add))
            v(lambda e: e.tensor_reduce(mi[:, :, :], ix[:, :, :], AX, ALU.min))
            v(lambda e: e.tensor_tensor(oh[:, :, :], ix[:, :, :], mi[:, :, :].to_broadcast([128, 4, n]),
                                        ALU.is_equal))
            return mx, oh

        gmx, goh = first_max(GL, 4, "g")
        gd, gs, pg = small("gd", 4, 4), small("gs", 4, 1), small("pg", 4, 1)
        t1 = v(lambda e: e.tensor_tensor(gd[:, :, :], GL, gmx[:, :, :].to_broadcast([128, 4, 4]), ALU.subtract))
        t2 = S.do(lambda e: e.activation(gd[:, :, :], gd[:, :, :], ACT.Exp), t1)
        ei4, ein = small("ei4", 4, 4, 8), small("ein", 4, 8)
        v(lambda e: e.tensor_tensor(ei4[:, :, :, :], EL, goh[:, :, :].unsqueeze(3).to_broadcast([128, 4, 4, 8]),
                                    ALU.mult))
        v(lambda e: e.tensor_reduce(ein[:, :, :], ei4[:, :, :, :].rearrange("p t g e -> p t e g"), AX, ALU.add))
        v(lambda e: e.tensor_reduce(gs[:, :, :], gd[:, :, :], AX, ALU.add), t2)
        v(lambda e: e.reciprocal(pg[:, :, :], gs[:, :, :]))
        m1, o1 = first_max(ein[:, :, :], 8, "u")
        e2 = small("e2", 4, 8)
        v(lambda e: e.scalar_tensor_tensor(e2[:, :, :], o1[:, :, :], NEG, ein[:, :, :], ALU.mult, ALU.add))
        m2, o2 = first_max(e2[:, :, :], 8, "v")
        dd, ex = small("dd", 4, 1), small("ex", 4, 1)
        t1 = v(lambda e: e.tensor_tensor(dd[:, :, :], m2[:, :, :], m1[:, :, :], ALU.subtract))
        t2 = S.do(lambda e: e.activation(ex[:, :, :], dd[:, :, :], ACT.Exp), t1)
        AS = [small(f"AS{k}", 4, 32) for k in range(3)]
        for k, o in ((0, o1), (1, o2)):
            v(lambda e: e.tensor_tensor(AS[k][:, :, :].rearrange("p t (g e) -> p t g e", e=8),
                                        goh[:, :, :].unsqueeze(3).to_broadcast([128, 4, 4, 8]),
                                        o[:, :, :].unsqueeze(2).to_broadcast([128, 4, 4, 8]), ALU.mult))
        t_as = v(lambda e: e.tensor_tensor(AS[2][:, :, :], AS[0][:, :, :], AS[1][:, :, :], ALU.add))
        dn, gt = small("dn", 4, 1), [small("gt0", 4, 1), small("gt1", 4, 1)]
        v(lambda e: e.tensor_scalar(dn[:, :, :], ex[:, :, :], 1.0, None, ALU.add), t2)
        v(lambda e: e.reciprocal(dn[:, :, :], dn[:, :, :]))
        v(lambda e: e.tensor_tensor(gt[0][:, :, :], dn[:, :, :], pg[:, :, :], ALU.mult))
        v(lambda e: e.tensor_tensor(gt[1][:, :, :], gt[0][:, :, :], ex[:, :, :], ALU.mult))
        rk = banks[6]
        P.wait(t_as, rk.free)
        for b in range(4):
            for b2 in range(b + 1):
                w = triu if b2 == b else ones
                fn = lambda e, b=b, b2=b2, w=w: e.matmul(rk.ap[:, 32 * b:32 * b + 32], w[:, :], AS[2][:, b2, :],
                                                         start=(b2 == 0), stop=(b2 == b))
                if b == 3 and b2 == 3:
                    t_rk = P.do(fn)
                else:
                    P.plain(fn)
        RK = small("RK", 4, 32)
        t1 = v(lambda e: e.tensor_copy(RK[:, :, :], rk.ap[:, 0:128].rearrange("p (t n) -> p t n", n=32)), t_rk)
        rk.free = [t1]
        tmp, rr, es, ok = small("tmp", 4, 32), small("rr", 4), small("es", 4), small("ok", 4)
        gov = small("gov", 2, 4)
        flag = small("flag", 8)
        for k in range(2):
            v(lambda e: e.tensor_tensor(tmp[:, :, :], AS[k][:, :, :], RK[:, :, :], ALU.mult))
            v(lambda e: e.tensor_reduce(rr[:, :], tmp[:, :, :], AX, ALU.add))
            v(lambda e: e.tensor_tensor(tmp[:, :, :], AS[k][:, :, :],
                                        io32[:, :].unsqueeze(1).to_broadcast([128, 4, 32]), ALU.mult))
            v(lambda e: e.tensor_reduce(es[:, :], tmp[:, :, :], AX, ALU.add))
            v(lambda e: e.tensor_scalar(ok[:, :], rr[:, :], float(CAP), None, ALU.is_lt))
            v(lambda e: e.scalar_tensor_tensor(es[:, :], es[:, :], float(CAP), rr[:, :], ALU.mult, ALU.add))
            v(lambda e: e.tensor_tensor(rr[:, :], es[:, :], ok[:, :], ALU.mult))
            v(lambda e: e.tensor_copy(keepi[:, 8 + 4 * k:12 + 4 * k], rr[:, :]))
            v(lambda e: e.tensor_scalar(es[:, :], es[:, :], -4096.0, None, ALU.add))
            v(lambda e: e.tensor_tensor(es[:, :], es[:, :], ok[:, :], ALU.mult))
            v(lambda e: e.tensor_scalar(es[:, :], es[:, :], 4096.0, None, ALU.add))
            t_idx = v(lambda e: e.tensor_copy(keepi[:, 4 * k:4 * k + 4], es[:, :]))
            g = keep[:, 4 + 4 * k:8 + 4 * k]
            v(lambda e: e.tensor_tensor(g, gt[k][:, :, 0], ok[:, :], ALU.mult))
            v(lambda e: e.tensor_tensor(gov[:, k, :], gt[k][:, :, 0], g, ALU.subtract))
            v(lambda e: e.tensor_scalar(flag[:, 4 * k:4 * k + 4], ok[:, :], -1.0, 1.0, ALU.mult, ALU.add))
        GO = at("GO", [128, 4, 32], F, 134.75)
        fl = at("fl", [128, 1], F, 135.25)
        fli = at("fli", [1, 1], I32, 135.375)
        v(lambda e: e.tensor_tensor(GO[:, :, :], AS[0][:, :, :],
                                    gov[:, 0, :].unsqueeze(2).to_broadcast([128, 4, 32]), ALU.mult))
        v(lambda e: e.tensor_tensor(tmp[:, :, :], AS[1][:, :, :],
                                    gov[:, 1, :].unsqueeze(2).to_broadcast([128, 4, 32]), ALU.mult))
        v(lambda e: e.tensor_tensor(GO[:, :, :], GO[:, :, :], tmp[:, :, :], ALU.add))
        t1 = v(lambda e: e.tensor_reduce(fl[:, :], flag[:, :], AX, ALU.add))
        t2 = P.do(lambda e: e.matmul(rk.ap[0:1, 0:1], fl[:, 0:1], ones[:, 0:1], start=True, stop=True), t1, rk.free)
        t_flag = v(lambda e: e.tensor_copy(fli[:, :], rk.ap[0:1, 0:1]), t2)
        rk.free = [t_flag]
        route_done = [(V.sem, V.n), (S.sem, S.n), (P.sem, P.n)]

        c_sc = count("s_scatter")
        for k in range(2):
            for b in range(4):
                t_sc = c_sc.load(G, lambda e, k=k, b=b: e.indirect_dma_start(
                    out=A["hbuf"], out_offset=bass.IndirectOffsetOnAxis(ap=keepi[:, 4 * k + b:4 * k + b + 1], axis=0),
                    in_=rows[b][:, :], in_offset=None, bounds_check=SLOTS - 1, oob_is_err=False),
                    t_idx, row_tok[b], zeroed)
        for q in (P, V, S, G, Y):
            q.wait(t_flag)
        left_over = nc.values_load(fli[0:1, 0:1], min_val=0, max_val=1024)

        hb = [at(f"hb{i}", [128, D], F, 196 + 4 * i) for i in range(2)]
        hT = at("hT", [128, 8, 128], F, 192)
        yb = at("yb", [128, D], F, 140)
        hid = at("hid", [128, 256], F, 204)
        hidT = at("hidT", [128, 2, 128], F, 205)
        c_hb, c_y = [count("s_hb0"), count("s_hb1")], count("s_y")
        table("silu_and_others")
        NP = NE // 2
        hb_free, hT_free, hT_tok, hb_at = [list(route_done), list(route_done)], list(route_done), {}, {}
        hid_free, hidT_free, yb_free = [list(route_done)], [list(route_done)], [list(route_done)]
        y_tok = None

        def load_rows(p):
            hb_at[p] = c_hb[p % 2].load(Y, lambda e: e.dma_start(
                hb[p % 2][:, :], A["hbuf"][p * 128:(p + 1) * 128, :]), t_sc, hb_free[p % 2])

        def turn_rows(p):
            t = hb_at[p]
            toks = []
            for hf in range(2):
                bank = banks[hf]
                P.wait(bank.free, t)
                for k in range(4):
                    fn = transpose(bank.ap[:, k * 128:(k + 1) * 128],
                                   hb[p % 2][:, (4 * hf + k) * 128:(4 * hf + k + 1) * 128], ident[:, :])
                    if k < 3:
                        P.plain(fn)
                    else:
                        t1 = P.do(fn)
                dst = hT[:, 4 * hf:4 * hf + 4, :]
                src = bank.ap[:, :].rearrange("p (k q) -> p k q", q=128)
                if hf:
                    t2 = V.do(lambda e: e.tensor_copy(dst, src), t1, hT_free)
                else:
                    t2 = S.do(lambda e: e.copy(dst, src), t1, hT_free)
                bank.free = [t2]
                toks.append(t2)
            hb_free[p % 2] = [t1]
            hT_tok[p] = toks

        load_rows(0)
        load_rows(1)
        for j in range(2):
            load_dn(2, j, t_sc)
        W2 = []
        for i in range(6):
            W2.append((A["w2_in"][i], 8, 128))
        for i in range(5):
            W2.append((A["w2_c"][i], 8, 128))
        W2.append((A["w2_kr"][0], 8, 128))
        for i in range(8):
            W2.append((A["w2_uq"][i], 3, 128))
        for i in range(4):
            W2.append((A["w2_uk"][i], 2, 128))
        W2.append((A["w2_uv"], 2, 512))
        for i in range(8):
            W2.append((A["w2_evo"][i], 8, 128))

        def ffn_chunks(l):
            for q in range(4):
                for i in range(8):
                    W2.append((A[f"w_up{l}"][8 * q + i], 8, 128))
                for i in range(8):
                    W2.append((A[f"w_down{l}"][8 * q + i], 8, 128))

        ffn_chunks(0)
        for i in range(24):
            W2.append((A["w2_qkv"][i], 8, 128))
        for i in range(8):
            W2.append((A["w2_odo"][i], 8, 128))
        ffn_chunks(1)

        turn_rows(0)
        for p in range(NP):
            s = p % 3
            bank = banks[2 + p % 2]
            P.wait(bank.free, hT_tok[p], gu_at[p])
            for k in range(8):
                for j in range(2):
                    fn = lambda e, k=k, j=j: e.matmul(bank.ap[64 * j:64 * j + 64, :],
                                                      hT[:, k, 64 * j:64 * j + 64], GU[s][j][:, k, :],
                                                      start=(k == 0), stop=(k == 7))
                    if k == 7 and j == 1:
                        t1 = P.do(fn)
                    else:
                        P.plain(fn)
            hT_free = [t1]
            t2 = S.do(lambda e: e.activation(hid[:, :], bank.ap[:, 0:256], ACT.Silu), t1, hid_free[0])
            t3 = V.do(lambda e: e.tensor_tensor(hid[:, :], hid[:, :], bank.ap[:, 256:512], ALU.mult), t2, t1)
            bank.free = [t3]
            if p + 1 < NP:
                turn_rows(p + 1)
            if p + 2 < NP:
                load_rows(p + 2)
            tb = banks[4]
            P.wait(t3, tb.free)
            P.plain(transpose(tb.ap[:, 0:128], hid[:, 0:128], ident[:, :]))
            t4 = P.do(transpose(tb.ap[:, 128:256], hid[:, 128:256], ident[:, :]))
            hid_free[0] = [t4]
            t5 = V.do(lambda e: e.tensor_copy(hidT[:, :, :], tb.ap[:, 0:256].rearrange("p (k q) -> p k q", q=128)),
                      t4, hidT_free[0])
            tb.free = [t5]
            toks = []
            for h2 in range(2):
                ob = banks[5 + h2]
                P.wait(t5, dn_at[p], ob.free)
                for k in range(2):
                    for j in range(2):
                        fn = lambda e, k=k, j=j, h2=h2, ob=ob: e.matmul(
                            ob.ap[64 * j:64 * j + 64, :], hidT[:, k, 64 * j:64 * j + 64],
                            DN[s][j][:, k, h2 * 512:(h2 + 1) * 512], start=(k == 0), stop=(k == 1))
                        if k == 1 and j == 1:
                            t6 = P.do(fn)
                        else:
                            P.plain(fn)
                dst = yb[:, h2 * 512:(h2 + 1) * 512]
                if h2:
                    t7 = V.do(lambda e: e.tensor_copy(dst, ob.ap[:, :]), t6, yb_free[0])
                else:
                    t7 = S.do(lambda e: e.copy(dst, ob.ap[:, :]), t6, yb_free[0])
                ob.free = [t7]
                toks.append(t7)
            hidT_free[0] = [t6]
            y_tok = c_y.load(Y, lambda e, p=p: e.dma_start(A["ybuf"][p * 128:(p + 1) * 128, :], yb[:, :]), toks)
            yb_free[0] = [y_tok]
            if p + 3 < NP:
                load_pair(p + 3, t6)
            if p == NP - 3:
                p13 = [t6]
                stream2 = Stream("b", W2, p13, [])
            if p == NP - 2:
                p14 = [t6]
                stream2.split_free = [list(p14) for _ in range(3)]
        moe_done = [t6]

        YG = [[at(f"YG{k}{b}", [128, D], F, 144 + 16 * k + 4 * b) for b in range(4)] for k in range(2)]
        c_yg = [count(f"s_yg{b}") for b in range(4)]
        cur[0] = 0
        c_t2 = count("s_tabs2")

        yg_tok = {}
        for b in range(4):
            for k in range(2):
                yg_tok[b] = c_yg[b].load(G, lambda e, k=k, b=b: e.indirect_dma_start(
                    out=YG[k][b][:, :], out_offset=None, in_=A["ybuf"],
                    in_offset=bass.IndirectOffsetOnAxis(ap=keepi[:, 8 + 4 * k + b:9 + 4 * k + b], axis=0),
                    bounds_check=SLOTS - 1, oob_is_err=False), y_tok, p14)
        xmoe = {}
        n3 = Norm(H[0], "gm0", n2.acc_read)
        bn = 0
        v_before = (V.sem, V.n)

        def weigh(b):
            y0, y1 = YG[0][b], YG[1][b]
            t1 = S.do(lambda e: e.activation(y0[:, :], y0[:, :], ACT.Copy, bias=0.0, scale=keep[:, 4 + b:5 + b]),
                      yg_tok[b], v_before)
            return V.do(lambda e: e.scalar_tensor_tensor(y0[:, :], y1[:, :], keep[:, 8 + b:9 + b], y0[:, :],
                                                         ALU.mult, ALU.add), t1, v_before)

        y_sum = {0: weigh(0)}
        for b in range(4):
            y0, t2 = YG[0][b], y_sum[b]
            if b + 1 < 4:
                y_sum[b + 1] = weigh(b + 1)
            for hf in range(2):
                bank = banks[bn % 8]
                bn += 1
                P.wait(bank.free, t2)
                for k in range(4):
                    fn = transpose(bank.ap[:, k * 128:(k + 1) * 128],
                                   y0[:, (4 * hf + k) * 128:(4 * hf + k + 1) * 128], ident[:, :])
                    if k < 3:
                        P.plain(fn)
                    else:
                        t3 = P.do(fn)
                xs = X[:, 4 * hf:4 * hf + 4, b * 128:(b + 1) * 128]
                t4 = V.do(lambda e: e.tensor_tensor(xs, xs, bank.ap[:, :].rearrange("p (k q) -> p k q", q=128),
                                                    ALU.add), t3)
                bank.free = [t4]
        xmoe = [t4]

        at_branch = [(V.sem, V.n), (S.sem, S.n), (G.sem, G.n), (P.sem, P.n)]
        oq = {q: Queue(q.eng, sem(f"o_{n}")) for q, n in ((P, "pe"), (V, "dve"), (S, "act"))}
        oY = Queue(nc.sync, None)
        oP, oV, oS = oq[P], oq[V], oq[S]
        ow = [count(f"s_ow{i}") for i in range(2)]
        oGU = [at(f"oGU{i}", [128, 8, 512], F, 16 + 16 * i) for i in range(2)]
        oDN = [at(f"oDN{i}", [128, 2, 1024], F, 48 + 8 * i) for i in range(2)]
        odg = at("odg", [128, T], F, 144)
        oa = [at(f"oa{i}", [128, T], F, 146 + 2 * i) for i in range(2)]
        ob_ = [at(f"ob{i}", [128, T], F, 150 + 2 * i) for i in range(2)]

        def rest_load(x, used):
            s = x % 2
            ow[s].load(oY, lambda e: e.dma_start(
                oGU[s][:, :, :], A["w_gu"][x].rearrange("p (k n) -> p k n", n=512)), used)
            return ow[s].load(oY, lambda e: e.dma_start(
                oDN[s][:, :, :], A["w_dn"][x].rearrange("p (k n) -> p k n", n=1024)), used)

        def rest_all():
            gate, ups, outs = banks[0].ap, [b.ap for b in banks[1:5]], [b.ap for b in banks[5:8]]
            free = {i: None for i in range(8)}
            used, hid_used, dg_used, wt, x_tok = {}, None, None, {}, None
            wt[0] = rest_load(0, None)
            wt[1] = rest_load(1, None)
            for x in range(NE):
                s = x % 2
                t0 = None
                for b in range(4):
                    t0 = oV.do(lambda e, b=b: e.tensor_scalar(odg[:, b * 128:(b + 1) * 128], ident[:, :],
                                                              GO[:, b, x:x + 1], None, ALU.mult), dg_used)
                tg = oP.do(lambda e: e.matmul(gate[:, :], ones[:, :], odg[:, :], start=True, stop=True), t0, free[0])
                dg_used = tg
                oP.wait(wt[x])
                hid_tok = []
                for m in range(2):
                    t = []
                    for j in range(2):
                        oP.wait(free[1 + 2 * m + j])
                        for k in range(8):
                            fn = lambda e, k=k: e.matmul(
                                ups[2 * m + j][:, :], oGU[s][:, k, (2 * j + m) * 128:(2 * j + m + 1) * 128],
                                XG[:, k, :], start=(k == 0), stop=(k == 7))
                            if k == 7:
                                t.append(oP.do(fn))
                            else:
                                oP.plain(fn)
                    a, b = oa[m], ob_[m]
                    t1 = oV.do(lambda e: e.tensor_tensor(a[:, :], ups[2 * m][:, :], rbc[:, :], ALU.mult), t[0], hid_used)
                    t2 = oV.do(lambda e: e.tensor_tensor(b[:, :], ups[2 * m + 1][:, :], rbc[:, :], ALU.mult), t[1])
                    free[1 + 2 * m], free[2 + 2 * m] = t1, t2
                    t3 = oS.do(lambda e: e.activation(a[:, :], a[:, :], ACT.Silu), t1)
                    t4 = oV.do(lambda e: e.tensor_tensor(b[:, :], b[:, :], gate[:, :], ALU.mult), t2, tg)
                    free[0] = t4
                    hid_tok.append(oV.do(lambda e: e.tensor_tensor(a[:, :], a[:, :], b[:, :], ALU.mult), t3, t4))
                for i in range(8):
                    n = 5 + i % 3
                    oP.wait(free[n], hid_tok)
                    for k in range(2):
                        fn = lambda e, k=k: e.matmul(outs[n - 5][:, :], oDN[s][:, k, i * 128:(i + 1) * 128],
                                                     oa[k][:, :], start=(k == 0), stop=(k == 1))
                        if k:
                            hid_used = oP.do(fn)
                        else:
                            oP.plain(fn)
                    x_tok = oV.do(lambda e: e.tensor_tensor(X[:, i, :], X[:, i, :], outs[n - 5][:, :], ALU.add),
                                  hid_used, x_tok)
                    free[n] = x_tok
                if x + 2 < NE:
                    wt[x + 2] = rest_load(x + 2, hid_used)

        with nc.If(left_over > 0):
            for q in (oP, oV, oS, oY):
                q.wait(at_branch)
            rest_all()
            for q in (oP, oV, oS, oY):
                q.wait((oP.sem, oP.n), (oV.sem, oV.n), (oS.sem, oS.n))
        table("natural_log_exp_and_others")

        before = [(V.sem, V.n), (S.sem, S.n), (G.sem, G.n), (P.sem, P.n)]
        for i in range(8):
            n3.tile(i, xmoe, moe_done + before)
            if i < 3:
                stream2.split_to(i)
        first = gemm_group(stream2, [nxt() for _ in range(3)], n3.tiles(), G8)
        n3.finish(banks[7], n2r)
        ropeA = at("ropeA", [128, 2, T], F, 156)
        ropeB = at("ropeB", [128, 2, T], F, 152)
        t_tabA = c_t2.load(Y, lambda e: e.dma_start(ropeA[:, :, :], A["c_ropeA"].rearrange("p (a t) -> p a t", a=2)),
                           before)
        qA = at("qA", [128, 4, T], F, 144)
        kA = at("kA", [128, T], F, 152)
        vA = at("vA", [128, 4, 128], F, 154)
        CH = at("CH", [128, 2, 5, T], R, 182)
        KR = at("KR", [128, T], F, 202)
        wz = [at(f"wz{i}", [128, T], F, 162 + 2 * i) for i in range(2)]
        ws = [at(f"ws{i}", [128, T], F, 166 + 2 * i) for i in range(2)]
        wn = [at(f"wn{i}", [128, T], F, 170 + 2 * i) for i in range(2)]
        facc = [at(f"facc{i}", [128, T], F, 174 + 2 * i) for i in range(2)]
        fq = [at(f"fq{i}", [128, T], F, 178 + 2 * i) for i in range(2)]
        fr = {0: list(before), 1: list(before)}
        rX = [n3.r, t_tabA]
        ZA = (wz, ws, wn)
        qk2 = {}

        def v_natural(i, z, t1, dst, names, p0=0, p1=128):
            b2 = banks[names]
            P.wait(t1, b2.free)
            w = p1 - p0
            for b in range(4):
                f = transpose(b2.ap[:, b * w:(b + 1) * w], z[p0:p1, b * 128:(b + 1) * 128], ident[p0:p1, p0:p1])
                if b < 3:
                    P.plain(f)
                else:
                    t2 = P.do(f)
            t3 = V.do(lambda e: e.tensor_copy(dst, b2.ap[:, 0:4 * w].rearrange("p (a b) -> p a b", b=w)), t2)
            b2.free = [t3]
            return [t3], t2

        for i in range(6):
            bank, tok = first[i]
            if i < 5:
                dst, g = (qA[:, i, :], "aqg") if i < 4 else (kA[:, :], "akg")
                head_norm_rope(i, bank, tok, rbc, col(g), permA, ropeA, dst, fr, rX, ZA,
                               lambda t, i=i: qk2.update({i if i < 4 else "k": t}))
            else:
                z = wz[i % 2]
                t1 = V.do(lambda e: e.tensor_tensor(z[:, :], bank.ap[:, :], rbc[:, :], ALU.mult), tok, rX,
                          fr.get(i % 2))
                bank.free = [t1]

                def w(i=i, z=z, t1=t1):
                    qk2["v"], t = v_natural(i, z, t1, vA[:, :, :], 4 + i % 2)
                    fr[i % 2] = [t]
                later(w)
            if i < 5:
                first.append(gemm(stream2, [(nxt(), n3.tiles())], G8))

        c_tok, fac_tok = {}, [[], []]
        for i in range(5):
            bank, tok = first[6 + i] if i < 2 else gemm(stream2, [(nxt(), n3.tiles())], G8)
            a = 0 if i < 3 else 1
            th = S.do(lambda e: e.activation(CH[:, 0, i, :], bank.ap[:, :], ACT.Identity, bias=0.0,
                                             scale=col("bg", i)), tok, before)
            q = tm[i % 2]
            dst = facc[a] if i in (0, 3) else q
            ts = S.do(lambda e: e.activation(dst[:, :], bank.ap[:, :], ACT.Square), tok, before,
                      [] if i in (0, 3) else sq_free[i % 2])
            tl = V.do(lambda e: e.scalar_tensor_tensor(CH[:, 1, i, :], bank.ap[:, :], col("bg", i),
                                                       CH[:, 0, i, :].bitcast(F), ALU.mult, ALU.subtract),
                      th, ts, tok, before)
            c_tok[i] = [th, tl]
            if i in (0, 3):
                fac_tok[a] = [ts]
            else:
                fac_tok[a] = [V.do(lambda e: e.tensor_tensor(facc[a][:, :], facc[a][:, :], q[:, :], ALU.add),
                                   ts, fac_tok[a])]
                sq_free[i % 2] = list(fac_tok[a])
            bank.free = [th, tl, ts]
        bank, tok = gemm(stream2, [(nxt(), n3.tiles())], G8)
        flush()
        t_krz = V.do(lambda e: e.tensor_tensor(KR[:, :], bank.ap[:, :], rbc[:, :], ALU.mult), tok, n3.r, before)
        bank.free = [t_krz]
        r2 = wn[0]
        f_ready = []
        t_r2 = V.do(lambda e: e.tensor_tensor(r2[:, :], rbc[:, :], rbc[:, :], ALU.mult), n3.r, fr[0], fr[1])
        for a, w in ((0, 384), (1, 256)):
            bk = banks[4 + a]
            t1 = P.do(lambda e: e.matmul(bk.ap[:, :], ones[:, :], facc[a][:, :], start=True, stop=True),
                      fac_tok[a], bk.free)
            t2 = V.do(lambda e: e.tensor_tensor(facc[a][:, :], bk.ap[:, :], r2[:, :], ALU.mult), t1, t_r2)
            bk.free = [t2]
            t3 = S.do(lambda e: e.activation(facc[a][:, :], facc[a][:, :], ACT.Ln, bias=col("eps"), scale=1.0 / w),
                      t2)
            t4 = S.do(lambda e: e.activation(facc[a][:, :], facc[a][:, :], ACT.Exp, scale=-0.5), t3)
            f_ready.append(V.do(lambda e: e.tensor_tensor(fq[a][:, :], facc[a][:, :], rbc[:, :], ALU.mult), t4, n3.r))
        fcol = keep[:, 16:20]
        P.wait(f_ready[1], banks[6].free)
        for b in range(4):
            fn = lambda e, b=b: e.matmul(banks[6].ap[:, b:b + 1], fq[1][0:1, b * 128:(b + 1) * 128], ones[0:1, 0:1],
                                         start=True, stop=True)
            if b < 3:
                P.plain(fn)
            else:
                t1 = P.do(fn)
        t_fcol = V.do(lambda e: e.tensor_copy(fcol, banks[6].ap[:, 0:4]), t1)
        banks[6].free = [t_fcol]

        PTA = [[at("PTA0", [128, 4, T], F, 162), at("PTA1", [128, 4, T], F, 170)],
               [at("PTA2", [128, 4, T], F, 24), at("PTA3", [128, 4, T], F, 32)]]
        PbA = [at(f"PbA{i}", [128, T], F, 16 + 2 * i) for i in range(4)]
        fQ = [at(f"fQ{i}", [128, T], F, 178 + 2 * i) for i in range(2)]
        before = [(V.sem, V.n), (S.sem, S.n), (G.sem, G.n), (P.sem, P.n)]
        FULL = [(0, 4)] * 4
        H1v = H[1]
        mix_tok = {}
        prs = []
        for i in range(4):
            def out(bank, to, i=i):
                mix_tok[i] = split_out(H1v[:, 0, i, :], H1v[:, 1, i, :])(bank, to)
                return mix_tok[i]

            prs.append(dict(
                q=lambda hd, b, i=i: qA[64 * hd:64 * hd + 64, i, b * 128:(b + 1) * 128],
                k=lambda hd, lo, hi: kA[64 * hd:64 * hd + 64, lo * 128:hi * 128],
                kbs=FULL, ready=lambda hd, b, i=i: [qk2[i], qk2["k"]], mask=None, sink=None,
                v=lambda kb, hd: vA[:, kb, 64 * hd:64 * hd + 64], v_ready=qk2["v"], out=out))
        attention(prs, PTA, PbA, 0.125, before, before, ([0, 1, 2, 7], [3, 4], [5, 6]))

        before = [(V.sem, V.n), (S.sem, S.n), (G.sem, G.n), (P.sem, P.n)]
        qB = at("qB", [128, 8, T], F, 16)
        kB = at("kB", [128, 8, T], F, 32)
        vB = at("vB", [128, 4, T], F, 144)
        c_tq = count("s_turn")
        turnQ = [at(f"turnQ{i}", [128, T], F, 156 + 2 * i) for i in range(2)]
        bz = at("bz", [128, T], F, 162)
        bs = at("bs", [128, T], F, 166)
        t_tabB = c_t2.load(Y, lambda e: e.dma_start(ropeB[:, :, :], A["c_ropeB"].rearrange("p (a t) -> p a t", a=2)),
                           before)
        for i in range(2):
            t_tabQ = c_tq.load(Y, lambda e: e.dma_start(turnQ[i][:, :], A["c_turnQ"][i]), before)
        cq = [(CH[:, 0, k, :], CH[:, 1, k, :], c_tok[k]) for k in range(3)]
        ckv = [(CH[:, 0, k, :], CH[:, 1, k, :], c_tok[k]) for k in range(3, 5)]
        t_kr = rope_only(1, KR, t_krz, permB, ropeB, bs[:, :], {}, [t_tabB, before], bz, bs)
        t_kc = []
        for odd in range(2):
            p0 = 0 if odd else 64
            t_kc.append(G.do(lambda e: e.tensor_copy(
                kB[p0:p0 + 64, :, :].rearrange("p (h o) t -> p h o t", o=2)[:, :, odd, :],
                bs[p0:p0 + 64, :].unsqueeze(1).to_broadcast([64, 4, T])), t_kr, before))
        t_fq = [V.do(lambda e, i=i: e.tensor_tensor(turnQ[i][:, :], turnQ[i][:, :], fq[0][:, :], ALU.mult),
                     t_tabQ, f_ready) for i in range(2)]
        bq, bk2, bv = {}, {}, {}
        for i in range(8):
            bank, tok = gemm(stream2, [(nxt(), cq)], G8)
            bq[i] = [V.do(lambda e: e.tensor_tensor(qB[:, i, :], bank.ap[:, :], turnQ[i % 2][:, :], ALU.mult), tok,
                          t_fq, before)]
            bank.free = bq[i]
        for i in range(4):
            bank, tok = gemm(stream2, [(nxt(), ckv)], G8)
            for odd in range(2):
                p0 = 64 * odd
                t1 = V.do(lambda e: e.tensor_tensor(kB[p0:p0 + 64, 2 * i + odd, :], bank.ap[p0:p0 + 64, :],
                                                    fq[1][p0:p0 + 64, :], ALU.mult), tok, f_ready, before)
                bk2[2 * i + odd] = [t1, t_kc]
            bank.free = [t1]
        c = nxt()
        stream2.split_to(c)
        for b in range(4):
            bank = banks[4 + b]
            P.wait(bank.free, stream2.ready[c], c_tok[3], c_tok[4])
            n = 0
            for k in range(2):
                hi, lo = (CH[:, a, 3 + k, b * 128:(b + 1) * 128] for a in range(2))
                wh, wl = (w[c % 3][:, k * 512:(k + 1) * 512] for w in (whi, wlo))
                for x, w in ((hi, wh), (lo, wh), (hi, wl)):
                    fn = lambda e, n=n: e.matmul(bank.ap[:, :], x, w, start=(n == 0), stop=(n == 5))
                    n += 1
                    if n == 6:
                        tok = P.do(fn)
                    else:
                        P.plain(fn)
            bv[b] = [S.do(lambda e: e.activation(vB[:, b, :], bank.ap[:, :], ACT.Copy, bias=0.0,
                                                 scale=fcol[:, b:b + 1]), tok, t_fcol, before)]
            bank.free = bv[b]
        stream2.used(c, tok)
        stream2.split_to(c + 2)
        PTB = [[at("PTB0", [128, 4, T], F, 162), at("PTB1", [128, 4, T], F, 170)],
               [at("PTB2", [128, 4, T], F, 190), at("PTB3", [128, 4, T], F, 198)]]
        PbB = [at(f"PbB{i}", [128, T], F, 182 + 2 * i) for i in range(4)]
        before = [(V.sem, V.n), (S.sem, S.n), (G.sem, G.n), (P.sem, P.n)]
        prs = []
        for i in range(4):
            def out(bank, to, i=i):
                mix_tok[4 + i] = split_out(H1v[:, 0, 4 + i, :], H1v[:, 1, 4 + i, :])(bank, to)
                return mix_tok[4 + i]

            prs.append(dict(
                q=lambda hd, b, i=i: qB[:, 2 * i + hd, b * 128:(b + 1) * 128],
                k=lambda hd, lo, hi, i=i: kB[:, 2 * i + hd, lo * 128:hi * 128],
                kbs=FULL, ready=lambda hd, b, i=i: [bq[2 * i + hd], bk2[2 * i + hd]], mask=None, sink=None,
                v=lambda kb, hd, i=i: vB[:, kb, 64 * (2 * i + hd):64 * (2 * i + hd) + 64],
                v_ready=[bv[b] for b in range(4)], out=out))
        attention(prs, PTB, PbB, float(np.float32(96.0) ** np.float32(-0.5)), before, before,
                  ([0, 1, 2, 7], [3, 4], [5, 6]))

        def project(tiles, Hn, gname, prev, h_free):
            nn = Norm(Hn, gname, prev.acc_read)
            for i in range(8):
                bank, tok = gemm(stream2, [(nxt(), tiles)], G8)
                xt = V.do(lambda e: e.tensor_tensor(X[:, i, :], X[:, i, :], bank.ap[:, :], ALU.add), tok, (V.sem, V.n))
                bank.free = [xt]
                nn.tile(i, [xt], h_free, split=Hn is not None)
            nn.finish(banks[7], [(V.sem, V.n), prev.r])
            return nn

        U = at("U", [128, 2, 8, T], R, 144)
        fu = [at(f"fu{i}", [128, T], F, 176 + 2 * i) for i in range(4)]

        def ffn(nn, Hn, gname, h_free):
            before = [(V.sem, V.n), (S.sem, S.n), (G.sem, G.n), (P.sem, P.n)]
            ffree = [list(before), list(before)]
            down = list(before)
            out = Norm(Hn, gname, nn.acc_read)
            for q in range(4):
                u_tok = {}
                for i in range(8):
                    bank, tok = gemm(stream2, [(nxt(), nn.tiles())], G8)
                    a, b = fu[2 * (i % 2)], fu[2 * (i % 2) + 1]
                    t1 = V.do(lambda e: e.scalar_tensor_tensor(a[:, :], bank.ap[:, :], 0.0, rbc[:, :],
                                                               ALU.max, ALU.mult), tok, nn.r, ffree[i % 2])
                    bank.free = [t1]
                    t2 = S.do(lambda e: e.activation(b[:, :], a[:, :], ACT.Square), t1, ffree[i % 2])
                    t3 = S.do(lambda e: e.copy(U[:, 0, i, :], b[:, :]), t2, down)
                    t4 = V.do(lambda e: e.tensor_tensor(U[:, 1, i, :], b[:, :], U[:, 0, i, :].bitcast(F),
                                                        ALU.subtract), t3, down)
                    ffree[i % 2] = [t4]
                    u_tok[i] = [t3, t4]
                tiles = [(U[:, 0, k, :], U[:, 1, k, :], u_tok[k]) for k in range(8)]
                for i in range(8):
                    bank, tok = gemm(stream2, [(nxt(), tiles)], G8)
                    xt = V.do(lambda e: e.tensor_tensor(X[:, i, :], X[:, i, :], bank.ap[:, :], ALU.add), tok,
                              (V.sem, V.n))
                    bank.free = [xt]
                    if q == 3:
                        out.tile(i, [xt], h_free, split=Hn is not None)
                down = [tok]
            out.finish(banks[7], [(V.sem, V.n)])
            return out

        before = [(V.sem, V.n), (S.sem, S.n), (G.sem, G.n), (P.sem, P.n)]
        mixt = [(H[1][:, 0, k, :], H[1][:, 1, k, :], mix_tok[k]) for k in range(8)]
        n4 = project(mixt, H[0], "gf0", n3, before)
        n5 = ffn(n4, H[1], "gm1", [(P.sem, P.n)])

        before = [(V.sem, V.n), (S.sem, S.n), (G.sem, G.n), (P.sem, P.n)]
        qC = at("qC", [128, 8, T], F, 144)
        kC = at("kC", [128, 8, T], F, 160)
        vC = at("vC", [128, 4, D], F, 176)
        cz = [at(f"cz{i}", [128, T], F, 192 + 2 * i) for i in range(2)]

        def by_row(ap):
            return ap.rearrange("p (r b c) -> p r b c", b=4, c=16)

        def blocked(ap):
            return ap.rearrange("p (b r c) -> p r b c", b=4, c=16)

        rb8 = at("rb8", [128, T], F, 196)
        t_rb8 = V.do(lambda e: e.tensor_scalar(rb8[:, :], rbc[:, :], 0.125, None, ALU.mult), n5.r, before)
        qc, kc, vc = {}, {}, {}
        zf = [list(before), list(before)]
        for i in range(24):
            bank, tok = gemm(stream2, [(nxt(), n5.tiles())], G8)

            if i < 16:
                dst = (qC if i < 8 else kC)[:, i % 8, :]
                if i < 8:
                    t1 = V.do(lambda e: e.tensor_tensor(blocked(dst), by_row(bank.ap[:, :]), by_row(rb8[:, :]),
                                                        ALU.mult), tok, t_rb8, before)
                else:
                    t1 = V.do(lambda e: e.tensor_tensor(blocked(dst), by_row(bank.ap[:, :]), by_row(rbc[:, :]),
                                                        ALU.mult), tok, n5.r, before)
                bank.free = [t1]
                (qc if i < 8 else kc)[i % 8] = [t1]
            else:
                def w(i=i, bank=bank, tok=tok):
                    z = cz[i % 2]
                    t1 = V.do(lambda e: e.tensor_tensor(blocked(z[:, :]), by_row(bank.ap[:, :]), by_row(rbc[:, :]),
                                                        ALU.mult), tok, n5.r, zf[i % 2])
                    bank.free = [t1]
                    vc[i % 8], tf = v_natural(i, z, t1, vC[:, :, 128 * (i % 8):128 * (i % 8) + 128], 4 + i % 2)
                    zf[i % 2] = [tf]
                later(w)
        flush()
        before = [(V.sem, V.n), (S.sem, S.n), (G.sem, G.n), (P.sem, P.n)]
        bia = [at(f"bia{i}", [128, 896], F, 192 + 3.5 * i) for i in range(2)]
        PTC = [[at("PTC0", [128, 4, T], F, 48), at("PTC1", [128, 4, T], F, 56)],
               [at("PTC2", [128, 4, T], F, 64), at("PTC3", [128, 4, T], F, 72)]]
        PbC = [at(f"PbC{i}", [128, 384], F, 199.25 + 1.5 * i) for i in range(4)]
        c_b = [count("s_bia0"), count("s_bia1")]
        bia_at, bia_free = {}, [list(before), list(before)]
        bia_used = {}

        def load_bias(h):
            bia_at[h] = c_b[h % 2].load(Y, lambda e: e.dma_start(bia[h % 2][:, :], A["c_bias"][h]), bia_free[h % 2])

        load_bias(0)
        load_bias(1)
        BO = [(0, 256), (256, 640), (256, 640), (640, 896)]

        def used(pi, hd, b, t):
            if b == 3:
                h = 2 * pi + hd
                bia_free[h % 2] = [t]
                if h + 2 < 16:
                    load_bias(h + 2)

        odd_tok = {}
        prs = []

        for i in range(8):
            def out(bank, to, i=i):
                view = lambda ap: ap[:, :].rearrange("p (b r c) -> p r b c", b=4, c=16)
                odd_tok[i] = split_out(by_row(H[0][:, 0, i, :]), by_row(H[0][:, 1, i, :]), view)(bank, to)
                return odd_tok[i]

            prs.append(dict(
                q=lambda hd, b, i=i: qC[64 * hd:64 * hd + 64, i, b * 128:(b + 1) * 128],
                k=lambda hd, lo, hi, i=i: kC[64 * hd:64 * hd + 64, i, lo * 128:hi * 128],
                kbs=KBS, ready=lambda hd, b, i=i: [qc[i], kc[i]],
                mask=lambda hd, b: bia[hd][:, BO[b][0]:BO[b][1]],
                mask_ready=lambda hd, i=i: bia_at[2 * i + hd], mask_used=lambda hd, b, t, i=i: used(i, hd, b, t),
                sink=None,
                v=lambda kb, hd, i=i: vC[:, kb, 128 * i + 64 * hd:128 * i + 64 * hd + 64], v_ready=vc[i], out=out))
        attention(prs, PTC, PbC, 1.0, before, before, ([0, 1, 2, 7], [3, 4], [5, 6]))

        before = [(V.sem, V.n), (S.sem, S.n), (G.sem, G.n), (P.sem, P.n)]
        oddt = [(H[0][:, 0, k, :], H[0][:, 1, k, :], odd_tok[k]) for k in range(8)]
        n6 = project(oddt, H[1], "gf1", n5, before)
        n7 = ffn(n6, None, None, [])

        c_out = count("s_out")
        for i in range(8):
            t1 = V.do(lambda e: e.scalar_tensor_tensor(X[:, i, :], X[:, i, :], col("gfin", i), rbc[:, :],
                                                       ALU.mult, ALU.mult), n7.r, (V.sem, V.n), (S.sem, S.n))
            t_out = c_out.load(Y, lambda e: e.dma_start(A["outT"][:, i * T:(i + 1) * T], X[:, i, :]), t1)
        Y.wait(t_out, y_tok, t_sc, zeroed)



VECS = [("eps", 1), ("g1", 8), ("g2", 8), ("gm0", 8), ("gf0", 8), ("gm1", 8), ("gf1", 8), ("gfin", 8),
        ("qg", 1), ("kg", 1), ("aqg", 1), ("akg", 1), ("sink", 8), ("cv0", 4), ("cv1", 4),
        ("cv2", 4), ("cvb", 4), ("bg", 5)]


def tables():
    f = np.float32
    c = {}
    eye = np.eye(128, dtype=f)
    c["c_ident"] = eye
    c["c_ones"] = np.ones((128, 128), f)
    b = np.zeros((128, 128), f)
    b[:64, :64] = 1
    b[64:, 64:] = 1
    c["c_bones"] = b
    c["c_triu"] = np.triu(np.ones((128, 128), f), 1)
    c["c_io32"] = np.broadcast_to(np.arange(32, dtype=f), (128, 32)).copy()

    def perm(pairs, size=128):
        m = np.zeros((128, 128), f)
        for a, b_ in pairs:
            m[b_, a] = -1
            m[a, b_] = 1
        return m

    t = np.arange(T, dtype=f)

    def table(size, parts):
        cs = np.zeros((size, 2, T), f)
        cs[:, 0] = 1
        for a, b_, ang in parts:
            for i in (a, b_):
                cs[i, 0], cs[i, 1] = np.cos(ang), np.sin(ang)
        return cs.reshape(size, 2 * T)

    inv = (f(500000.0) ** (-np.arange(0, 16, 2, dtype=f) / f(16))).astype(f)
    pf = [(64 * h + i, 64 * h + i + 8) for h in range(2) for i in range(8)]
    c["c_permF"] = perm(pf)
    c["c_ropeF"] = table(128, [(64 * h + i, 64 * h + i + 8, (t * inv[i]).astype(f)) for h in range(2) for i in range(8)])
    row, colm = (t // 64).astype(f), (t % 64).astype(f)

    def axial(base, d):
        inv = (f(10000.0) ** (-np.arange(0, d, 2, dtype=f) / f(d))).astype(f)
        out = []
        for part, pos in ((0, row), (1, colm)):
            for i in range(d // 2):
                a = base + part * d + i
                out.append((a, a + d // 2, (pos * inv[i]).astype(f)))
        return out

    pa = axial(0, 32) + axial(64, 32)
    c["c_permA"] = perm([x[:2] for x in pa])
    c["c_ropeA"] = table(128, pa)
    pb = [x for p in range(4) for x in axial(32 * p, 16)]
    c["c_permB"] = perm([x[:2] for x in pb])
    c["c_ropeB"] = table(128, pb)
    turn = np.ones((2, 128, T), f)
    for i, p in enumerate((64, 0)):
        for a, b_, ang in axial(0, 16):
            turn[i, p + a], turn[i, p + b_] = np.cos(ang), np.cos(ang)
            turn[i, p + 32 + a], turn[i, p + 32 + b_] = -np.sin(ang), np.sin(ang)
    c["c_turnQ"] = turn
    i, j = np.arange(128)[:, None], np.arange(384)[None, :] - 128
    c["c_maskF"] = np.where(np.abs(i - j) <= 128, 0, NEG).astype(f)
    return c


def layout(v):
    f = np.float32
    a = {}

    def arr(n):
        return np.asarray(v[n])

    def tiles(w, m=128):
        k, n = w.shape
        return np.ascontiguousarray(w.reshape(k // 128, 128, n // m, m).transpose(2, 1, 0, 3)).reshape(
            n // m, 128, (k // 128) * m)

    x = arr("x")[0]
    a["xT"] = np.ascontiguousarray(x.T.reshape(8, 128, T).transpose(1, 0, 2)).reshape(128, 8 * T)
    w = arr("w_in")[0]
    pair = np.concatenate([np.r_[64 * i:64 * i + 64, 64 * (i + 4):64 * (i + 4) + 64] for i in range(4)])
    a["w1_in"] = tiles(np.concatenate([w[:, 0:512][:, pair], w[:, 512:768]], 1))
    cb, cc, cx = w[:, 768:1280], w[:, 1280:1792], w[:, 1792:2304]
    a["w1_conv"] = tiles(np.concatenate([p[:, 128 * i:128 * i + 128] for i in range(4) for p in (cc, cx, cb)], 1))
    a["w1_ga"] = tiles(w[:, 2304:3328])
    a["w1_gc"] = tiles(w[:, 3328:4352])
    a["w1_ap"] = tiles(arr("w_attn_proj")[0][pair])
    a["w1_cp"] = tiles(arr("w_conv_proj")[0])
    a["w1_out"] = tiles(arr("w_out")[0])
    wr = np.concatenate([arr("w_router_group")[0], arr("w_router_expert")[0]], 1)
    a["w_router"] = np.ascontiguousarray(wr.reshape(8, 128, 36).transpose(1, 0, 2)).reshape(128, 288)
    br = np.concatenate([arr("b_router_group")[0], arr("b_router_expert")[0]])
    a["b_router"] = np.broadcast_to(br, (128, 36)).copy()
    gu = np.concatenate([arr("w_gate_e")[0], arr("w_up_e")[0]], 2)
    a["w_gu"] = np.ascontiguousarray(gu.reshape(NE, 8, 128, 512).transpose(0, 2, 1, 3)).reshape(NE, 128, 4096)
    a["w_dn"] = np.ascontiguousarray(arr("w_down_e")[0].reshape(NE, 2, 128, D).transpose(0, 2, 1, 3)).reshape(
        NE, 128, 2048)
    w = arr("ev_w_in_2")[0]
    a["w2_in"] = tiles(np.concatenate([w[:, 0:512][:, pair], w[:, 512:768]], 1))
    a["w2_c"] = tiles(w[:, 768:1408])
    a["w2_kr"] = tiles(np.concatenate([w[:, 1408:1440]] * 4, 1))
    partner = np.arange(32) ^ 8
    uq = []
    for i in range(8):
        h = arr("ev_b_w_uq_2")[0][:, 96 * i:96 * i + 96]
        nope, rope = h[:, :64], h[:, 64:]
        uq += [rope, rope[:, partner], nope] if i % 2 else [nope, rope, rope[:, partner]]
    a["w2_uq"] = tiles(np.concatenate(uq, 1))
    ukv = arr("ev_b_w_ukv_2")[0].reshape(256, 8, 128)
    a["w2_uk"] = tiles(np.ascontiguousarray(ukv[:, :, :64]).reshape(256, 512))
    a["w2_uv"] = np.ascontiguousarray(ukv[:, :, 64:]).reshape(2, 128, 512).transpose(1, 0, 2).reshape(128, 1024).copy()
    rows = np.concatenate([pair, np.arange(512, 1024)])
    a["w2_evo"] = tiles(arr("ev_w_out_2")[0][rows])
    for l in range(2):
        a[f"w_up{l}"] = tiles(arr("ffn_w_up_2")[l])
        d = arr("ffn_w_down_2")[l].reshape(4, 8, 128, 8, 128).transpose(0, 3, 2, 1, 4)
        a[f"w_down{l}"] = np.ascontiguousarray(d).reshape(32, 128, 1024)
    a["w2_qkv"] = tiles(arr("od_w_qkv_2")[0])
    a["w2_odo"] = tiles(arr("od_w_out_2")[0])

    rpb = arr("od_rpb_2")[0]
    q = np.arange(128)
    qr, qcl = q // 16, q % 16
    out = np.full((16, 128, 896), NEG, f)
    for base, nb, first, lo in ((0, 2, 0, 0), (256, 3, 1, 0), (640, 2, 3, 2)):
        k = np.arange(nb * 128)
        kr, kcl = (k % 128) // 16, (lo + k // 128) * 16 + k % 16
        c = first * 16 + qcl
        cs = np.clip(c - 8, 0, 48)
        valid = (kcl[None] >= cs[:, None]) & (kcl[None] < cs[:, None] + 16)
        qi, ki = np.nonzero(valid)
        out[:, qi, base + ki] = rpb[:, kr[ki] - qr[qi] + 7, kcl[ki] - c[qi] + 15]
    a["c_bias"] = out

    vec = np.zeros((128, 128), f)
    cols = {"eps": np.full((1, 128), EPS, f)}

    def feat(g):
        return np.asarray(g).reshape(-1, 128)

    cols["g1"], cols["g2"] = feat(arr("norm1_g")[0]), feat(arr("norm2_g")[0])
    for l in range(2):
        cols[f"gm{l}"], cols[f"gf{l}"] = feat(arr("norm_mix_2")[l]), feat(arr("norm_ffn_2")[l])
    cols["gfin"] = feat(arr("final_norm_2"))
    for n, s in (("qg", "q_norm_g"), ("kg", "k_norm_g"), ("aqg", "ev_a_q_norm_2"), ("akg", "ev_a_k_norm_2")):
        g = arr(s)[0]
        cols[n] = np.concatenate([g, g])[None]
    cols["sink"] = np.broadcast_to(arr("attn_sink")[0][:, None], (8, 128))
    for j in range(3):
        cols[f"cv{j}"] = feat(arr("conv_w")[0, j])
    cols["cvb"] = feat(arr("conv_b")[0])
    cols["bg"] = feat(np.concatenate([arr("ev_b_q_norm_2")[0], arr("ev_b_kv_norm_2")[0]]))
    c = 0
    for n, w_ in VECS:
        if n in cols:
            vec[:, c:c + w_] = cols[n].T
        c += w_
    a["vec"] = vec
    a.update(tables())
    return a


def kernel(**inputs):
    import concourse.bacc as bacc
    from concourse.bass_utils import run_bass_kernel_spmd as run

    nc = bacc.Bacc("TRN2", target_bir_lowering=False, num_devices=1)
    arrays = layout(inputs)
    A = {}
    for name, a in arrays.items():
        A[name] = nc.dram_tensor("in_" + name, a.shape, mybir.dt.from_np(a.dtype), kind="ExternalInput").ap()
    A["hbuf"] = nc.dram_tensor("hbuf", (SLOTS, D), F, kind="Internal").ap()
    A["ybuf"] = nc.dram_tensor("ybuf", (SLOTS, D), F, kind="Internal").ap()
    A["outT"] = nc.dram_tensor("outT", (128, 8 * T), F, kind="ExternalOutput").ap()
    program(nc, A)
    r = run(nc, [{"in_" + n: a for n, a in arrays.items()}], core_ids=[0])
    o = r.results[0]["outT"].reshape(128, 8, T).transpose(2, 1, 0).reshape(1, T, D)
    return np.ascontiguousarray(o)
```

```python
from contextlib import ExitStack

import numpy as np

import concourse.bass as bass
from concourse import mybir

F = mybir.dt.float32
R = mybir.dt.float32r
I32 = mybir.dt.int32
U32 = mybir.dt.uint32
ALU = mybir.AluOpType
ACT = mybir.ActivationFunctionType
AX = mybir.AxisListType.X

T = 512
D = 1024
KB = 1024
BASE = 16512
EPS = 1e-6
NEG = -1e30
CAP = 64
NE = 32
SLOTS = NE * CAP


class Queue:

    def __init__(self, eng, sem):
        self.eng, self.sem, self.n, self.seen = eng, sem, 0, {}

    def wait(self, *tokens):
        for t in tokens:
            if t is None:
                continue
            if isinstance(t, list):
                self.wait(*t)
                continue
            sem, value = t
            if self.seen.get(sem.name, 0) < value:
                self.seen[sem.name] = value
                self.eng.wait_ge(sem, value)

    def do(self, fn, *tokens):
        self.wait(*tokens)
        self.n += 1
        fn(self.eng).then_inc(self.sem, 1)
        return (self.sem, self.n)

    def plain(self, fn, *tokens):
        self.wait(*tokens)
        fn(self.eng)


class Count:

    def __init__(self, sem):
        self.sem, self.n = sem, 0

    def load(self, queue, fn, *tokens):
        queue.wait(*tokens)
        self.n += 16
        fn(queue.eng).then_inc(self.sem, 16)
        return (self.sem, self.n)


class Bank:
    def __init__(self, ap):
        self.ap, self.free = ap, []


def program(nc, A):
    ctx = ExitStack()
    with ctx:
        def sem(name):
            return ctx.enter_context(nc.semaphore(name))

        def at(name, shape, dt, kb):
            return nc.alloc_sbuf_tensor_at(name, shape, dt, offset=BASE + int(kb * KB))

        P, V, S, G, Y = (Queue(e, sem(f"q_{n}")) for n, e in (
            ("pe", nc.tensor), ("dve", nc.vector), ("act", nc.scalar), ("pool", nc.gpsimd), ("sp", nc.sync)))

        def count(name):
            return Count(sem(name))

        banks = [Bank(ctx.enter_context(nc.psum_tensor(f"bank{i}", [128, 512], F))) for i in range(8)]

        X = at("X", [128, 8, T], F, 0)
        H = [at(f"H{i}", [128, 2, 8, T], R, 16 + 32 * i) for i in range(2)]
        raw = [at(f"raw{i}", [128, 1024], F, 80 + 4 * i) for i in range(6)]
        whi = [at(f"whi{i}", [128, 1024], R, 104 + 4 * i) for i in range(3)]
        wlo = [at(f"wlo{i}", [128, 1024], R, 116 + 4 * i) for i in range(3)]
        ident = at("ident", [128, 128], F, 128)
        ones = at("ones", [128, 128], F, 128.5)
        bones = at("bones", [128, 128], F, 129)
        permF = at("permF", [128, 128], F, 129.5)
        permA = at("permA", [128, 128], F, 130)
        permB = at("permB", [128, 128], F, 130.5)
        triu = at("triu", [128, 128], F, 131)
        vec = at("vec", [128, 128], F, 131.5)
        st = [at(f"st{i}", [128, 8], F, 132 + i / 32) for i in range(6)]
        keep = at("keep", [128, 96], F, 132.25)
        keepi = at("keepi", [128, 16], U32, 132.75)
        io32 = at("io32", [128, 32], F, 133)
        bro = at("bro", [128, 36], F, 133.25)
        wr = at("wr", [128, 8, 36], F, 133.5)
        rbc = at("rbc", [128, T], F, 136)
        acc = at("acc", [128, T], F, 138)
        tm = [at(f"tm{i}", [128, T], F, 140 + 2 * i) for i in range(2)]

        c_const, c_vec = count("s_const"), count("s_vec")
        vec_ready = c_vec.load(Y, lambda e: e.dma_start(vec[:], A["vec"]))
        c_x = [count(f"s_x{i}") for i in range(8)]
        xT = A["xT"].rearrange("p (k t) -> p k t", t=T)
        x_load = []

        def load_x(i):
            x_load.append(c_x[i].load(Y, lambda e: e.dma_start(X[:, i, :], xT[:, i, :])))

        consts = ((ident, "c_ident"), (ones, "c_ones"), (bones, "c_bones"), (permF, "c_permF"),
                          (permA, "c_permA"), (permB, "c_permB"), (triu, "c_triu"),
                  (io32, "c_io32"), (bro, "b_router"), (wr, "w_router"))
        VEC = {}
        for n, (name, w) in enumerate(VECS):
            VEC[name] = sum(k for _, k in VECS[:n])

        nsink = at("nsink", [128, 8], F, 134.625)
        t_ns = V.do(lambda e: e.tensor_scalar(nsink[:, :], vec[:, VEC["sink"]:VEC["sink"] + 8], -1.0, None,
                                              ALU.mult), vec_ready)

        def col(name, i=0, p0=0, p1=128):
            c = VEC[name] + i
            return vec[p0:p1, c:c + 1]

        class Stream:
            def __init__(self, name, chunks, guard, split_guard, ahead=6):
                self.chunks, self.sems = chunks, [count(f"s_{name}{i}") for i in range(6)]
                self.raw_free = [list(guard) for _ in range(6)]
                self.split_free = [list(split_guard) for _ in range(3)]
                self.loaded, self.ready, self.done_load, self.done_split = {}, {}, 0, 0
                for _ in range(ahead):
                    self.load()

            def load(self):
                c = self.done_load
                if c >= len(self.chunks):
                    return
                ap, kt, m = self.chunks[c]
                self.loaded[c] = self.sems[c % 6].load(
                    Y, lambda e: e.dma_start(raw[c % 6][:, 0:kt * m], ap), self.raw_free[c % 6])
                self.done_load += 1

            def split_to(self, last):
                while self.done_split <= min(last, len(self.chunks) - 1):
                    c = self.done_split
                    _, kt, m = self.chunks[c]
                    r, h, lo = raw[c % 6][:, 0:kt * m], whi[c % 3][:, 0:kt * m], wlo[c % 3][:, 0:kt * m]
                    th = S.do(lambda e, r=r, h=h: e.copy(h, r), self.loaded[c], self.split_free[c % 3])
                    tl = V.do(lambda e, r=r, h=h, lo=lo: e.tensor_tensor(lo, r, h.bitcast(F), ALU.subtract),
                              th, self.loaded[c], self.split_free[c % 3])
                    self.ready[c] = [th, tl]
                    self.raw_free[c % 6] = [th, tl]
                    self.done_split += 1
                    self.load()

            def used(self, c, token):
                self.split_free[c % 3] = [token]

        class Group:

            def __init__(self, stream, n, tiles, pool):
                self.stream, self.tiles, self.k = stream, tiles, 0
                self.chunks = [nxt() for _ in range(n)]
                self.outs = [banks[b] for b in pool[:n]]
                bank_turn[0] = n
                stream.split_to(self.chunks[0] + 2)

            def to(self, end):
                last_k = len(self.tiles) - 1
                toks = []
                while self.k < end:
                    k = self.k
                    hi, lo, tok = self.tiles[k]
                    P.wait(tok)
                    for out, c in zip(self.outs, self.chunks):
                        if k == 0:
                            P.wait(self.stream.ready[c], out.free)
                        wh = whi[c % 3][:, k * 128:(k + 1) * 128]
                        wl = wlo[c % 3][:, k * 128:(k + 1) * 128]
                        for n, (w, x) in enumerate(((wh, hi), (wh, lo), (wl, hi))):
                            first, last = k == 0 and n == 0, k == last_k and n == 2
                            fn = lambda e: e.matmul(out.ap[:, :], w, x, start=first, stop=last)
                            if last:
                                toks.append(P.do(fn))
                                self.stream.used(c, toks[-1])
                                self.stream.split_to(c + 3)
                            else:
                                P.plain(fn)
                    self.k += 1
                return list(zip(self.outs, toks))

        bank_turn = [0]
        pend = []

        def later(fn, n=1):
            pend.append([n, fn])

        def tick():
            due = []
            for p in pend:
                p[0] -= 1
                if p[0] <= 0:
                    due.append(p)
            for p in due:
                pend.remove(p)
                p[1]()

        def flush():
            while pend:
                tick()

        def gemm(stream, parts, pool, m=128):
            bank = banks[pool[bank_turn[0] % len(pool)]]
            bank_turn[0] += 1
            out = bank.ap[0:m, :]
            P.wait(bank.free)
            total = sum(len(tiles) for _, tiles in parts) * 3
            n = 0
            for c, tiles in parts:
                stream.split_to(c)
                P.wait(stream.ready[c])
                for k, (hi, lo, tok) in enumerate(tiles):
                    P.wait(tok)
                    wh = whi[c % 3][:, k * m:(k + 1) * m]
                    wl = wlo[c % 3][:, k * m:(k + 1) * m]
                    for w, x in ((wh, hi), (wh, lo), (wl, hi)):
                        fn = lambda e, w=w, x=x, n=n: e.matmul(out, w, x, start=(n == 0), stop=(n == total - 1))
                        n += 1
                        if k == len(tiles) - 1 and w is wl:
                            tok = P.do(fn)
                        else:
                            P.plain(fn)
                stream.used(c, tok)
                stream.split_to(c + 2)
            tick()
            return bank, tok

        def newton(total, n, y2, y, out, *tokens):
            t = V.do(lambda e: e.scalar_tensor_tensor(y2[:, :], total[:, :], n * EPS, y2[:, :], ALU.add, ALU.mult),
                     *tokens)
            t = V.do(lambda e: e.tensor_scalar(y2[:, :], y2[:, :], -0.5 / n, 1.5, ALU.mult, ALU.add), t)
            return V.do(lambda e: e.tensor_tensor(out[:, :], y[:, :], y2[:, :], ALU.mult), t)

        sq_free = [[], []]

        class Norm:

            def __init__(self, Hn, gname, acc_free=()):
                self.H, self.g, self.tok = Hn, gname, {}
                self.acc_tok = list(acc_free)

            def tile(self, i, xtok, free, split=True, f32=None):
                self.scale(i, xtok, free, split, f32)
                self.square(i, xtok)

            def scale(self, i, xtok, free, split=True, f32=None):
                if split:
                    hi, lo = self.H[:, 0, i, :], self.H[:, 1, i, :]
                    th = S.do(lambda e: e.activation(hi, X[:, i, :], ACT.Identity, bias=0.0, scale=col(self.g, i)),
                              xtok, free, vec_ready)
                    tl = V.do(lambda e: e.scalar_tensor_tensor(lo, X[:, i, :], col(self.g, i), hi.bitcast(F),
                                                               ALU.mult, ALU.subtract), th, xtok, free)
                    self.tok[i] = [th, tl]
                elif f32 is not None:
                    self.tok[i] = [S.do(lambda e: e.activation(f32[:, i, :], X[:, i, :], ACT.Identity, bias=0.0,
                                                               scale=col(self.g, i)), xtok, free)]

            def square(self, i, xtok):
                if i == 0:
                    self.acc_tok = [S.do(lambda e: e.activation(acc[:, :], X[:, i, :], ACT.Square),
                                         xtok, self.acc_tok)]
                else:
                    q = tm[i % 2]
                    ts = S.do(lambda e: e.activation(q[:, :], X[:, i, :], ACT.Square), xtok, sq_free[i % 2])
                    self.acc_tok = [V.do(lambda e: e.tensor_tensor(acc[:, :], acc[:, :], q[:, :], ALU.add),
                                         ts, self.acc_tok)]
                    sq_free[i % 2] = list(self.acc_tok)

            def tiles(self):
                return [(self.H[:, 0, i, :], self.H[:, 1, i, :], self.tok[i]) for i in range(8)]

            def finish(self, bank, rfree, fine=False):
                tp = P.do(lambda e: e.matmul(bank.ap[:, :], ones[:, :], acc[:, :], start=True, stop=True),
                          self.acc_tok, bank.free, c_ready)
                self.acc_read = [tp]
                t = S.do(lambda e: e.activation(rbc[:, :], bank.ap[:, :], ACT.Ln, bias=col("eps"), scale=1.0 / D),
                         tp, rfree)
                bank.free = [t]
                self.r = [S.do(lambda e: e.activation(rbc[:, :], rbc[:, :], ACT.Exp, scale=-0.5), t)]
                if fine:
                    t = S.do(lambda e: e.activation(acc[:, :], rbc[:, :], ACT.Square), self.r, tp)
                    self.r = [newton(bank.ap, D, acc, rbc, rbc, t, self.r, tp)]
                    bank.free = self.acc_read = list(self.r)

        def table(name, *tokens):
            S.plain(lambda e: e.preload_act_table_set(name), *tokens)

        def transpose(out, in_, idn):
            return lambda e: e.transpose(out, in_, idn)

        def attention(pairs, PT, Pb, scale, pt_free, p_free, head=None, tail=None, between=None, OB=(5, 6)):
            units = []
            for pi, pr in enumerate(pairs):
                for hd in range(2):
                    for b in range(4):
                        units.append((pi, hd, b))
            n = len(units)
            state = {}
            pt_ready = {}
            pfree = [list(p_free) for _ in Pb]
            ptfree = [list(pt_free), list(pt_free)]
            LAG = 4
            VALUES = {2: (0,), 4: (1,), 5: (2,), 7: (3,)}
            sfree = [[] for _ in st]
            SB, TB = [0, 1, 2], [3, 4, 7]
            NS = len(st)

            def scores(u):
                pi, hd, b = units[u]
                pr = pairs[pi]
                lo, hi = pr["kbs"][b]
                nk = (hi - lo) * 128
                bank = banks[SB[u % len(SB)]]
                q, k = pr["q"](hd, b), pr["k"](hd, lo, hi)
                ts = P.do(lambda e: e.matmul(bank.ap[:, 0:nk], q, k, start=True, stop=True),
                          bank.free, pr["ready"](hd, b))
                pb, s = Pb[u % len(Pb)], st[u % NS]
                if pr["mask"]:
                    m = pr["mask"](hd, b)
                    tv = V.do(lambda e: e.tensor_tensor_reduce(out=pb[:, 0:nk], in0=bank.ap[:, 0:nk], in1=m,
                                                               scale=1.0, scalar=-3e38, op0=ALU.add, op1=ALU.max,
                                                               accum_out=s[:, 0:1]),
                              ts, pfree[u % len(Pb)], sfree[u % NS],
                              pr["mask_ready"](hd) if callable(pr["mask_ready"]) else pr["mask_ready"])
                    bank.free = [tv]
                    pr["mask_used"](hd, b, tv)
                    src = pb
                else:
                    tv = V.do(lambda e: e.tensor_reduce(s[:, 0:1], bank.ap[:, 0:nk], AX, ALU.max),
                              ts, sfree[u % NS])
                    src = bank.ap
                if pr["sink"] is not None:
                    ns, sk = pr["sink"](hd)
                    tn = V.do(lambda e: e.tensor_scalar(s[:, 1:2], s[:, 0:1], -scale, ns, ALU.mult, ALU.min), tv)
                else:
                    tn = V.do(lambda e: e.tensor_scalar(s[:, 1:2], s[:, 0:1], -scale, None, ALU.mult), tv)
                te = S.do(lambda e: e.activation(pb[:, 0:nk], src[:, 0:nk], ACT.Exp, bias=s[:, 1:2], scale=scale,
                                                 accum_out=s[:, 2:3]), tn, tv, ts, pfree[u % len(Pb)])
                if not pr["mask"]:
                    bank.free = [te]
                toks = [te]
                if pr["sink"] is not None:
                    toks.append(S.do(lambda e: e.activation(s[:, 3:4], s[:, 1:2], ACT.Exp, bias=sk, scale=1.0), tn))
                state[u] = toks

            def norm(u):
                pi, hd, b = units[u]
                lo, hi = pairs[pi]["kbs"][b]
                nk = (hi - lo) * 128
                pb, s = Pb[u % len(Pb)], st[u % NS]
                t = state[u]
                if pairs[pi]["sink"] is not None:
                    t = [V.do(lambda e: e.tensor_tensor(s[:, 2:3], s[:, 2:3], s[:, 3:4], ALU.add), t)]
                tr = V.do(lambda e: e.reciprocal(s[:, 4:5], s[:, 2:3]), t)
                tg = G.do(lambda e: e.tensor_scalar(pb[:, 0:nk], pb[:, 0:nk], s[:, 4:5], 1.0, ALU.mult, ALU.mult),
                          tr, state[u])
                sfree[u % NS] = [tg]
                state[u] = [tg]

            def turn(u):
                pi, hd, b = units[u]
                lo, hi = pairs[pi]["kbs"][b]
                pb = Pb[u % len(Pb)]
                bank = banks[TB[u % len(TB)]]
                P.wait(state[u], bank.free)
                for j in range(hi - lo):
                    fn = transpose(bank.ap[:, j * 128:(j + 1) * 128], pb[:, j * 128:(j + 1) * 128], ident[:, :])
                    if j == hi - lo - 1:
                        tt = P.do(fn)
                    else:
                        P.plain(fn)
                pfree[u % len(Pb)] = [tt]
                dst = PT[pi % 2][hd][:, lo:hi, b * 128:(b + 1) * 128]
                srcb = bank.ap[:, 0:(hi - lo) * 128].rearrange("p (k q) -> p k q", q=128)
                if u % 2:
                    tc = S.do(lambda e: e.copy(dst, srcb), tt, ptfree[pi % 2])
                else:
                    tc = V.do(lambda e: e.tensor_copy(dst, srcb), tt, ptfree[pi % 2])
                bank.free = [tc]
                pt_ready.setdefault(pi, []).append(tc)

            def values(pi, part):
                pr = pairs[pi]
                bank = banks[OB[pi % len(OB)]]
                if 0 in part:
                    P.wait(bank.free, pt_ready[pi], pr["v_ready"]())
                full = all(k == (0, 4) for k in pr["kbs"])
                for kb in part:
                    qs = [b for b in range(4) if pr["kbs"][b][0] <= kb < pr["kbs"][b][1]]
                    q0, q1 = qs[0] * 128, (qs[-1] + 1) * 128
                    for hd in range(2):
                        fn = lambda e, kb=kb, hd=hd, q0=q0, q1=q1: e.matmul(
                            bank.ap[64 * hd:64 * hd + 64, q0:q1], pr["v"](kb, hd), PT[pi % 2][hd][:, kb, q0:q1],
                            start=(kb == 0), stop=(kb == 3), skip_group_check=not full)
                        if kb == 3 and hd == 1:
                            to = P.do(fn)
                        else:
                            P.plain(fn)
                if 3 in part:
                    ptfree[pi % 2] = [to]
                    bank.free = pr["out"](bank, to)

            for t in range(n + LAG):
                if t < n:
                    scores(t)
                if between and t in between:
                    between[t]()
                if 1 <= t <= n:
                    norm(t - 1)
                u = t - LAG
                if t == 2 and head:
                    ptfree[0].extend(head() or [])
                    ptfree[1].extend(ptfree[0])
                if u >= 0:
                    turn(u)
                    if u % 8 in VALUES and u > 7:
                        values(u // 8 - 1, VALUES[u % 8])
            if tail:
                tail()
            values(len(pairs) - 1, range(4))

        W1 = []
        for i in range(6):
            W1.append((A["w1_in"][i], 8, 128))
        for i in range(12):
            W1.append((A["w1_conv"][i], 8, 128))
        for i in range(8):
            W1 += [(A["w1_ga"][i], 8, 128), (A["w1_gc"][i], 8, 128), (A["w1_ap"][i], 4, 128), (A["w1_cp"][i], 4, 128)]
        for i in range(8):
            W1.append((A["w1_out"][i], 8, 128))

        load_x(0)
        stream = Stream("a", W1, [], [], 1)
        for i in range(1, 8):
            load_x(i)
            if i % 3 == 0:
                stream.load()
        for sb_, name in consts:
            src = A[name]
            if name == "w_router":
                src = src.rearrange("p (k n) -> p k n", n=36)
            c_ready = c_const.load(Y, lambda e, a=sb_, b=src: e.dma_start(a[:], b))
        for i in range(3):
            stream.load()
        cur = [0]

        def nxt():
            cur[0] += 1
            return cur[0] - 1

        c_t = count("s_tabs")
        ropeF = at("ropeF", [128, 2, T], F, 156)
        maskF = at("maskF", [128, 384], F, 160)
        zero = at("zero", [128, 1024], F, 200)
        t_tab = c_t.load(Y, lambda e: e.dma_start(ropeF[:, :, :], A["c_ropeF"].rearrange("p (a t) -> p a t", a=2)))
        t_tab = c_t.load(Y, lambda e: e.dma_start(maskF[:, :], A["c_maskF"]))

        c_zero = count("s_zero")
        t_z = G.do(lambda e: e.memset(zero[:, :], 0.0))

        def zero_rows(i):
            return c_zero.load(Y, lambda e: e.dma_start(A["hbuf"][i * 128:(i + 1) * 128, :], zero[:, :]), t_z)

        G8 = [0, 1, 2, 3]
        table("natural_log_exp_and_others")
        n1 = Norm(H[0], "g1")
        for i in range(8):
            n1.scale(i, x_load[i], [])
            if i in (0, 3, 6):
                stream.split_to(i // 3)
        for i in range(8):
            n1.square(i, x_load[i])
        first = Group(stream, 2, n1.tiles(), G8).to(8)
        first.append(gemm(stream, [(nxt(), n1.tiles())], G8))
        n1.finish(banks[7], [])

        qF = at("qF", [128, 4, T], F, 144)
        kF = at("kF", [128, T], F, 152)
        vF = at("vF", [128, 4, 128], F, 154)
        qz = [at(f"qz{i}", [128, T], F, 188 + 2 * i) for i in range(2)]
        qs = [at(f"qs{i}", [128, T], F, 192 + 2 * i) for i in range(2)]
        qn = [at(f"qn{i}", [128, T], F, 196 + 2 * i) for i in range(2)]

        def head_norm_rope(i, bank, tok, r, g, perm, rope, dst, fr, extra, Z, done, fine=False):
            z, s, m = Z[0][i % 2], Z[1][i % 2], Z[2][i % 2]
            f = fr.setdefault(i % 2, [])
            t1 = V.do(lambda e: e.tensor_tensor(z[:, :], bank.ap[:, :], r[:, :], ALU.mult), tok, extra, f)
            bank.free = [t1]
            t2 = S.do(lambda e: e.activation(s[:, :], z[:, :], ACT.Square), t1, f)

            def norm():
                b2 = banks[4 + i % 2]
                t3 = P.do(lambda e: e.matmul(b2.ap[:, :], bones[:, :], s[:, :], start=True, stop=True), t2, b2.free,
                          c_ready)
                t4 = S.do(lambda e: e.activation(s[:, :], b2.ap[:, :], ACT.Ln, bias=col("eps"), scale=1.0 / 64), t3)
                b2.free = [t4]
                t5 = S.do(lambda e: e.activation(s[:, :], s[:, :], ACT.Exp, scale=-0.5), t4)
                if fine:
                    t = S.do(lambda e: e.activation(m[:, :], s[:, :], ACT.Square), t5, f)
                    t5 = newton(b2.ap, 64, m, s, s, t, t5, t3)
                    b2.free = [t5]
                t6 = V.do(lambda e: e.scalar_tensor_tensor(m[:, :], z[:, :], g, s[:, :], ALU.mult, ALU.mult),
                          t5, t1, f)
                later(lambda: turned(t6))

            def turned(t6):
                done(rope_only(i, m, t6, perm, rope, dst, fr, extra, z, s))

            later(norm)

        def rope_only(i, m, t6, perm, rope, dst, fr, extra, z, s):
            b3 = banks[6 + i % 2]
            t7 = P.do(lambda e: e.matmul(b3.ap[:, :], perm[:, :], m[:, :], start=True, stop=True), t6, b3.free)
            t8 = G.do(lambda e: e.tensor_tensor(z[:, :], m[:, :], rope[0], ALU.mult), t6, extra)
            t9 = V.do(lambda e: e.tensor_tensor(s[:, :], b3.ap[:, :], rope[1], ALU.mult), t7, t6, extra)
            b3.free = [t9]
            t10 = V.do(lambda e: e.tensor_tensor(dst, z[:, :], s[:, :], ALU.add), t8, t9, extra)
            fr[i % 2] = [t10, t7]
            return [t10]

        fr = {}
        qk_ready = {}
        rX = [n1.r, t_tab]

        ZF = (qz, qs, qn)
        ropeF = (ropeF[:, 0, :], ropeF[:, 1, :])
        for i in range(6):
            bank, tok = first[i]
            if i < 5:
                dst, g = (qF[:, i, :], "qg") if i < 4 else (kF[:, :], "kg")
                head_norm_rope(i, bank, tok, rbc, col(g), permF, ropeF, dst, fr, rX, ZF,
                               lambda t, i=i: qk_ready.update({i if i < 4 else "k": t}))
            else:
                z = qz[i % 2]
                t1 = V.do(lambda e: e.tensor_tensor(z[:, :], bank.ap[:, :], rbc[:, :], ALU.mult), tok, rX,
                          fr.get(i % 2))
                bank.free = [t1]

                def w(i=i, z=z, t1=t1):
                    b2 = banks[4 + i % 2]
                    P.wait(t1, b2.free)
                    for b in range(4):
                        f = transpose(b2.ap[:, b * 128:(b + 1) * 128], z[:, b * 128:(b + 1) * 128], ident[:, :])
                        if b < 3:
                            P.plain(f)
                        else:
                            t2 = P.do(f)
                    t3 = V.do(lambda e: e.tensor_copy(vF[:, :, :], b2.ap[:, :].rearrange("p (a b) -> p a b", b=128)), t2)
                    b2.free = [t3]
                    qk_ready["v"] = [t3]
                later(w)
            if i < 5:
                first.append(gemm(stream, [(nxt(), n1.tiles())], G8))

        upad = [at(f"upad{i}", [128, T + 2], F, 183 + 2.25 * i) for i in range(2)]
        cf = [at(f"cf{i}", [128, T], F, 162 + 2 * i) for i in range(6)]
        t_pad = []
        for i in range(2):
            t_pad.append(V.do(lambda e, i=i: e.memset(upad[i][:, 0:1], 0.0)))
            t_pad.append(V.do(lambda e, i=i: e.memset(upad[i][:, T + 1:T + 2], 0.0)))
        H1 = H[1][:, :, :, :].rearrange("p a k t -> p (a k) t")
        attn_hi, attn_lo = (lambda i: H1[:, i, :]), (lambda i: H1[:, 4 + i, :])
        conv_hi, conv_lo = (lambda i: H1[:, 8 + i, :]), (lambda i: H1[:, 12 + i, :])
        conv_tok, cfree = {}, [[], []]
        for i in range(4):
            bc = first[6] if i == 0 else gemm(stream, [(nxt(), n1.tiles())], G8)
            for j in range(4):
                zeroed = zero_rows(4 * i + j)
            bx = first[7] if i == 0 else gemm(stream, [(nxt(), n1.tiles())], G8)
            bb = gemm(stream, [(nxt(), n1.tiles())], G8)
            u, (ta, tb, tc) = upad[i % 2], cf[3 * (i % 2):3 * (i % 2) + 3]
            f = cfree[i % 2]
            a1 = V.do(lambda e: e.tensor_tensor(ta[:, :], bc[0].ap[:, :], rbc[:, :], ALU.mult), bc[1], n1.r, f)
            bc[0].free = [a1]
            a2 = V.do(lambda e: e.tensor_tensor(tb[:, :], bx[0].ap[:, :], rbc[:, :], ALU.mult), bx[1], f)
            bx[0].free = [a2]
            a3 = V.do(lambda e: e.tensor_tensor(u[:, 1:T + 1], ta[:, :], tb[:, :], ALU.mult), a1, a2, t_pad, f)
            a4 = S.do(lambda e: e.activation(tc[:, :], u[:, 1:T + 1], ACT.Identity, bias=col("cvb", i),
                                             scale=col("cv1", i)), a3, f)
            a5 = V.do(lambda e: e.scalar_tensor_tensor(ta[:, :], u[:, 0:T], col("cv0", i), tc[:, :],
                                                       ALU.mult, ALU.add), a4, a3)
            a6 = V.do(lambda e: e.scalar_tensor_tensor(tb[:, :], u[:, 2:T + 2], col("cv2", i), ta[:, :],
                                                       ALU.mult, ALU.add), a5)
            a7 = V.do(lambda e: e.tensor_tensor(tc[:, :], bb[0].ap[:, :], rbc[:, :], ALU.mult), bb[1], a5)
            bb[0].free = [a7]
            a8 = V.do(lambda e: e.tensor_tensor(ta[:, :], tc[:, :], tb[:, :], ALU.mult), a6, a7)
            a9 = S.do(lambda e: e.copy(conv_hi(i), ta[:, :]), a8)
            a10 = V.do(lambda e: e.tensor_tensor(conv_lo(i), ta[:, :], conv_hi(i).bitcast(F), ALU.subtract), a9)
            cfree[i % 2] = [a10]
            conv_tok[i] = [a9, a10]

        PTF = [[at("PTF0", [128, 4, T], F, 162), at("PTF1", [128, 4, T], F, 170)],
               [at("PTF2", [128, 4, T], F, 178), at("PTF3", [128, 4, T], F, 194)]]
        PbF = [at(f"PbF{i}", [128, 384], F, 186 + 1.5 * i) for i in range(5)]
        flush()
        before = [(V.sem, V.n), (S.sem, S.n), (G.sem, G.n), (P.sem, P.n), zeroed]
        attn_tok = {}

        def split_out(hi, lo, view=None):
            def out(bank, to):
                src = view(bank.ap) if view else bank.ap[:, :]
                a = S.do(lambda e: e.copy(hi, src), to)
                b = V.do(lambda e: e.tensor_tensor(lo, src, hi.bitcast(F), ALU.subtract), a, to)
                return [a, b]
            return out

        KBS = [(0, 2), (0, 3), (1, 4), (2, 4)]
        early = {}

        def first_gate():
            early[0] = gemm(stream, [(nxt(), n1.tiles())], [6])

        def second_gate():
            early[1] = gemm(stream, [(nxt(), n1.tiles())], [0])

        prs = []
        for i in range(4):
            def out(bank, to, i=i):
                attn_tok[i] = split_out(attn_hi(i), attn_lo(i))(bank, to)
                return attn_tok[i]

            prs.append(dict(
                q=lambda hd, b, i=i: qF[64 * hd:64 * hd + 64, i, b * 128:(b + 1) * 128],
                k=lambda hd, lo, hi: kF[64 * hd:64 * hd + 64, lo * 128:hi * 128],
                kbs=KBS, ready=lambda hd, b, i=i: [qk_ready[i], qk_ready["k"]],
                mask=lambda hd, b: maskF[:, 128 if b == 0 else 0:256 if b == 3 else 384],
                mask_ready=[t_tab, t_ns], mask_used=lambda *a: None,
                sink=lambda hd, i=i: (nsink[:, i + 4 * hd:i + 4 * hd + 1], col("sink", i + 4 * hd)),
                v=lambda kb, hd: vF[:, kb, 64 * hd:64 * hd + 64], v_ready=lambda: qk_ready["v"], out=out))
        attention(prs, PTF, PbF, 0.125, before, before, head=first_gate, tail=second_gate, OB=(5,))

        table("sigmoid_and_others")
        M1 = at("M1", [128, 2, 8, T], R, 144)
        gm = [at(f"gm{i}", [128, T], F, 176 + 2 * i) for i in range(8)]
        before = [(V.sem, V.n), (S.sem, S.n), (G.sem, G.n), (P.sem, P.n)]
        gfree = [list(before), list(before)]
        merged = {}
        at_tiles = [(attn_hi(k), attn_lo(k), attn_tok[k]) for k in range(4)]
        cv_tiles = [(conv_hi(k), conv_lo(k), conv_tok[k]) for k in range(4)]
        AB = [0, 1, 2, 3, 4, 5, 6, 7]
        for i in range(8):
            if i == 0:
                ga, gc = early[0], early[1]
                bank_turn[0] = 1
            else:
                ga = gemm(stream, [(nxt(), n1.tiles())], AB)
                gc = gemm(stream, [(nxt(), n1.tiles())], AB)
            ap = gemm(stream, [(nxt(), at_tiles)], AB)
            cp = gemm(stream, [(nxt(), cv_tiles)], AB)
            a, b, c, d = gm[4 * (i % 2):4 * (i % 2) + 4]
            f = gfree[i % 2]
            t1 = V.do(lambda e: e.tensor_tensor(a[:, :], ga[0].ap[:, :], rbc[:, :], ALU.mult), ga[1], f)
            ga[0].free = [t1]
            t2 = S.do(lambda e: e.activation(a[:, :], a[:, :], ACT.Sigmoid), t1)
            t3 = V.do(lambda e: e.tensor_tensor(b[:, :], a[:, :], ap[0].ap[:, :], ALU.mult), t2, ap[1], f)
            ap[0].free = [t3]
            t4 = V.do(lambda e: e.tensor_tensor(c[:, :], gc[0].ap[:, :], rbc[:, :], ALU.mult), gc[1], f)
            gc[0].free = [t4]
            t5 = S.do(lambda e: e.activation(c[:, :], c[:, :], ACT.Sigmoid), t4)
            t6 = V.do(lambda e: e.tensor_tensor(d[:, :], c[:, :], cp[0].ap[:, :], ALU.mult), t5, cp[1], f)
            cp[0].free = [t6]
            t7 = V.do(lambda e: e.tensor_tensor(b[:, :], b[:, :], d[:, :], ALU.add), t3, t6)
            t8 = S.do(lambda e: e.copy(M1[:, 0, i, :], b[:, :]), t7, before)
            t9 = V.do(lambda e: e.tensor_tensor(M1[:, 1, i, :], b[:, :], M1[:, 0, i, :].bitcast(F), ALU.subtract),
                      t8, before)
            gfree[i % 2] = [t9]
            merged[i] = [t8, t9]
        table("natural_log_exp_and_others")
        r_read = [(V.sem, V.n)]

        XG = at("XG", [128, 8, T], F, 176)
        m_tiles = [(M1[:, 0, k, :], M1[:, 1, k, :], merged[k]) for k in range(8)]
        n2 = Norm(None, "g2", n1.acc_read)
        lg = banks[7]
        h_dead = [(P.sem, P.n)]
        gates_done = [(V.sem, V.n), (S.sem, S.n)]

        GU = [[at("GU00", [128, 8, 512], F, 16), at("GU01", [128, 8, 512], F, 32)],
              [at("GU10", [128, 8, 512], F, 64), at("GU11", [128, 8, 512], F, 80)],
              [at("GU20", [128, 8, 512], F, 112), at("GU21", [128, 8, 512], F, 144)]]
        DN = [[at("DN00", [128, 2, 1024], F, 48), at("DN01", [128, 2, 1024], F, 56)],
              [at("DN10", [128, 2, 1024], F, 96), at("DN11", [128, 2, 1024], F, 104)],
              [at("DN20", [128, 2, 1024], F, 192), at("DN21", [128, 2, 1024], F, 168)]]
        c_gu = [count(f"s_gu{i}") for i in range(3)]
        c_dn = [count(f"s_dn{i}") for i in range(3)]
        gu_at, dn_at = {}, {}

        def load_gu(p, j, *tokens):
            s = p % 3
            gu_at[p] = c_gu[s].load(Y, lambda e: e.dma_start(
                GU[s][j][:, :, :], A["w_gu"][2 * p + j].rearrange("p (k n) -> p k n", n=512)), *tokens)

        def load_dn(p, j, *tokens):
            s = p % 3
            dn_at[p] = c_dn[s].load(Y, lambda e: e.dma_start(
                DN[s][j][:, :, :], A["w_dn"][2 * p + j].rearrange("p (k n) -> p k n", n=1024)), *tokens)

        def load_pair(p, *tokens):
            for load in (load_gu, load_dn):
                for j in range(2):
                    load(p, j, *tokens)

        def logits(k):
            P.wait(lg.free, n2.tok[k], c_ready)
            fn = lambda e: e.matmul(lg.ap[0:36, :], wr[:, k, :], XG[:, k, :], start=(k == 0), stop=(k == 7))
            if k == 7:
                return P.do(fn)
            P.plain(fn)

        start = Group(stream, 2, m_tiles, G8).to(8)
        for i in range(8):
            bank, tok = start[i] if i < 2 else gemm(stream, [(nxt(), m_tiles)], G8)
            if i == 0:
                load_pair(0, h_dead)
                load_gu(1, 0, h_dead)
                load_dn(2, 0, gates_done)
            if i >= 2:
                logits(i - 2)
            xt = V.do(lambda e: e.tensor_tensor(X[:, i, :], X[:, i, :], bank.ap[:, :], ALU.add), tok, x_load)
            bank.free = [xt]
            n2.tile(i, [xt], gates_done, split=False, f32=XG)
        logits(6)
        t_lg = logits(7)
        w_done = [(P.sem, P.n)]
        ring_done = [w_done, (V.sem, V.n), (S.sem, S.n)]
        load_gu(1, 1, stream.raw_free[0:4])
        load_dn(1, 0, stream.raw_free[4:6])
        load_dn(1, 1, ring_done)
        for j in range(2):
            load_gu(2, j, ring_done)
        rc = keep[:, 0:4]
        sc = banks[4]
        P.wait(sc.free, n2.acc_tok)
        for b in range(4):
            fn = lambda e, b=b: e.matmul(sc.ap[:, b:b + 1], acc[:, b * 128:(b + 1) * 128], ones[:, 0:1],
                                         start=True, stop=True)
            if b < 3:
                P.plain(fn)
            else:
                ts = P.do(fn)
        t1 = S.do(lambda e: e.activation(rc, sc.ap[:, 0:4], ACT.Ln, bias=col("eps"), scale=1.0 / D), ts)
        sc.free = [t1]
        t_rc = S.do(lambda e: e.activation(rc, rc, ACT.Exp, scale=-0.5), t1)
        n2.finish(banks[5], r_read)
        n2r = n2.r

        lgs = at("lgs", [36, T], F, 200)
        t1 = V.do(lambda e: e.tensor_copy(lgs[:, :], lg.ap[0:36, :]), t_lg, gates_done)
        lg.free = [t1]
        lb = banks[6]
        P.wait(t1, lb.free)
        for b in range(4):
            fn = transpose(lb.ap[:, b * 36:(b + 1) * 36], lgs[:, b * 128:(b + 1) * 128], ident[0:36, 0:36])
            if b < 3:
                P.plain(fn)
            else:
                t_lt = P.do(fn)

        rows = [at(f"rows{b}", [128, D], F, 160 + 4 * b) for b in range(4)]
        row_tok = {b: [] for b in range(4)}
        n = 0
        for b in range(4):
            for hf in range(2):
                bank = banks[n % 4]
                P.wait(bank.free, n2.tok[7])
                for k in range(4):
                    fn = transpose(bank.ap[:, k * 128:(k + 1) * 128], XG[:, 4 * hf + k, b * 128:(b + 1) * 128],
                                   ident[:, :])
                    if k < 3:
                        P.plain(fn)
                    else:
                        t1 = P.do(fn)
                dst = rows[b][:, hf * 512:(hf + 1) * 512]
                t2 = S.do(lambda e: e.activation(dst, bank.ap[:, :], ACT.Copy, bias=0.0, scale=rc[:, b:b + 1]),
                          t1, t_rc, w_done)
                bank.free = [t2]
                row_tok[b].append(t2)
                n += 1

        off = [202.0]

        def small(name, *shape):
            n = int(np.prod(shape))
            t = at(name, [128] + list(shape), F, off[0])
            off[0] += max(n * 4, 32) / 1024
            return t

        L = small("L", 4, 36)
        last = None
        for b in range(4):
            last = V.do(lambda e: e.scalar_tensor_tensor(L[:, b, :], lb.ap[:, b * 36:(b + 1) * 36], rc[:, b:b + 1],
                                                         bro[:, :], ALU.mult, ALU.add), t_lt, t_rc, c_ready)
        lb.free = [last]
        GL = L[:, :, 0:4]
        EL = L[:, :, 4:36].rearrange("p t (g e) -> p t g e", e=8)

        def v(fn, *tokens):
            return V.do(fn, (V.sem, V.n), *tokens)

        def first_max(vals, n, name):
            mx, df, ix, mi, oh = (small(name + c, 4, 1 if c in "mi" else n) for c in ("m", "d", "x", "i", "o"))
            v(lambda e: e.tensor_reduce(mx[:, :, :], vals, AX, ALU.max))
            v(lambda e: e.tensor_tensor(df[:, :, :], vals, mx[:, :, :].to_broadcast([128, 4, n]), ALU.is_ge))
            v(lambda e: e.scalar_tensor_tensor(ix[:, :, :], df[:, :, :], -100.0,
                                               io32[:, 0:n].unsqueeze(1).to_broadcast([128, 4, n]), ALU.mult, ALU.add))
            v(lambda e: e.tensor_reduce(mi[:, :, :], ix[:, :, :], AX, ALU.min))
            v(lambda e: e.tensor_tensor(oh[:, :, :], ix[:, :, :], mi[:, :, :].to_broadcast([128, 4, n]),
                                        ALU.is_equal))
            return mx, oh

        gmx, goh = first_max(GL, 4, "g")
        gd, gs, pg = small("gd", 4, 4), small("gs", 4, 1), small("pg", 4, 1)
        t1 = v(lambda e: e.tensor_tensor(gd[:, :, :], GL, gmx[:, :, :].to_broadcast([128, 4, 4]), ALU.subtract))
        t2 = S.do(lambda e: e.activation(gd[:, :, :], gd[:, :, :], ACT.Exp), t1)
        ei4, ein = small("ei4", 4, 4, 8), small("ein", 4, 8)
        v(lambda e: e.tensor_tensor(ei4[:, :, :, :], EL, goh[:, :, :].unsqueeze(3).to_broadcast([128, 4, 4, 8]),
                                    ALU.mult))
        v(lambda e: e.tensor_reduce(ein[:, :, :], ei4[:, :, :, :].rearrange("p t g e -> p t e g"), AX, ALU.add))
        v(lambda e: e.tensor_reduce(gs[:, :, :], gd[:, :, :], AX, ALU.add), t2)
        v(lambda e: e.reciprocal(pg[:, :, :], gs[:, :, :]))
        m1, o1 = first_max(ein[:, :, :], 8, "u")
        e2 = small("e2", 4, 8)
        v(lambda e: e.scalar_tensor_tensor(e2[:, :, :], o1[:, :, :], NEG, ein[:, :, :], ALU.mult, ALU.add))
        m2, o2 = first_max(e2[:, :, :], 8, "v")
        dd, ex = small("dd", 4, 1), small("ex", 4, 1)
        t1 = v(lambda e: e.tensor_tensor(dd[:, :, :], m2[:, :, :], m1[:, :, :], ALU.subtract))
        t2 = S.do(lambda e: e.activation(ex[:, :, :], dd[:, :, :], ACT.Exp), t1)
        AK, AS = small("AK", 2, 4, 32), small("AS", 4, 32)
        for k, o in ((0, o1), (1, o2)):
            v(lambda e: e.tensor_tensor(AK[:, k, :, :].rearrange("p t (g e) -> p t g e", e=8),
                                        goh[:, :, :].unsqueeze(3).to_broadcast([128, 4, 4, 8]),
                                        o[:, :, :].unsqueeze(2).to_broadcast([128, 4, 4, 8]), ALU.mult))
        t_as = v(lambda e: e.tensor_tensor(AS[:, :, :], AK[:, 0, :, :], AK[:, 1, :, :], ALU.add))
        rk = banks[6]
        P.wait(t_as, rk.free)
        for n in range(4):
            w = ones if n else triu
            fn = lambda e: e.matmul(rk.ap[:, 32 * n:128], w[:, :], AS[:, 0:4 - n, :].rearrange("p t n -> p (t n)"),
                                    start=(n == 0), stop=(n == 3), skip_group_check=True)
            if n < 3:
                P.plain(fn)
            else:
                t_rk = P.do(fn)
        tmp, rr, es, ok = small("tmp", 2, 4, 32), small("rr", 2, 4), small("es", 2, 4), small("ok", 2, 4)
        dn, gt, gov = small("dn", 4, 1), small("gt", 2, 4), small("gov", 2, 4)
        flag = small("flag", 8)
        v(lambda e: e.tensor_tensor(tmp[:, :, :, :].rearrange("p k t n -> p (k t) n"),
                                    AK[:, :, :, :].rearrange("p k t n -> p (k t) n"),
                                    io32[:, :].unsqueeze(1).to_broadcast([128, 8, 32]), ALU.mult))
        v(lambda e: e.tensor_reduce(es[:, :, :], tmp[:, :, :, :], AX, ALU.add))
        v(lambda e: e.tensor_scalar(dn[:, :, :], ex[:, :, :], 1.0, None, ALU.add), t2)
        v(lambda e: e.reciprocal(dn[:, :, :], dn[:, :, :]))
        v(lambda e: e.tensor_tensor(gt[:, 0, :], dn[:, :, 0], pg[:, :, 0], ALU.mult))
        v(lambda e: e.tensor_tensor(gt[:, 1, :], gt[:, 0, :], ex[:, :, 0], ALU.mult))
        v(lambda e: e.tensor_tensor(tmp[:, :, :, :], AK[:, :, :, :],
                                    rk.ap[:, 0:128].rearrange("p (t n) -> p t n", n=32).unsqueeze(1)
                                    .to_broadcast([128, 2, 4, 32]), ALU.mult), t_rk)
        rk.free = [(V.sem, V.n)]
        v(lambda e: e.tensor_reduce(rr[:, :, :], tmp[:, :, :, :], AX, ALU.add))
        v(lambda e: e.tensor_scalar(ok[:, :, :], rr[:, :, :], float(CAP), None, ALU.is_lt))
        v(lambda e: e.scalar_tensor_tensor(es[:, :, :], es[:, :, :], float(CAP), rr[:, :, :], ALU.mult, ALU.add))
        v(lambda e: e.scalar_tensor_tensor(rr[:, :, :], es[:, :, :], -4096.0, ok[:, :, :], ALU.add, ALU.mult))
        t_idx = v(lambda e: e.tensor_scalar(keepi[:, 0:8].rearrange("p (k t) -> p k t", t=4), rr[:, :, :], 4096.0, None,
                                            ALU.add))
        v(lambda e: e.tensor_tensor(keepi[:, 8:16].rearrange("p (k t) -> p k t", t=4), es[:, :, :], ok[:, :, :],
                                    ALU.mult))
        gk = keep[:, 4:12].rearrange("p (k t) -> p k t", t=4)
        v(lambda e: e.tensor_tensor(gk, gt[:, :, :], ok[:, :, :], ALU.mult))
        v(lambda e: e.tensor_tensor(gov[:, :, :], gt[:, :, :], gk, ALU.subtract))
        v(lambda e: e.tensor_scalar(flag[:, :].rearrange("p (k t) -> p k t", t=4), ok[:, :, :], -1.0, 1.0,
                                    ALU.mult, ALU.add))
        GO = at("GO", [128, 4, 32], F, 134.75)
        fl = at("fl", [128, 1], F, 135.25)
        fli = at("fli", [1, 1], I32, 135.375)
        v(lambda e: e.tensor_tensor(GO[:, :, :], AK[:, 0, :, :],
                                    gov[:, 0, :].unsqueeze(2).to_broadcast([128, 4, 32]), ALU.mult))
        v(lambda e: e.tensor_tensor(tmp[:, 0, :, :], AK[:, 1, :, :],
                                    gov[:, 1, :].unsqueeze(2).to_broadcast([128, 4, 32]), ALU.mult))
        v(lambda e: e.tensor_tensor(GO[:, :, :], GO[:, :, :], tmp[:, 0, :, :], ALU.add))
        t1 = v(lambda e: e.tensor_reduce(fl[:, :], flag[:, :], AX, ALU.add))
        t2 = P.do(lambda e: e.matmul(rk.ap[0:1, 0:1], fl[:, 0:1], ones[:, 0:1], start=True, stop=True), t1, rk.free)
        t_flag = v(lambda e: e.tensor_copy(fli[:, :], rk.ap[0:1, 0:1]), t2)
        rk.free = [t_flag]
        route_done = [(V.sem, V.n), (S.sem, S.n), (P.sem, P.n)]

        c_sc = count("s_scatter")
        for k in range(2):
            for b in range(4):
                t_sc = c_sc.load(G, lambda e, k=k, b=b: e.indirect_dma_start(
                    out=A["hbuf"], out_offset=bass.IndirectOffsetOnAxis(ap=keepi[:, 4 * k + b:4 * k + b + 1], axis=0),
                    in_=rows[b][:, :], in_offset=None, bounds_check=SLOTS - 1, oob_is_err=False),
                    t_idx, row_tok[b], zeroed)
        for q in (P, V, S, G, Y):
            q.wait(t_flag)
        left_over = nc.values_load(fli[0:1, 0:1], min_val=0, max_val=1024)

        hb = [[at(f"hb{i}{j}", [128, 512], F, k) for j, k in enumerate(ks)]
              for i, ks in enumerate(((200, 202), (164, 166), (204, 138)))]
        hT = at("hT", [128, 8, 128], F, 160)
        yb = at("yb", [128, D], F, 140)
        hid = at("hid", [128, 256], F, 206)
        hidT = at("hidT", [128, 2, 128], F, 133.5)
        c_hb, c_y = [count(f"s_hb{i}") for i in range(3)], count("s_y")
        table("silu_and_others")
        NP = NE // 2
        hb_free, hT_free, hT_tok, hb_at = [list(route_done) for _ in range(3)], list(route_done), {}, {}
        hid_free, hidT_free, yb_free = [list(route_done)], [list(route_done)], [list(route_done)]
        y_tok = None

        def load_rows(p):
            for j in range(2):
                hb_at[p] = c_hb[p % 3].load(Y, lambda e: e.dma_start(
                    hb[p % 3][j][:, :], A["hbuf"][p * 128:(p + 1) * 128, j * 512:(j + 1) * 512]), t_sc, hb_free[p % 3])

        def turn_rows(p):
            t = hb_at[p]
            toks = []
            for hf in range(2):
                bank = banks[hf]
                P.wait(bank.free, t)
                for k in range(4):
                    fn = transpose(bank.ap[:, k * 128:(k + 1) * 128],
                                   hb[p % 3][hf][:, k * 128:(k + 1) * 128], ident[:, :])
                    if k < 3:
                        P.plain(fn)
                    else:
                        t1 = P.do(fn)
                dst = hT[:, 4 * hf:4 * hf + 4, :]
                src = bank.ap[:, :].rearrange("p (k q) -> p k q", q=128)
                if hf:
                    t2 = V.do(lambda e: e.tensor_copy(dst, src), t1, hT_free)
                else:
                    t2 = S.do(lambda e: e.copy(dst, src), t1, hT_free)
                bank.free = [t2]
                toks.append(t2)
            hb_free[p % 3] = [t1]
            hT_tok[p] = toks

        load_rows(0)
        load_rows(1)
        load_rows(2)
        load_dn(2, 1, t_sc)
        W2 = []
        for i in range(6):
            W2.append((A["w2_in"][i], 8, 128))
        for i in range(5):
            W2.append((A["w2_c"][i], 8, 128))
        W2.append((A["w2_kr"][0], 8, 128))
        for i in range(8):
            W2.append((A["w2_uq"][i], 3, 128))
        for i in range(4):
            W2.append((A["w2_uk"][i], 2, 128))
        W2.append((A["w2_uv"], 2, 512))
        for i in range(8):
            W2.append((A["w2_evo"][i], 8, 128))

        def ffn_chunks(l):
            for q in range(4):
                for i in range(8):
                    W2.append((A[f"w_up{l}"][8 * q + i], 8, 128))
                for i in range(8):
                    W2.append((A[f"w_down{l}"][8 * q + i], 8, 128))

        ffn_chunks(0)
        for i in range(24):
            W2.append((A["w2_qkv"][i], 8, 128))
        for i in range(8):
            W2.append((A["w2_odo"][i], 8, 128))
        ffn_chunks(1)

        turn_rows(0)
        for p in range(NP):
            s = p % 3
            bank = banks[2 + p % 2]
            P.wait(bank.free, hT_tok[p], gu_at[p])
            for k in range(8):
                for j in range(2):
                    fn = lambda e, k=k, j=j: e.matmul(bank.ap[64 * j:64 * j + 64, :],
                                                      hT[:, k, 64 * j:64 * j + 64], GU[s][j][:, k, :],
                                                      start=(k == 0), stop=(k == 7))
                    if k == 7 and j == 1:
                        t1 = P.do(fn)
                    else:
                        P.plain(fn)
            hT_free = [t1]
            if p + 3 < NP:
                load_rows(p + 3)
            if p + 3 < NP:
                for j in range(2):
                    load_gu(p + 3, j, t1)
            t2 = S.do(lambda e: e.activation(hid[:, :], bank.ap[:, 0:256], ACT.Silu), t1, hid_free[0])
            t3 = V.do(lambda e: e.tensor_tensor(hid[:, :], hid[:, :], bank.ap[:, 256:512], ALU.mult), t2, t1)
            bank.free = [t3]
            if p + 1 < NP:
                turn_rows(p + 1)
            tb = banks[4]
            P.wait(t3, tb.free)
            P.plain(transpose(tb.ap[:, 0:128], hid[:, 0:128], ident[:, :]))
            t4 = P.do(transpose(tb.ap[:, 128:256], hid[:, 128:256], ident[:, :]))
            hid_free[0] = [t4]
            t5 = V.do(lambda e: e.tensor_copy(hidT[:, :, :], tb.ap[:, 0:256].rearrange("p (k q) -> p k q", q=128)),
                      t4, hidT_free[0])
            tb.free = [t5]
            toks = []
            for h2 in range(2):
                ob = banks[5 + h2]
                P.wait(t5, dn_at[p], ob.free)
                for k in range(2):
                    for j in range(2):
                        fn = lambda e, k=k, j=j, h2=h2, ob=ob: e.matmul(
                            ob.ap[64 * j:64 * j + 64, :], hidT[:, k, 64 * j:64 * j + 64],
                            DN[s][j][:, k, h2 * 512:(h2 + 1) * 512], start=(k == 0), stop=(k == 1))
                        if k == 1 and j == 1:
                            t6 = P.do(fn)
                        else:
                            P.plain(fn)
                dst = yb[:, h2 * 512:(h2 + 1) * 512]
                if h2:
                    t7 = V.do(lambda e: e.tensor_copy(dst, ob.ap[:, :]), t6, yb_free[0])
                else:
                    t7 = S.do(lambda e: e.copy(dst, ob.ap[:, :]), t6, yb_free[0])
                ob.free = [t7]
                toks.append(t7)
            hidT_free[0] = [t6]
            y_tok = c_y.load(Y, lambda e, p=p: e.dma_start(A["ybuf"][p * 128:(p + 1) * 128, :], yb[:, :]), toks)
            yb_free[0] = [y_tok]
            if p + 3 < NP:
                for j in range(2):
                    load_dn(p + 3, j, t6)
            if p == NP - 3:
                p13 = [t6]
                stream2 = Stream("b", W2, p13, [])
            if p == NP - 2:
                p14 = [t6]
                stream2.split_free = [list(p14) for _ in range(3)]
        moe_done = [t6]
        stream2.split_to(2)

        YG = [[at(f"YG{k}{b}", [128, D], F, 144 + 16 * k + 4 * b) for b in range(4)] for k in range(2)]
        c_yg = [count(f"s_yg{b}") for b in range(4)]
        table("natural_log_exp_and_others")
        cur[0] = 0
        c_t2 = count("s_tabs2")

        yg_tok = {}
        for b in range(4):
            for k in range(2):
                yg_tok[b] = c_yg[b].load(G, lambda e, k=k, b=b: e.indirect_dma_start(
                    out=YG[k][b][:, :], out_offset=None, in_=A["ybuf"],
                    in_offset=bass.IndirectOffsetOnAxis(ap=keepi[:, 8 + 4 * k + b:9 + 4 * k + b], axis=0),
                    bounds_check=SLOTS - 1, oob_is_err=False), y_tok, p14)
        n3 = Norm(H[0], "gm0", n2.acc_read)
        v_before = (V.sem, V.n)

        def weigh(b, hf):
            y0, y1 = (YG[k][b][:, hf * 512:(hf + 1) * 512] for k in range(2))
            t1 = S.do(lambda e: e.activation(y0, y0, ACT.Copy, bias=0.0, scale=keep[:, 4 + b:5 + b]),
                      yg_tok[b], v_before)
            return V.do(lambda e: e.scalar_tensor_tensor(y0, y1, keep[:, 8 + b:9 + b], y0, ALU.mult, ALU.add),
                        t1, v_before)

        parts_ = [(b, hf) for b in range(4) for hf in range(2)]
        y_sum = {parts_[0]: weigh(0, 0)}
        x_half = [[], []]
        for n, (b, hf) in enumerate(parts_):
            if n + 1 < 8:
                y_sum[parts_[n + 1]] = weigh(*parts_[n + 1])
            bank = banks[n % 8]
            P.wait(bank.free, y_sum[b, hf])
            for k in range(4):
                fn = transpose(bank.ap[:, k * 128:(k + 1) * 128],
                               YG[0][b][:, (4 * hf + k) * 128:(4 * hf + k + 1) * 128], ident[:, :])
                if k < 3:
                    P.plain(fn)
                else:
                    t3 = P.do(fn)
            xs = X[:, 4 * hf:4 * hf + 4, b * 128:(b + 1) * 128]
            x_half[hf] = [V.do(lambda e: e.tensor_tensor(xs, xs, bank.ap[:, :].rearrange("p (k q) -> p k q", q=128),
                                                         ALU.add), t3)]
            bank.free = x_half[hf]

        at_branch = [(V.sem, V.n), (S.sem, S.n), (G.sem, G.n), (P.sem, P.n)]
        oq = {q: Queue(q.eng, sem(f"o_{n}")) for q, n in ((P, "pe"), (V, "dve"), (S, "act"))}
        oY = Queue(nc.sync, None)
        oP, oV, oS = oq[P], oq[V], oq[S]
        ow = [count(f"s_ow{i}") for i in range(2)]
        oGU = [at(f"oGU{i}", [128, 8, 512], F, 16 + 16 * i) for i in range(2)]
        oDN = [at(f"oDN{i}", [128, 2, 1024], F, 48 + 8 * i) for i in range(2)]
        odg = at("odg", [128, T], F, 144)
        oa = [at(f"oa{i}", [128, T], F, 146 + 2 * i) for i in range(2)]
        ob_ = [at(f"ob{i}", [128, T], F, 150 + 2 * i) for i in range(2)]

        def rest_load(x, used):
            s = x % 2
            ow[s].load(oY, lambda e: e.dma_start(
                oGU[s][:, :, :], A["w_gu"][x].rearrange("p (k n) -> p k n", n=512)), used)
            return ow[s].load(oY, lambda e: e.dma_start(
                oDN[s][:, :, :], A["w_dn"][x].rearrange("p (k n) -> p k n", n=1024)), used)

        def rest_all():
            gate, ups, outs = banks[0].ap, [b.ap for b in banks[1:5]], [b.ap for b in banks[5:8]]
            free = {i: None for i in range(8)}
            used, hid_used, dg_used, wt, x_tok = {}, None, None, {}, None
            wt[0] = rest_load(0, None)
            wt[1] = rest_load(1, None)
            for x in range(NE):
                s = x % 2
                t0 = None
                for b in range(4):
                    t0 = oV.do(lambda e, b=b: e.tensor_scalar(odg[:, b * 128:(b + 1) * 128], ident[:, :],
                                                              GO[:, b, x:x + 1], None, ALU.mult), dg_used)
                tg = oP.do(lambda e: e.matmul(gate[:, :], ones[:, :], odg[:, :], start=True, stop=True), t0, free[0])
                dg_used = tg
                oP.wait(wt[x])
                hid_tok = []
                for m in range(2):
                    t = []
                    for j in range(2):
                        oP.wait(free[1 + 2 * m + j])
                        for k in range(8):
                            fn = lambda e, k=k: e.matmul(
                                ups[2 * m + j][:, :], oGU[s][:, k, (2 * j + m) * 128:(2 * j + m + 1) * 128],
                                XG[:, k, :], start=(k == 0), stop=(k == 7))
                            if k == 7:
                                t.append(oP.do(fn))
                            else:
                                oP.plain(fn)
                    a, b = oa[m], ob_[m]
                    t1 = oV.do(lambda e: e.tensor_tensor(a[:, :], ups[2 * m][:, :], rbc[:, :], ALU.mult), t[0], hid_used)
                    t2 = oV.do(lambda e: e.tensor_tensor(b[:, :], ups[2 * m + 1][:, :], rbc[:, :], ALU.mult), t[1])
                    free[1 + 2 * m], free[2 + 2 * m] = t1, t2
                    t3 = oS.do(lambda e: e.activation(a[:, :], a[:, :], ACT.Silu), t1)
                    t4 = oV.do(lambda e: e.tensor_tensor(b[:, :], b[:, :], gate[:, :], ALU.mult), t2, tg)
                    free[0] = t4
                    hid_tok.append(oV.do(lambda e: e.tensor_tensor(a[:, :], a[:, :], b[:, :], ALU.mult), t3, t4))
                for i in range(8):
                    n = 5 + i % 3
                    oP.wait(free[n], hid_tok)
                    for k in range(2):
                        fn = lambda e, k=k: e.matmul(outs[n - 5][:, :], oDN[s][:, k, i * 128:(i + 1) * 128],
                                                     oa[k][:, :], start=(k == 0), stop=(k == 1))
                        if k:
                            hid_used = oP.do(fn)
                        else:
                            oP.plain(fn)
                    x_tok = oV.do(lambda e: e.tensor_tensor(X[:, i, :], X[:, i, :], outs[n - 5][:, :], ALU.add),
                                  hid_used, x_tok)
                    free[n] = x_tok
                if x + 2 < NE:
                    wt[x + 2] = rest_load(x + 2, hid_used)

        with nc.If(left_over > 0):
            for q in (oP, oV, oS, oY):
                q.wait(at_branch)
            oS.plain(lambda e: e.preload_act_table_set("silu_and_others"))
            rest_all()
            oS.plain(lambda e: e.preload_act_table_set("natural_log_exp_and_others"))
            for q in (oP, oV, oS, oY):
                q.wait((oP.sem, oP.n), (oV.sem, oV.n), (oS.sem, oS.n))

        before = [(V.sem, V.n), (S.sem, S.n), (G.sem, G.n), (P.sem, P.n)]
        ropeA = at("ropeA", [128, 2, T], F, 156)
        t_tabA = c_t2.load(Y, lambda e: e.dma_start(ropeA[:, :, :], A["c_ropeA"].rearrange("p (a t) -> p a t", a=2)),
                           before)
        for i in range(8):
            n3.scale(i, x_half[i // 4], moe_done)
        for i in range(8):
            n3.square(i, x_half[i // 4])
        first = Group(stream2, 3, n3.tiles(), G8).to(8)
        n3.finish(banks[7], n2r, fine=True)
        ropeB = [at("ropeB0", [128, T], F, 160), at("ropeB1", [128, T], F, 204)]
        ropeA = (ropeA[:, 0, :], ropeA[:, 1, :])
        qA = at("qA", [128, 4, T], F, 144)
        kA = at("kA", [128, T], F, 152)
        vA = at("vA", [128, 4, 128], F, 154)
        CH = at("CH", [128, 2, 5, T], R, 182)
        KR = at("KR", [128, T], F, 202)
        wz = [at(f"wz{i}", [128, T], F, 162 + 2 * i) for i in range(2)]
        ws = [at(f"ws{i}", [128, T], F, 166 + 2 * i) for i in range(2)]
        wn = [at(f"wn{i}", [128, T], F, 170 + 2 * i) for i in range(2)]
        facc = [at(f"facc{i}", [128, T], F, 76 + 2 * i) for i in range(2)]
        r2 = at("r2", [128, T], F, 74)
        fq = [at(f"fq{i}", [128, T], F, 178 + 2 * i) for i in range(2)]
        fr = {0: list(before), 1: list(before)}
        rX = [n3.r, t_tabA]
        ZA = (wz, ws, wn)
        qk2 = {}

        def v_natural(i, z, t1, dst, names, p0=0, p1=128):
            b2 = banks[names]
            P.wait(t1, b2.free)
            w = p1 - p0
            for b in range(4):
                f = transpose(b2.ap[:, b * w:(b + 1) * w], z[p0:p1, b * 128:(b + 1) * 128], ident[p0:p1, p0:p1])
                if b < 3:
                    P.plain(f)
                else:
                    t2 = P.do(f)
            t3 = V.do(lambda e: e.tensor_copy(dst, b2.ap[:, 0:4 * w].rearrange("p (a b) -> p a b", b=w)), t2)
            b2.free = [t3]
            return [t3], t2

        for i in range(6):
            bank, tok = first[i]
            if i < 5:
                dst, g = (qA[:, i, :], "aqg") if i < 4 else (kA[:, :], "akg")
                head_norm_rope(i, bank, tok, rbc, col(g), permA, ropeA, dst, fr, rX, ZA,
                               lambda t, i=i: qk2.update({i if i < 4 else "k": t}), fine=True)
            else:
                z = wz[i % 2]
                t1 = V.do(lambda e: e.tensor_tensor(z[:, :], bank.ap[:, :], rbc[:, :], ALU.mult), tok, rX,
                          fr.get(i % 2))
                bank.free = [t1]

                def w(i=i, z=z, t1=t1):
                    qk2["v"], t = v_natural(i, z, t1, vA[:, :, :], 4 + i % 2)
                    fr[i % 2] = [t]
                later(w)
            if i < 5:
                first.append(gemm(stream2, [(nxt(), n3.tiles())], G8))

        c_tok, fac_tok = {}, [[], []]
        for i in range(5):
            bank, tok = first[6 + i] if i < 2 else gemm(stream2, [(nxt(), n3.tiles())], G8)
            a = 0 if i < 3 else 1
            th = S.do(lambda e: e.activation(CH[:, 0, i, :], bank.ap[:, :], ACT.Identity, bias=0.0,
                                             scale=col("bg", i)), tok, before)
            q = tm[i % 2]
            dst = facc[a] if i in (0, 3) else q
            ts = S.do(lambda e: e.activation(dst[:, :], bank.ap[:, :], ACT.Square), tok, before,
                      [] if i in (0, 3) else sq_free[i % 2])
            tl = V.do(lambda e: e.scalar_tensor_tensor(CH[:, 1, i, :], bank.ap[:, :], col("bg", i),
                                                       CH[:, 0, i, :].bitcast(F), ALU.mult, ALU.subtract),
                      th, ts, tok, before)
            c_tok[i] = [th, tl]
            if i in (0, 3):
                fac_tok[a] = [ts]
            else:
                fac_tok[a] = [V.do(lambda e: e.tensor_tensor(facc[a][:, :], facc[a][:, :], q[:, :], ALU.add),
                                   ts, fac_tok[a])]
                sq_free[i % 2] = list(fac_tok[a])
            bank.free = [th, tl, ts]
        flush()
        krz = []

        c_tb, c_tq = count("s_ropeB"), count("s_turn")
        turnQ = [at(f"turnQ{i}", [128, T], F, 156 + 2 * i) for i in range(2)]
        before = [(V.sem, V.n), (S.sem, S.n), (G.sem, G.n), (P.sem, P.n)]
        ropeBv = (ropeB[0][:, :], ropeB[1][:, :])
        for i in range(2):
            t_tabB = c_tb.load(Y, lambda e: e.dma_start(ropeB[i][:, :], A["c_ropeB"][:, i * T:(i + 1) * T]), before)
            t_tabQ = c_tq.load(Y, lambda e: e.dma_start(turnQ[i][:, :], A["c_turnQ"][i]), before)
        f_mean, f_root, f_ready, t_fq = [], [], [], []
        head_free = list(before)
        fcol = keep[:, 16:20]

        def low_rank_factors():
            bank, tok = gemm(stream2, [(nxt(), n3.tiles())], [7])
            t1 = V.do(lambda e: e.tensor_tensor(KR[:, :], bank.ap[:, :], rbc[:, :], ALU.mult), tok, n3.r, head_free)
            bank.free = [t1]
            krz.append(t1)
            t_r2 = V.do(lambda e: e.tensor_tensor(r2[:, :], rbc[:, :], rbc[:, :], ALU.mult), n3.r, head_free)
            for a in range(2):
                bk = banks[4 + a]
                t1 = P.do(lambda e: e.matmul(bk.ap[:, :], ones[:, :], facc[a][:, :], start=True, stop=True),
                          fac_tok[a], bk.free)
                f_mean.append(V.do(lambda e: e.tensor_tensor(facc[a][:, :], bk.ap[:, :], r2[:, :], ALU.mult), t1, t_r2))
                bk.free = [f_mean[a]]
            return [tok]

        def low_rank_roots():
            for a, w in ((0, 384), (1, 256)):
                t3 = S.do(lambda e: e.activation(fq[a][:, :], facc[a][:, :], ACT.Ln, bias=col("eps"), scale=1.0 / w),
                          f_mean[a], head_free)
                f_root.append(S.do(lambda e: e.activation(fq[a][:, :], fq[a][:, :], ACT.Exp, scale=-0.5), t3))

        def low_rank_products(a, w):
            t = V.do(lambda e: e.tensor_tensor(r2[:, :], fq[a][:, :], fq[a][:, :], ALU.mult), f_root[a],
                     (V.sem, V.n))
            t = newton(facc[a], w, r2, fq[a], fq[a], t)
            f_ready.append(V.do(lambda e: e.tensor_tensor(fq[a][:, :], fq[a][:, :], rbc[:, :], ALU.mult), t, n3.r))

        def query_table(i):
            t_fq.append(V.do(lambda e: e.tensor_tensor(turnQ[i][:, :], turnQ[i][:, :], fq[0][:, :], ALU.mult),
                             t_tabQ, f_ready))

        early2, t_kr, t_fcol = [], [], []

        def first_queries():
            early2.extend(gemm(stream2, [(nxt(), cq)], [j]) for j in range(2))
            t_kr.extend(rope_only(1, KR, krz, permB, ropeBv, KR[:, :], {}, [t_tabB, head_free], tm[0], tm[1]))
            bank = banks[2]
            P.wait(f_ready[1], bank.free)
            for b in range(4):
                fn = lambda e: e.matmul(bank.ap[:, b:b + 1], fq[1][0:1, b * 128:(b + 1) * 128], ones[0:1, 0:1],
                                        start=True, stop=True)
                if b < 3:
                    P.plain(fn)
                else:
                    t1 = P.do(fn)
            t_fcol.append(V.do(lambda e: e.tensor_copy(fcol, bank.ap[:, 0:4]), t1))
            bank.free = [t_fcol[0]]

        cq = [(CH[:, 0, k, :], CH[:, 1, k, :], c_tok[k]) for k in range(3)]
        PTA = [[at("PTA0", [128, 4, T], F, 162), at("PTA1", [128, 4, T], F, 170)],
               [at("PTA2", [128, 4, T], F, 26), at("PTA3", [128, 4, T], F, 34)]]
        PbA = [at(f"PbA{i}", [128, T], F, k) for i, k in enumerate((56, 58, 60, 62, 72))]
        before = [(V.sem, V.n), (S.sem, S.n), (G.sem, G.n), (P.sem, P.n)]
        FULL = [(0, 4)] * 4
        H1v = H[1]
        mix_tok = {}
        prs = []
        for i in range(4):
            def out(bank, to, i=i):
                mix_tok[i] = split_out(H1v[:, 0, i, :], H1v[:, 1, i, :])(bank, to)
                return mix_tok[i]

            prs.append(dict(
                q=lambda hd, b, i=i: qA[64 * hd:64 * hd + 64, i, b * 128:(b + 1) * 128],
                k=lambda hd, lo, hi: kA[64 * hd:64 * hd + 64, lo * 128:hi * 128],
                kbs=FULL, ready=lambda hd, b, i=i: [qk2[i], qk2["k"]], mask=None, sink=None,
                v=lambda kb, hd: vA[:, kb, 64 * hd:64 * hd + 64], v_ready=lambda: qk2["v"], out=out))
        attention(prs, PTA, PbA, 0.125, before, before, head=low_rank_factors, tail=first_queries,
                  between={7: low_rank_roots, 10: lambda: low_rank_products(0, 384),
                           13: lambda: low_rank_products(1, 256), 16: lambda: query_table(0),
                           18: lambda: query_table(1)})

        before = [(V.sem, V.n), (S.sem, S.n), (G.sem, G.n), (P.sem, P.n)]
        qB = at("qB", [128, 8, T], F, 16)
        kB = at("kB", [128, 8, T], F, 32)
        vB = at("vB", [128, 4, T], F, 144)
        ckv = [(CH[:, 0, k, :], CH[:, 1, k, :], c_tok[k]) for k in range(3, 5)]
        t_kc = []
        for odd in range(2):
            p0 = 0 if odd else 64
            t_kc.append(S.do(lambda e: e.copy(
                kB[p0:p0 + 64, :, :].rearrange("p (h o) t -> p h o t", o=2)[:, :, odd, :],
                KR[p0:p0 + 64, :].unsqueeze(1).to_broadcast([64, 4, T])), t_kr, before))
        bq, bk2, bv = {}, {}, []
        for i in range(8):
            bank, tok = early2[i] if i < 2 else gemm(stream2, [(nxt(), cq)], [2, 3, 0, 1])
            bq[i] = [V.do(lambda e: e.tensor_tensor(qB[:, i, :], bank.ap[:, :], turnQ[i % 2][:, :], ALU.mult), tok,
                          t_fq, before)]
            bank.free = bq[i]
        for i in range(4):
            bank, tok = gemm(stream2, [(nxt(), ckv)], G8)
            for odd in range(2):
                p0 = 64 * odd
                t1 = V.do(lambda e: e.tensor_tensor(kB[p0:p0 + 64, 2 * i + odd, :], bank.ap[p0:p0 + 64, :],
                                                    fq[1][p0:p0 + 64, :], ALU.mult), tok, f_ready, before)
                bk2[2 * i + odd] = [t1, t_kc]
            bank.free = [t1]
        b_free = list(before)

        def values_b():
            c = nxt()
            stream2.split_to(c)
            for b in range(4):
                bank = banks[4 + b]
                P.wait(bank.free, stream2.ready[c], c_tok[3], c_tok[4])
                n = 0
                for k in range(2):
                    hi, lo = (CH[:, a, 3 + k, b * 128:(b + 1) * 128] for a in range(2))
                    wh, wl = (w[c % 3][:, k * 512:(k + 1) * 512] for w in (whi, wlo))
                    for x, w in ((hi, wh), (lo, wh), (hi, wl)):
                        fn = lambda e, n=n: e.matmul(bank.ap[:, :], x, w, start=(n == 0), stop=(n == 5))
                        n += 1
                        if n == 6:
                            tok = P.do(fn)
                        else:
                            P.plain(fn)
                bv.append(S.do(lambda e: e.activation(vB[:, b, :], bank.ap[:, :], ACT.Copy, bias=0.0,
                                                     scale=fcol[:, b:b + 1]), tok, t_fcol, b_free))
                bank.free = [bv[b]]
            stream2.used(c, tok)
            stream2.split_to(c + 2)
            return [(P.sem, P.n)]

        PTB = [[at("PTB0", [128, 4, T], F, 162), at("PTB1", [128, 4, T], F, 170)],
               [at("PTB2", [128, 4, T], F, 188), at("PTB3", [128, 4, T], F, 196)]]
        PbB = [at(f"PbB{i}", [128, T], F, 178 + 2 * i) for i in range(5)]
        before = [(V.sem, V.n), (S.sem, S.n), (G.sem, G.n), (P.sem, P.n)]

        class Later:

            def __init__(self, Hn, toks):
                self.H, self.toks = Hn, toks

            def __len__(self):
                return 8

            def __getitem__(self, k):
                if k > 7:
                    raise IndexError
                return self.H[:, 0, k, :], self.H[:, 1, k, :], self.toks[k]

        def halves(tiles):
            group = []

            def first_tiles():
                group.append(Group(stream2, 2, tiles, G8))
                group[0].to(7)

            return lambda: group[0].to(8), first_tiles

        prs = []
        for i in range(4):
            def out(bank, to, i=i):
                mix_tok[4 + i] = split_out(H1v[:, 0, 4 + i, :], H1v[:, 1, 4 + i, :])(bank, to)
                return mix_tok[4 + i]

            prs.append(dict(
                q=lambda hd, b, i=i: qB[:, 2 * i + hd, b * 128:(b + 1) * 128],
                k=lambda hd, lo, hi, i=i: kB[:, 2 * i + hd, lo * 128:hi * 128],
                kbs=FULL, ready=lambda hd, b, i=i: [bq[2 * i + hd], bk2[2 * i + hd]], mask=None, sink=None,
                v=lambda kb, hd, i=i: vB[:, kb, 64 * (2 * i + hd):64 * (2 * i + hd) + 64],
                v_ready=lambda: bv, out=out))
        mixt = Later(H[1], mix_tok)
        last_tile, first_tiles = halves(mixt)
        attention(prs, PTB, PbB, float(np.float32(96.0) ** np.float32(-0.5)), before, before, head=values_b,
                  tail=first_tiles)

        def project(start, tiles, Hn, gname, prev, h_free):
            nn = Norm(Hn, gname, prev.acc_read)
            for i in range(8):
                bank, tok = start[i] if i < 2 else gemm(stream2, [(nxt(), tiles)], G8)
                xt = V.do(lambda e: e.tensor_tensor(X[:, i, :], X[:, i, :], bank.ap[:, :], ALU.add), tok, (V.sem, V.n))
                bank.free = [xt]
                nn.tile(i, [xt], h_free, split=Hn is not None)
            return nn, Group(stream2, 2, nn.tiles(), G8).to(8)

        U = at("U", [128, 2, 8, T], R, 144)
        fu = [at(f"fu{i}", [128, T], F, 176 + 2 * i) for i in range(4)]

        def ffn(nn, start, Hn, gname, h_free):
            before = [(V.sem, V.n), (S.sem, S.n), (G.sem, G.n), (P.sem, P.n)]
            ffree = [list(before), list(before)]
            down = list(before)
            nn.finish(banks[7], [(V.sem, V.n)])
            out = Norm(Hn, gname, nn.acc_read)
            for q in range(4):
                u_tok = {}
                for i in range(8):
                    bank, tok = start[i] if q == 0 and i < 2 else gemm(stream2, [(nxt(), nn.tiles())], G8)
                    a, b = fu[2 * (i % 2)], fu[2 * (i % 2) + 1]
                    t1 = V.do(lambda e: e.scalar_tensor_tensor(a[:, :], bank.ap[:, :], 0.0, rbc[:, :],
                                                               ALU.max, ALU.mult), tok, nn.r, ffree[i % 2])
                    bank.free = [t1]
                    t2 = S.do(lambda e: e.activation(b[:, :], a[:, :], ACT.Square), t1, ffree[i % 2])
                    t3 = S.do(lambda e: e.copy(U[:, 0, i, :], b[:, :]), t2, down)
                    t4 = V.do(lambda e: e.tensor_tensor(U[:, 1, i, :], b[:, :], U[:, 0, i, :].bitcast(F),
                                                        ALU.subtract), t3, down)
                    ffree[i % 2] = [t4]
                    u_tok[i] = [t3, t4]
                tiles = [(U[:, 0, k, :], U[:, 1, k, :], u_tok[k]) for k in range(8)]
                for i in range(8):
                    bank, tok = gemm(stream2, [(nxt(), tiles)], G8)
                    xt = V.do(lambda e: e.tensor_tensor(X[:, i, :], X[:, i, :], bank.ap[:, :], ALU.add), tok,
                              (V.sem, V.n))
                    bank.free = [xt]
                    if q == 3:
                        out.tile(i, [xt], h_free, split=Hn is not None)
                down = [tok]
            return out

        before = [(V.sem, V.n), (S.sem, S.n), (G.sem, G.n), (P.sem, P.n)]
        n4, start = project(last_tile(), mixt, H[0], "gf0", n3, before)
        n5 = ffn(n4, start, H[1], "gm1", [(P.sem, P.n)])
        start = Group(stream2, 2, n5.tiles(), G8).to(8)
        n5.finish(banks[7], [(V.sem, V.n)], fine=True)

        before = [(V.sem, V.n), (S.sem, S.n), (G.sem, G.n), (P.sem, P.n)]
        qC = at("qC", [128, 8, T], F, 144)
        kC = at("kC", [128, 8, T], F, 160)
        vC = at("vC", [128, 4, D], F, 176)
        cz = tm

        def by_row(ap):
            return ap.rearrange("p (r b c) -> p r b c", b=4, c=16)

        def blocked(ap):
            return ap.rearrange("p (b r c) -> p r b c", b=4, c=16)

        rb8 = at("rb8", [128, T], F, 196)
        t_rb8 = V.do(lambda e: e.tensor_scalar(rb8[:, :], rbc[:, :], 0.125, None, ALU.mult), n5.r, before)
        qc, kc, vc = {}, {}, {}
        zf = [list(before), list(before)]

        def qkv_tile(i, bank, tok):
            if i < 16:
                dst = (qC if i < 8 else kC)[:, i % 8, :]
                if i < 8:
                    t1 = V.do(lambda e: e.tensor_tensor(blocked(dst), by_row(bank.ap[:, :]), by_row(rb8[:, :]),
                                                        ALU.mult), tok, t_rb8, before)
                else:
                    t1 = V.do(lambda e: e.tensor_tensor(blocked(dst), by_row(bank.ap[:, :]), by_row(rbc[:, :]),
                                                        ALU.mult), tok, n5.r, before)
                bank.free = [t1]
                (qc if i < 8 else kc)[i % 8] = [t1]
            else:
                def w(i=i, bank=bank, tok=tok):
                    z = cz[i % 2]
                    t1 = V.do(lambda e: e.tensor_tensor(blocked(z[:, :]), by_row(bank.ap[:, :]), by_row(rbc[:, :]),
                                                        ALU.mult), tok, n5.r, zf[i % 2])
                    bank.free = [t1]
                    vc[i % 8], tf = v_natural(i, z, t1, vC[:, :, 128 * (i % 8):128 * (i % 8) + 128], 4 + i % 2)
                    zf[i % 2] = [tf]
                later(w)

        for i in range(23):
            bank, tok = start[i] if i < 2 else gemm(stream2, [(nxt(), n5.tiles())], G8)
            qkv_tile(i, bank, tok)
        flush()

        def last_values():
            bank, tok = gemm(stream2, [(nxt(), n5.tiles())], [7])
            qkv_tile(23, bank, tok)
            flush()
            return [tok]

        before = [(V.sem, V.n), (S.sem, S.n), (G.sem, G.n), (P.sem, P.n)]
        bia = [at(f"bia{i}", [128, 896], F, 192 + 3.5 * i) for i in range(2)]
        PTC = [[at("PTC0", [128, 4, T], F, 48), at("PTC1", [128, 4, T], F, 56)],
               [at("PTC2", [128, 4, T], F, 64), at("PTC3", [128, 4, T], F, 72)]]
        PbC = [at(f"PbC{i}", [128, 384], F, 199.25 + 1.5 * i) for i in range(5)]
        c_b = [count("s_bia0"), count("s_bia1")]
        bia_at, bia_free = {}, [list(before), list(before)]

        def load_bias(h):
            bia_at[h] = c_b[h % 2].load(Y, lambda e: e.dma_start(bia[h % 2][:, :], A["c_bias"][h]), bia_free[h % 2])

        load_bias(0)
        load_bias(1)
        BO = [(0, 256), (256, 640), (256, 640), (640, 896)]

        def used(pi, hd, b, t):
            if b == 3:
                h = 2 * pi + hd
                bia_free[h % 2] = [t]
                if h + 2 < 16:
                    load_bias(h + 2)

        odd_tok = {}
        prs = []

        for i in range(8):
            def out(bank, to, i=i):
                view = lambda ap: ap[:, :].rearrange("p (b r c) -> p r b c", b=4, c=16)
                odd_tok[i] = split_out(by_row(H[0][:, 0, i, :]), by_row(H[0][:, 1, i, :]), view)(bank, to)
                return odd_tok[i]

            prs.append(dict(
                q=lambda hd, b, i=i: qC[64 * hd:64 * hd + 64, i, b * 128:(b + 1) * 128],
                k=lambda hd, lo, hi, i=i: kC[64 * hd:64 * hd + 64, i, lo * 128:hi * 128],
                kbs=KBS, ready=lambda hd, b, i=i: [qc[i], kc[i]],
                mask=lambda hd, b: bia[hd][:, BO[b][0]:BO[b][1]],
                mask_ready=lambda hd, i=i: bia_at[2 * i + hd], mask_used=lambda hd, b, t, i=i: used(i, hd, b, t),
                sink=None,
                v=lambda kb, hd, i=i: vC[:, kb, 128 * i + 64 * hd:128 * i + 64 * hd + 64], v_ready=lambda i=i: vc[i], out=out))
        oddt = Later(H[0], odd_tok)
        last_tile, first_tiles = halves(oddt)
        attention(prs, PTC, PbC, 1.0, before, before, head=last_values, tail=first_tiles)

        before = [(V.sem, V.n), (S.sem, S.n), (G.sem, G.n), (P.sem, P.n)]
        n6, start = project(last_tile(), oddt, H[1], "gf1", n5, before)
        n7 = ffn(n6, start, None, None, [])
        n7.finish(banks[7], [(V.sem, V.n)])

        c_out = count("s_out")
        for i in range(8):
            t1 = V.do(lambda e: e.scalar_tensor_tensor(X[:, i, :], X[:, i, :], col("gfin", i), rbc[:, :],
                                                       ALU.mult, ALU.mult), n7.r, (V.sem, V.n), (S.sem, S.n))
            t_out = c_out.load(Y, lambda e: e.dma_start(A["outT"][:, i * T:(i + 1) * T], X[:, i, :]), t1)
        Y.wait(t_out, y_tok, t_sc, zeroed)


VECS = [("eps", 1), ("g1", 8), ("g2", 8), ("gm0", 8), ("gf0", 8), ("gm1", 8), ("gf1", 8), ("gfin", 8),
        ("qg", 1), ("kg", 1), ("aqg", 1), ("akg", 1), ("sink", 8), ("cv0", 4), ("cv1", 4),
        ("cv2", 4), ("cvb", 4), ("bg", 5)]


def tables():
    f = np.float32
    c = {}
    eye = np.eye(128, dtype=f)
    c["c_ident"] = eye
    c["c_ones"] = np.ones((128, 128), f)
    b = np.zeros((128, 128), f)
    b[:64, :64] = 1
    b[64:, 64:] = 1
    c["c_bones"] = b
    c["c_triu"] = np.triu(np.ones((128, 128), f), 1)
    c["c_io32"] = np.broadcast_to(np.arange(32, dtype=f), (128, 32)).copy()

    def perm(pairs, size=128):
        m = np.zeros((128, 128), f)
        for a, b_ in pairs:
            m[b_, a] = -1
            m[a, b_] = 1
        return m

    t = np.arange(T, dtype=f)

    def table(size, parts):
        cs = np.zeros((size, 2, T), f)
        cs[:, 0] = 1
        for a, b_, ang in parts:
            for i in (a, b_):
                cs[i, 0], cs[i, 1] = np.cos(ang), np.sin(ang)
        return cs.reshape(size, 2 * T)

    inv = (f(500000.0) ** (-np.arange(0, 16, 2, dtype=f) / f(16))).astype(f)
    pf = [(64 * h + i, 64 * h + i + 8) for h in range(2) for i in range(8)]
    c["c_permF"] = perm(pf)
    c["c_ropeF"] = table(128, [(64 * h + i, 64 * h + i + 8, (t * inv[i]).astype(f)) for h in range(2) for i in range(8)])
    row, colm = (t // 64).astype(f), (t % 64).astype(f)

    def axial(base, d):
        inv = (f(10000.0) ** (-np.arange(0, d, 2, dtype=f) / f(d))).astype(f)
        out = []
        for part, pos in ((0, row), (1, colm)):
            for i in range(d // 2):
                a = base + part * d + i
                out.append((a, a + d // 2, (pos * inv[i]).astype(f)))
        return out

    pa = axial(0, 32) + axial(64, 32)
    c["c_permA"] = perm([x[:2] for x in pa])
    c["c_ropeA"] = table(128, pa)
    pb = [x for p in range(4) for x in axial(32 * p, 16)]
    c["c_permB"] = perm([x[:2] for x in pb])
    c["c_ropeB"] = table(128, pb)
    turn = np.ones((2, 128, T), f)
    for i, p in enumerate((64, 0)):
        for a, b_, ang in axial(0, 16):
            turn[i, p + a], turn[i, p + b_] = np.cos(ang), np.cos(ang)
            turn[i, p + 32 + a], turn[i, p + 32 + b_] = -np.sin(ang), np.sin(ang)
    c["c_turnQ"] = turn
    i, j = np.arange(128)[:, None], np.arange(384)[None, :] - 128
    c["c_maskF"] = np.where(np.abs(i - j) <= 128, 0, NEG).astype(f)
    return c


def layout(v):
    f = np.float32
    a = {}

    def arr(n):
        return np.asarray(v[n])

    def tiles(w, m=128):
        k, n = w.shape
        return np.ascontiguousarray(w.reshape(k // 128, 128, n // m, m).transpose(2, 1, 0, 3)).reshape(
            n // m, 128, (k // 128) * m)

    x = arr("x")[0]
    a["xT"] = np.ascontiguousarray(x.T.reshape(8, 128, T).transpose(1, 0, 2)).reshape(128, 8 * T)
    w = arr("w_in")[0]
    pair = np.concatenate([np.r_[64 * i:64 * i + 64, 64 * (i + 4):64 * (i + 4) + 64] for i in range(4)])
    a["w1_in"] = tiles(np.concatenate([w[:, 0:512][:, pair], w[:, 512:768]], 1))
    cb, cc, cx = w[:, 768:1280], w[:, 1280:1792], w[:, 1792:2304]
    a["w1_conv"] = tiles(np.concatenate([p[:, 128 * i:128 * i + 128] for i in range(4) for p in (cc, cx, cb)], 1))
    a["w1_ga"] = tiles(w[:, 2304:3328])
    a["w1_gc"] = tiles(w[:, 3328:4352])
    a["w1_ap"] = tiles(arr("w_attn_proj")[0][pair])
    a["w1_cp"] = tiles(arr("w_conv_proj")[0])
    a["w1_out"] = tiles(arr("w_out")[0])
    wr = np.concatenate([arr("w_router_group")[0], arr("w_router_expert")[0]], 1)
    a["w_router"] = np.ascontiguousarray(wr.reshape(8, 128, 36).transpose(1, 0, 2)).reshape(128, 288)
    br = np.concatenate([arr("b_router_group")[0], arr("b_router_expert")[0]])
    a["b_router"] = np.broadcast_to(br, (128, 36)).copy()
    gu = np.concatenate([arr("w_gate_e")[0], arr("w_up_e")[0]], 2)
    a["w_gu"] = np.ascontiguousarray(gu.reshape(NE, 8, 128, 512).transpose(0, 2, 1, 3)).reshape(NE, 128, 4096)
    a["w_dn"] = np.ascontiguousarray(arr("w_down_e")[0].reshape(NE, 2, 128, D).transpose(0, 2, 1, 3)).reshape(
        NE, 128, 2048)
    w = arr("ev_w_in_2")[0]
    a["w2_in"] = tiles(np.concatenate([w[:, 0:512][:, pair], w[:, 512:768]], 1))
    a["w2_c"] = tiles(w[:, 768:1408])
    a["w2_kr"] = tiles(np.concatenate([w[:, 1408:1440]] * 4, 1))
    partner = np.arange(32) ^ 8
    uq = []
    for i in range(8):
        h = arr("ev_b_w_uq_2")[0][:, 96 * i:96 * i + 96]
        nope, rope = h[:, :64], h[:, 64:]
        uq += [rope, rope[:, partner], nope] if i % 2 else [nope, rope, rope[:, partner]]
    a["w2_uq"] = tiles(np.concatenate(uq, 1))
    ukv = arr("ev_b_w_ukv_2")[0].reshape(256, 8, 128)
    a["w2_uk"] = tiles(np.ascontiguousarray(ukv[:, :, :64]).reshape(256, 512))
    a["w2_uv"] = np.ascontiguousarray(ukv[:, :, 64:]).reshape(2, 128, 512).transpose(1, 0, 2).reshape(128, 1024).copy()
    rows = np.concatenate([pair, np.arange(512, 1024)])
    a["w2_evo"] = tiles(arr("ev_w_out_2")[0][rows])
    for l in range(2):
        a[f"w_up{l}"] = tiles(arr("ffn_w_up_2")[l])
        d = arr("ffn_w_down_2")[l].reshape(4, 8, 128, 8, 128).transpose(0, 3, 2, 1, 4)
        a[f"w_down{l}"] = np.ascontiguousarray(d).reshape(32, 128, 1024)
    a["w2_qkv"] = tiles(arr("od_w_qkv_2")[0])
    a["w2_odo"] = tiles(arr("od_w_out_2")[0])

    rpb = arr("od_rpb_2")[0]
    q = np.arange(128)
    qr, qcl = q // 16, q % 16
    out = np.full((16, 128, 896), NEG, f)
    for base, nb, first, lo in ((0, 2, 0, 0), (256, 3, 1, 0), (640, 2, 3, 2)):
        k = np.arange(nb * 128)
        kr, kcl = (k % 128) // 16, (lo + k // 128) * 16 + k % 16
        c = first * 16 + qcl
        cs = np.clip(c - 8, 0, 48)
        valid = (kcl[None] >= cs[:, None]) & (kcl[None] < cs[:, None] + 16)
        qi, ki = np.nonzero(valid)
        out[:, qi, base + ki] = rpb[:, kr[ki] - qr[qi] + 7, kcl[ki] - c[qi] + 15]
    a["c_bias"] = out

    vec = np.zeros((128, 128), f)
    cols = {"eps": np.full((1, 128), EPS, f)}

    def feat(g):
        return np.asarray(g).reshape(-1, 128)

    cols["g1"], cols["g2"] = feat(arr("norm1_g")[0]), feat(arr("norm2_g")[0])
    for l in range(2):
        cols[f"gm{l}"], cols[f"gf{l}"] = feat(arr("norm_mix_2")[l]), feat(arr("norm_ffn_2")[l])
    cols["gfin"] = feat(arr("final_norm_2"))
    for n, s in (("qg", "q_norm_g"), ("kg", "k_norm_g"), ("aqg", "ev_a_q_norm_2"), ("akg", "ev_a_k_norm_2")):
        g = arr(s)[0]
        cols[n] = np.concatenate([g, g])[None]
    cols["sink"] = np.broadcast_to(arr("attn_sink")[0][:, None], (8, 128))
    for j in range(3):
        cols[f"cv{j}"] = feat(arr("conv_w")[0, j])
    cols["cvb"] = feat(arr("conv_b")[0])
    cols["bg"] = feat(np.concatenate([arr("ev_b_q_norm_2")[0], arr("ev_b_kv_norm_2")[0]]))
    c = 0
    for n, w_ in VECS:
        if n in cols:
            vec[:, c:c + w_] = cols[n].T
        c += w_
    a["vec"] = vec
    a.update(tables())
    return a


def kernel(**inputs):
    import concourse.bacc as bacc
    from concourse.bass_utils import run_bass_kernel_spmd as run

    nc = bacc.Bacc("TRN2", target_bir_lowering=False, num_devices=1)
    arrays = layout(inputs)
    A = {}
    for name, a in arrays.items():
        A[name] = nc.dram_tensor("in_" + name, a.shape, mybir.dt.from_np(a.dtype), kind="ExternalInput").ap()
    A["hbuf"] = nc.dram_tensor("hbuf", (SLOTS, D), F, kind="Internal").ap()
    A["ybuf"] = nc.dram_tensor("ybuf", (SLOTS, D), F, kind="Internal").ap()
    A["outT"] = nc.dram_tensor("outT", (128, 8 * T), F, kind="ExternalOutput").ap()
    program(nc, A)
    r = run(nc, [{"in_" + n: a for n, a in arrays.items()}], core_ids=[0])
    o = r.results[0]["outT"].reshape(128, 8, T).transpose(2, 1, 0).reshape(1, T, D)
    return np.ascontiguousarray(o)
```
